# Optimizing a Trainium2 kernel written in Bass

```python
import jax, jax.numpy as jnp
from jax import lax
import numpy as np

D_MODEL = 1024
BATCH = 1
SEQ = 512
DEPTH = 1

CHUNK = 64
Q_BLOCK = 128
SB_HEADS = 8
SB_HEAD_DIM = 64
SB_WIDTH = SB_HEADS * SB_HEAD_DIM
HG_HEADS = 4
HG_HEAD_DIM = 128
HG_WIDTH = HG_HEADS * HG_HEAD_DIM
N_BRANCH = 2
D_FF = 4 * D_MODEL
IN_COLS = 3 * SB_WIDTH + 4 * HG_WIDTH + N_BRANCH * D_MODEL
EPS = 1e-6


def rmsnorm(x, g):
    xf = x.astype(jnp.float32)
    y = xf * lax.rsqrt(jnp.mean(xf * xf, axis=-1, keepdims=True) + EPS)
    return y * g.astype(jnp.float32)

def split_heads(t, n_heads):
    b, s, w = t.shape
    return t.reshape(b, s, n_heads, w // n_heads).transpose(0, 2, 1, 3)

def merge_heads(t):
    b, h, s, d = t.shape
    return t.transpose(0, 2, 1, 3).reshape(b, s, h * d)

def stick_breaking_attention(q, k, v):
    b, h, s, dh = q.shape
    nb = s // Q_BLOCK
    scale = dh ** -0.5
    qb = q.reshape(b, h, nb, Q_BLOCK, dh).transpose(2, 0, 1, 3, 4)
    kpos = jnp.arange(s)

    def block(args):
        qi, i = args
        qpos = i * Q_BLOCK + jnp.arange(Q_BLOCK)
        z = jnp.einsum('bhqd,bhkd->bhqk', qi, k) * scale
        mask = kpos[None, :] < qpos[:, None]
        log_beta = jax.nn.log_sigmoid(z)
        log_rem = jnp.where(mask, log_beta - z, 0.0)
        between = lax.cumsum(log_rem, axis=3, reverse=True) - log_rem
        w = jnp.where(mask, jnp.exp(log_beta + between), 0.0)
        return jnp.einsum('bhqk,bhkd->bhqd', w, v)

    out = lax.map(block, (qb, jnp.arange(nb)))
    return out.transpose(1, 2, 0, 3, 4).reshape(b, h, s, dh)

def hgrn2_chunkwise(q, k, v, log_f):
    b, h, s, dk = q.shape
    dv = v.shape[-1]
    nc = s // CHUNK

    def to_chunks(t):
        return t.reshape(b, h, nc, CHUNK, t.shape[-1]).transpose(2, 0, 1, 3, 4)

    qc, kc, vc, gc = to_chunks(q), to_chunks(k), to_chunks(v), to_chunks(log_f)
    causal = jnp.arange(CHUNK)[:, None] >= jnp.arange(CHUNK)[None, :]

    def step(state, inp):
        qi, ki, vi, gi = inp
        bcum = jnp.cumsum(gi, axis=2)
        diff = bcum[:, :, :, None, :] - bcum[:, :, None, :, :]
        decay = jnp.exp(jnp.where(causal[:, :, None], diff, -jnp.inf))
        scores = jnp.einsum('bhtd,bhsd,bhtsd->bhts', qi, ki, decay)
        o = jnp.einsum('bhts,bhse->bhte', scores, vi) \
            + jnp.einsum('bhtd,bhde->bhte', qi * jnp.exp(bcum), state)
        b_last = bcum[:, :, -1:, :]
        k_dec = ki * jnp.exp(b_last - bcum)
        state = jnp.exp(b_last[:, :, 0, :])[..., None] * state \
            + jnp.einsum('bhsd,bhse->bhde', k_dec, vi)
        return state, o

    s0 = jnp.zeros((b, h, dk, dv), jnp.float32)
    _, o = lax.scan(step, s0, (qc, kc, vc, gc))
    return o.transpose(1, 2, 0, 3, 4).reshape(b, h, s, dv)

def hybrid_layer(x, layer, norm1_g, w_in, b_gate, lb_logits, hg_norm_g, w_o_sb, w_o_hg, w_out,
                 norm2_g, w_ff1, w_ff2):
    f32 = jnp.float32
    xn = rmsnorm(x, norm1_g[layer])
    u = xn @ w_in[layer].astype(f32)
    c = np.cumsum([SB_WIDTH, SB_WIDTH, SB_WIDTH, HG_WIDTH, HG_WIDTH, HG_WIDTH, HG_WIDTH, D_MODEL])
    q_sb, k_sb, v_sb, f_raw, i_hg, q_hg, g_hg, gate_sb, gate_hg = jnp.split(u, list(c), axis=-1)

    o_sb = stick_breaking_attention(split_heads(q_sb, SB_HEADS), split_heads(k_sb, SB_HEADS),
                                    split_heads(v_sb, SB_HEADS))
    o_sb = merge_heads(o_sb)

    lb_all = jnp.cumsum(jax.nn.softmax(lb_logits.astype(f32), axis=0), axis=0)
    lb = lb_all[layer]
    sig = jax.nn.sigmoid(f_raw)
    f = lb + (1.0 - lb) * sig
    log_f = jnp.log(f)
    k_hg = (1.0 - lb) * jax.nn.sigmoid(-f_raw)
    o_hg = hgrn2_chunkwise(split_heads(jax.nn.silu(q_hg), HG_HEADS), split_heads(k_hg, HG_HEADS),
                           split_heads(i_hg, HG_HEADS), split_heads(log_f, HG_HEADS))
    o_hg = rmsnorm(o_hg, hg_norm_g[layer].reshape(HG_HEADS, 1, HG_HEAD_DIM))
    o_hg = merge_heads(o_hg) * jax.nn.silu(g_hg)

    bg = b_gate[layer].astype(f32)
    g_a = jax.nn.sigmoid(gate_sb + bg[:D_MODEL])
    g_b = jax.nn.sigmoid(gate_hg + bg[D_MODEL:])
    merged = g_a * (o_sb @ w_o_sb[layer].astype(f32)) + g_b * (o_hg @ w_o_hg[layer].astype(f32))
    h = x.astype(f32) + merged @ w_out[layer].astype(f32)

    hn = rmsnorm(h, norm2_g[layer])
    a = jnp.square(jax.nn.relu(hn @ w_ff1[layer].astype(f32)))
    h = h + a @ w_ff2[layer].astype(f32)
    return h

def first_inputs(seed: int = 0) -> dict:
    key = jax.random.key(seed)
    ks = jax.random.split(key, 14)
    f32 = jnp.float32

    def nrm(k, shape, fan_in):
        return jax.random.normal(k, shape, f32) * (fan_in ** -0.5)

    return {
        "x": jax.random.normal(ks[0], (BATCH, SEQ, D_MODEL), f32),
        "norm1_g": 1.0 + 0.05 * jax.random.normal(ks[1], (DEPTH, D_MODEL), f32),
        "w_in": nrm(ks[2], (DEPTH, D_MODEL, IN_COLS), D_MODEL),
        "b_gate": 0.05 * jax.random.normal(ks[3], (DEPTH, N_BRANCH * D_MODEL), f32),
        "lb_logits": 0.5 * jax.random.normal(ks[4], (DEPTH + 1, HG_WIDTH), f32),
        "hg_norm_g": 1.0 + 0.05 * jax.random.normal(ks[5], (DEPTH, HG_WIDTH), f32),
        "w_o_sb": nrm(ks[6], (DEPTH, SB_WIDTH, D_MODEL), SB_WIDTH),
        "w_o_hg": nrm(ks[7], (DEPTH, HG_WIDTH, D_MODEL), HG_WIDTH),
        "w_out": nrm(ks[8], (DEPTH, D_MODEL, D_MODEL), D_MODEL),
        "norm2_g": 1.0 + 0.05 * jax.random.normal(ks[9], (DEPTH, D_MODEL), f32),
        "w_ff1": nrm(ks[10], (DEPTH, D_MODEL, D_FF), D_MODEL),
        "w_ff2": nrm(ks[11], (DEPTH, D_FF, D_MODEL), D_FF),
        "final_g": 1.0 + 0.05 * jax.random.normal(ks[12], (D_MODEL,), f32),
    }

def first_block(x, norm1_g, w_in, b_gate, lb_logits, hg_norm_g, w_o_sb, w_o_hg, w_out,
              norm2_g, w_ff1, w_ff2, final_g):
    h = x.astype(jnp.float32)
    for layer in range(DEPTH):
        h = hybrid_layer(h, layer, norm1_g, w_in, b_gate, lb_logits, hg_norm_g, w_o_sb, w_o_hg,
                         w_out, norm2_g, w_ff1, w_ff2)
    return rmsnorm(h, final_g).astype(x.dtype)


DEPTH_2 = 2

GRID_W = 64
CTX_LEN = 256
N_MIXERS = 2
N_A = (DEPTH_2 + 1) // 2
N_B = DEPTH_2 // 2
MLA_HEADS = 8
QK_NOPE = 128
QK_ROPE = 64
V_DIM = 128
QK_DIM = QK_NOPE + QK_ROPE
Q_LORA = 384
KV_LORA = 256
ROPE_THETA = 10000.0
GM_CHUNK = 128
GM_GROUPS = 8
GM_HALF = 2 * D_MODEL
GM_GROUP_DIM = GM_HALF // GM_GROUPS
FFN_HIDDEN = 4 * D_MODEL
N_MOD = 6


def rmsnorm_2(x, g):
    xf = x.astype(jnp.float32)
    y = xf * lax.rsqrt(jnp.mean(xf * xf, axis=-1, keepdims=True) + EPS)
    return (y * g.astype(jnp.float32)).astype(x.dtype)

def layernorm(x, g, b):
    xf = x.astype(jnp.float32)
    mu = jnp.mean(xf, axis=-1, keepdims=True)
    var = jnp.mean(jnp.square(xf - mu), axis=-1, keepdims=True)
    y = (xf - mu) * lax.rsqrt(var + EPS)
    return (y * g.astype(jnp.float32) + b.astype(jnp.float32)).astype(x.dtype)

def modulate(x, g, shift, scale):
    return rmsnorm_2(x, g) * (1.0 + scale) + shift

def axial_rope_tables(n_tokens, dtype):
    rows = n_tokens // GRID_W
    row = jnp.repeat(jnp.arange(rows, dtype=jnp.float32), GRID_W)
    col = jnp.tile(jnp.arange(GRID_W, dtype=jnp.float32), rows)
    half = QK_ROPE // 2
    inv = ROPE_THETA ** (-jnp.arange(0, half, 2, dtype=jnp.float32) / half)
    ang_r = row[:, None] * inv[None, :]
    ang_c = col[:, None] * inv[None, :]
    ang = jnp.concatenate([ang_r, ang_r, ang_c, ang_c], axis=-1)
    return jnp.cos(ang).astype(dtype), jnp.sin(ang).astype(dtype)

def rotate_axial(x):
    a1, a2, b1, b2 = jnp.split(x, 4, axis=-1)
    return jnp.concatenate([-a2, a1, -b2, b1], axis=-1)

def rope_part(t, cos, sin):
    nope, pe = t[..., :QK_NOPE], t[..., QK_NOPE:]
    c = cos[None, :, None, :]
    s = sin[None, :, None, :]
    return jnp.concatenate([nope, pe * c + rotate_axial(pe) * s], axis=-1)

def block_attention(q, k, v, scale):
    B, Sq, H, Dk = q.shape
    nb = Sq // Q_BLOCK
    qb = q.reshape(B, nb, Q_BLOCK, H, Dk).transpose(1, 0, 2, 3, 4)

    def one(qi):
        s = jnp.einsum('bqhd,bkhd->bhqk', qi, k, preferred_element_type=jnp.float32) * scale
        p = jax.nn.softmax(s, axis=-1)
        return jnp.einsum('bhqk,bkhd->bqhd', p.astype(v.dtype), v)

    o = lax.map(one, qb)
    return o.transpose(1, 0, 2, 3, 4).reshape(B, Sq, H, v.shape[-1])

def mla_queries(h, wq_a, q_a_norm, wq_b, q_norm):
    B, S, _ = h.shape
    cq = rmsnorm_2(h @ wq_a, q_a_norm)
    q = (cq @ wq_b).reshape(B, S, MLA_HEADS, QK_DIM)
    return rmsnorm_2(q, q_norm)

def mla_keys_values(h, wkv_a, kv_a_norm, wkv_b, k_norm):
    B, S, _ = h.shape
    kv_a = h @ wkv_a
    ckv, k_pe = kv_a[..., :KV_LORA], kv_a[..., KV_LORA:]
    kv = (rmsnorm_2(ckv, kv_a_norm) @ wkv_b).reshape(B, S, MLA_HEADS, QK_NOPE + V_DIM)
    k_nope, v = kv[..., :QK_NOPE], kv[..., QK_NOPE:]
    k_pe = jnp.broadcast_to(k_pe[:, :, None, :], (B, S, MLA_HEADS, QK_ROPE))
    k = rmsnorm_2(jnp.concatenate([k_nope, k_pe], axis=-1), k_norm)
    return k, v

def mla_mixer(h_lat, h_ctx, cos, sin, wq_a, q_a_norm, wq_b, wkv_a, kv_a_norm, wkv_b,
              q_norm, k_norm, wo, with_ctx):
    B, S, _ = h_lat.shape
    scale = QK_DIM ** -0.5
    k_lat, v_lat = mla_keys_values(h_lat, wkv_a, kv_a_norm, wkv_b, k_norm)
    k_ctx, v_ctx = mla_keys_values(h_ctx, wkv_a, kv_a_norm, wkv_b, k_norm)
    k_lat = rope_part(k_lat, cos, sin)
    q_lat = rope_part(mla_queries(h_lat, wq_a, q_a_norm, wq_b, q_norm), cos, sin)
    k_all = jnp.concatenate([k_ctx, k_lat], axis=1)
    v_all = jnp.concatenate([v_ctx, v_lat], axis=1)
    o_lat = block_attention(q_lat, k_all, v_all, scale).reshape(B, S, MLA_HEADS * V_DIM) @ wo
    o_ctx = None
    if with_ctx:
        q_ctx = mla_queries(h_ctx, wq_a, q_a_norm, wq_b, q_norm)
        o_ctx = block_attention(q_ctx, k_ctx, v_ctx, scale).reshape(
            B, h_ctx.shape[1], MLA_HEADS * V_DIM) @ wo
    return o_lat, o_ctx

def gmlp_mixer(h, w_in, ln_g, ln_b, ws, bs, w_out):
    B, S, _ = h.shape
    z = jax.nn.gelu(h @ w_in, approximate=False)
    u, v = z[..., :GM_HALF], z[..., GM_HALF:]
    v = layernorm(v, ln_g, ln_b)
    vc = v.reshape(B, S // GM_CHUNK, GM_CHUNK, GM_GROUPS, GM_GROUP_DIM)
    mixed = jnp.einsum('gpq,bnqgc->bnpgc', ws, vc) + bs.T[None, None, :, :, None]
    return (u * mixed.reshape(B, S, GM_HALF)) @ w_out

def squared_relu_mlp(h, w1, w2):
    return jnp.square(jax.nn.relu(h @ w1)) @ w2

def second_inputs(seed: int = 0) -> dict:
    key = jax.random.key(seed)
    ks = jax.random.split(key, 32)
    D = D_MODEL

    def nrm(k, shape, scale):
        return jax.random.normal(k, shape, jnp.float32) * scale

    def gain(k, shape):
        return 1.0 + 0.05 * jax.random.normal(k, shape, jnp.float32)

    return {
        "x": nrm(ks[0], (BATCH, SEQ, D), 1.0),
        "c": nrm(ks[1], (BATCH, D), 1.0),
        "ctx": nrm(ks[2], (BATCH, CTX_LEN, D), 1.0),
        "c_ctx": nrm(ks[3], (D,), 1.0),
        "ada_w": nrm(ks[4], (DEPTH_2, D, N_MOD * D), 0.5 * D ** -0.5),
        "ada_b": nrm(ks[5], (DEPTH_2, N_MOD * D), 0.01),
        "norm_mix_g": gain(ks[6], (DEPTH_2, D)),
        "norm_ffn_g": gain(ks[7], (DEPTH_2, D)),
        "mla_wq_a": nrm(ks[8], (N_A, D, Q_LORA), D ** -0.5),
        "mla_q_a_norm": gain(ks[9], (N_A, Q_LORA)),
        "mla_wq_b": nrm(ks[10], (N_A, Q_LORA, MLA_HEADS * QK_DIM), Q_LORA ** -0.5),
        "mla_wkv_a": nrm(ks[11], (N_A, D, KV_LORA + QK_ROPE), D ** -0.5),
        "mla_kv_a_norm": gain(ks[12], (N_A, KV_LORA)),
        "mla_wkv_b": nrm(ks[13], (N_A, KV_LORA, MLA_HEADS * (QK_NOPE + V_DIM)), KV_LORA ** -0.5),
        "mla_q_norm": gain(ks[14], (N_A, QK_DIM)),
        "mla_k_norm": gain(ks[15], (N_A, QK_DIM)),
        "mla_wo": nrm(ks[16], (N_A, MLA_HEADS * V_DIM, D), (MLA_HEADS * V_DIM) ** -0.5),
        "gm_w_in": nrm(ks[17], (N_B, D, 2 * GM_HALF), D ** -0.5),
        "gm_ln_g": gain(ks[18], (N_B, GM_HALF)),
        "gm_ln_b": nrm(ks[19], (N_B, GM_HALF), 0.02),
        "gm_ws": nrm(ks[20], (N_B, GM_GROUPS, GM_CHUNK, GM_CHUNK), GM_CHUNK ** -0.5),
        "gm_bs": gain(ks[21], (N_B, GM_GROUPS, GM_CHUNK)),
        "gm_w_out": nrm(ks[22], (N_B, GM_HALF, D), GM_HALF ** -0.5),
        "ffn_w1": nrm(ks[23], (DEPTH_2, D, FFN_HIDDEN), D ** -0.5),
        "ffn_w2": nrm(ks[24], (DEPTH_2, FFN_HIDDEN, D), FFN_HIDDEN ** -0.5),
    }

def second_block(x, c, ctx, c_ctx, ada_w, ada_b, norm_mix_g, norm_ffn_g,
              mla_wq_a, mla_q_a_norm, mla_wq_b, mla_wkv_a, mla_kv_a_norm, mla_wkv_b,
              mla_q_norm, mla_k_norm, mla_wo,
              gm_w_in, gm_ln_g, gm_ln_b, gm_ws, gm_bs, gm_w_out,
              ffn_w1, ffn_w2):
    S = x.shape[1]
    cos, sin = axial_rope_tables(S, x.dtype)
    silu_c = jax.nn.silu(c)
    silu_cc = jax.nn.silu(c_ctx)
    y = ctx
    for i in range(DEPTH_2):
        with_ctx = i < DEPTH_2 - 1
        use_mla = (i % N_MIXERS) == 0
        j = i // N_MIXERS
        m_lat = (silu_c @ ada_w[i] + ada_b[i])[:, None, :]
        m_ctx = silu_cc @ ada_w[i] + ada_b[i]
        sh_m, sc_m, g_m, sh_f, sc_f, g_f = jnp.split(m_lat, N_MOD, axis=-1)
        csh_m, csc_m, cg_m, csh_f, csc_f, cg_f = jnp.split(m_ctx, N_MOD, axis=-1)

        h_lat = modulate(x, norm_mix_g[i], sh_m, sc_m)
        if use_mla:
            h_ctx = modulate(y, norm_mix_g[i], csh_m, csc_m)
            o_lat, o_ctx = mla_mixer(h_lat, h_ctx, cos, sin, mla_wq_a[j], mla_q_a_norm[j],
                                     mla_wq_b[j], mla_wkv_a[j], mla_kv_a_norm[j], mla_wkv_b[j],
                                     mla_q_norm[j], mla_k_norm[j], mla_wo[j], with_ctx)
        else:
            o_lat = gmlp_mixer(h_lat, gm_w_in[j], gm_ln_g[j], gm_ln_b[j], gm_ws[j], gm_bs[j],
                               gm_w_out[j])
            o_ctx = None
            if with_ctx:
                h_ctx = modulate(y, norm_mix_g[i], csh_m, csc_m)
                o_ctx = gmlp_mixer(h_ctx, gm_w_in[j], gm_ln_g[j], gm_ln_b[j], gm_ws[j], gm_bs[j],
                                   gm_w_out[j])
        x = x + g_m * o_lat
        x = x + g_f * squared_relu_mlp(modulate(x, norm_ffn_g[i], sh_f, sc_f), ffn_w1[i], ffn_w2[i])
        if with_ctx:
            y = y + cg_m * o_ctx
            y = y + cg_f * squared_relu_mlp(modulate(y, norm_ffn_g[i], csh_f, csc_f),
                                            ffn_w1[i], ffn_w2[i])
    return x


def setup_inputs(seed=0):
    out = dict(first_inputs(seed))
    for name, value in second_inputs(seed + 1).items():
        if name != "x":
            out[name + "_2"] = value
    return out


def reference(
    x, norm1_g, w_in, b_gate, lb_logits, hg_norm_g, w_o_sb, w_o_hg, w_out, norm2_g, w_ff1,
    w_ff2, final_g, c_2, ctx_2, c_ctx_2, ada_w_2, ada_b_2, norm_mix_g_2, norm_ffn_g_2,
    mla_wq_a_2, mla_q_a_norm_2, mla_wq_b_2, mla_wkv_a_2, mla_kv_a_norm_2, mla_wkv_b_2,
    mla_q_norm_2, mla_k_norm_2, mla_wo_2, gm_w_in_2, gm_ln_g_2, gm_ln_b_2, gm_ws_2, gm_bs_2,
    gm_w_out_2, ffn_w1_2, ffn_w2_2,
):
    x = first_block(
        x, norm1_g, w_in, b_gate, lb_logits, hg_norm_g, w_o_sb, w_o_hg, w_out, norm2_g, w_ff1,
        w_ff2, final_g,
    )
    return second_block(
        x, c_2, ctx_2, c_ctx_2, ada_w_2, ada_b_2, norm_mix_g_2, norm_ffn_g_2, mla_wq_a_2,
        mla_q_a_norm_2, mla_wq_b_2, mla_wkv_a_2, mla_kv_a_norm_2, mla_wkv_b_2, mla_q_norm_2,
        mla_k_norm_2, mla_wo_2, gm_w_in_2, gm_ln_g_2, gm_ln_b_2, gm_ws_2, gm_bs_2, gm_w_out_2,
        ffn_w1_2, ffn_w2_2,
    )


_drawn_inputs = setup_inputs


def setup_inputs(seed=0):
    import zlib

    import numpy as np

    out = dict(_drawn_inputs(seed))
    spreads = {}
    factors = {'b_gate': 6.064,
     'lb_logits': 2.766,
     'hg_norm_g': 3.349,
     'ctx_2': 4.913,
     'norm_mix_g_2': 3.259,
     'mla_q_a_norm_2': 8.0,
     'mla_kv_a_norm_2': 8.0,
     'mla_q_norm_2': 8.0,
     'mla_k_norm_2': 8.0,
     'gm_ln_g_2': 5.454,
     'gm_ln_b_2': 24.207,
     'gm_bs_2': 5.698,
     'norm_ffn_g_2': 4.561}
    for name, (base, spread) in spreads.items():
        noise = np.random.default_rng([zlib.crc32(name.encode()), seed]).standard_normal(out[name].shape)
        drawn = base * np.exp(spread * noise) if base else spread * noise
        out[name] = __import__('jax').numpy.asarray(drawn.astype(out[name].dtype))
    for name, factor in factors.items():
        out[name] = (out[name] * factor).astype(out[name].dtype)
    return out
```

```python
from contextlib import ExitStack

import concourse.bass as bass
from concourse import mybir

P = 128
T = 512
TC = 256
TK = T + TC
KT = 8
NC4 = T // P
SB_HEADS = 8
HG_HEADS = 4
MLA_HEADS = 8
EPS = 1e-6
D_MODEL = 1024
UNIT = 1024
W_SLOTS = 4
RAW_SLOTS = 4
CHUNK_UNITS = 2
HGRN_LEVELS = (64, 32, 16, 8, 4, 2, 1)
ADA_CHUNKS = 28
ADA_PER_IT = 7

F32 = mybir.dt.float32
F32R = mybir.dt.float32r
I32 = mybir.dt.int32
ALU = mybir.AluOpType
ACT = mybir.ActivationFunctionType

STREAM = [
    ("sb_q", 4), ("sb_k", 4), ("sb_v", 4), ("hg_f", 4), ("hg_i", 4), ("hg_q", 4), ("hg_g", 4),
    ("merge", 24), ("w_out", 8), ("ff0", 64),
    ("q_a", 3), ("kv_a", 3), ("q_b", 5), ("k_b", 2), ("v_b", 2), ("mla_o", 8), ("ff1", 64),
    ("gm_v", 16), ("gm_u", 32), ("ff2", 64),
]
N_UNITS = sum(n for _, n in STREAM)
FIRST = {}
_at = 0
for _name, _n in STREAM:
    FIRST[_name] = _at
    _at += _n

VECS = {}
_at = 0
for _name, _n in [
    ("norm1", 8), ("gate_a", 8), ("gate_b", 8), ("lb0", 4), ("lb1", 4), ("hg_norm", 4), ("norm2", 8),
    ("final", 8), ("mix0", 8), ("ffn0", 8), ("mix1", 8), ("ffn1", 8), ("q_a_norm", 3),
    ("kv_a_norm", 2), ("q_nope", 1), ("q_rope", 1), ("k_nope", 1), ("k_rope", 1), ("ln_g", 16),
    ("ln_b", 16), ("ada_b", 4 * ADA_CHUNKS), ("c", 8), ("c_ctx", 8),
]:
    VECS[_name] = (_at, _n)
    _at += _n
N_VECS = _at

CONSTS = {}
_at = 0
for _name, _n in [("neg_tri", P), ("big_neg", P), ("strict", P), ("levels", 8 * P), ("restart", T)]:
    CONSTS[_name] = (_at, _n)
    _at += _n
N_CONST_A = _at
_at = 0
for _name, _n in [("rot", P), ("cos", T), ("sin", T), ("half", 2)]:
    CONSTS[_name] = (_at, _n)
    _at += _n
N_CONST_B = _at


def build_program(nc, weights, ada, x_t, ctx_t, vecs_in, const_a, const_b, ident_in, ws_t, bs_in, out):
    ctx = ExitStack()
    with ctx:
        KB = 1024
        a0 = (nc.sbuf_base + 31) // 32 * 32

        def at(name, off, cols, dt=F32):
            return nc.alloc_sbuf_tensor_at(name, [P, cols], dt, offset=a0 + off)

        raw = at("raw", 0, RAW_SLOTS * 2 * UNIT)
        w_hi = at("w_hi", 32 * KB, W_SLOTS * UNIT, F32R)
        w_lo = at("w_lo", 48 * KB, W_SLOTS * UNIT, F32R)
        XH0, HH0, HL0, H0 = 64 * KB, 96 * KB, 112 * KB, 128 * KB
        M0 = 144 * KB
        x_hi = at("x_hi", XH0, KT * T, F32R)
        x_lo = at("x_lo", XH0 + 16 * KB, KT * T, F32R)
        h_hi = at("h_hi", HH0, KT * T, F32R)
        h_lo = at("h_lo", HL0, KT * T, F32R)
        hres = at("hres", H0, KT * T)
        n_sq = at("n_sq", HL0, 2 * TK)
        n_acc = at("n_acc", HL0 + 6 * KB, TK)
        n_r = at("n_r", HL0 + 9 * KB, TK)
        n_t = at("n_t", HL0 + 12 * KB, 2 * T)
        S0 = M0 + 60 * KB
        ones = at("ones", S0, P)
        ident = at("ident", S0 + 512, P)
        neg_ones = at("neg_ones", S0 + 1024, P)
        vecs = at("vecs", S0 + 1536, N_VECS)
        mods = at("mods", S0 + 1536 + 4 * N_VECS + 12, 4 * ADA_CHUNKS)
        derived = at("derived", S0 + 1536 + 4 * N_VECS + 12 + 448, 120)

        cst_a = at("cst_a", M0, N_CONST_A)
        sb_q = at("sb_q", M0 + 8 * KB, 4 * T)
        sb_k = at("sb_k", M0 + 16 * KB, 4 * T)
        sb_v = at("sb_v", M0 + 24 * KB, 4 * T)
        sb_e = at("sb_e", M0 + 32 * KB, 1280)
        sb_l = at("sb_l", M0 + 37 * KB, 1280)
        sb_sp = at("sb_sp", M0 + 42 * KB, 2 * 1280)
        sb_w = at("sb_w", M0 + 52 * KB, 1280)
        hg_b = at("hg_b", M0 + 8 * KB, 4 * T)
        hg_k = at("hg_k", M0 + 16 * KB, 4 * T)
        hg_q = at("hg_q", M0 + 24 * KB, 4 * T)
        hg_v = at("hg_v", M0 + 32 * KB, 4 * T)
        hg_a = at("hg_a", M0 + 40 * KB, 4 * T)
        hg_p = at("hg_p", M0 + 48 * KB, 4 * T)
        hg_s = at("hg_s", M0 + 56 * KB, 2 * T)
        hg_off = at("hg_off", H0, 4 * 6 * P)
        hg_edge = at("hg_edge", H0 + 12 * KB, 2 * 4 * P)
        m_hi = at("m_hi", M0, KT * T, F32R)
        m_lo = at("m_lo", M0 + 16 * KB, KT * T, F32R)
        m_t = at("m_t", M0 + 32 * KB, 6 * T)
        ada_w = at("ada_w", M0, 2 * 4096)
        ada_acc = at("ada_acc", M0 + 32 * KB, ADA_PER_IT * T)
        f_r = at("f_r", M0 + 46 * KB, 2 * T)
        f_s = at("f_s", M0 + 50 * KB, 2 * T)
        cst_b = at("cst_b", M0, N_CONST_B)
        cq_hi = at("cq_hi", M0 + 5 * KB, 3 * T, F32R)
        cq_lo = at("cq_lo", M0 + 11 * KB, 3 * T, F32R)
        ck_hi = at("ck_hi", M0 + 17 * KB, 2 * TK, F32R)
        ck_lo = at("ck_lo", M0 + 23 * KB, 2 * TK, F32R)
        kpe = at("kpe", M0 + 29 * KB, TK)
        ml_v = at("ml_v", M0 + 36 * KB, 6 * 1024)
        ctxx = at("ctxx", M0 + 36 * KB, KT * TC)
        cq_raw = at("cq_raw", M0 + 44 * KB, 3 * T)
        ck_raw = at("ck_raw", M0 + 50 * KB, 2 * TK)
        kpe_raw = at("kpe_raw", M0 + 56 * KB, TK)
        kpe_sq = at("kpe_sq", M0 + 32 * KB, TK)
        q_sq = at("q_sq", M0 + 36 * KB, 3 * T)
        q_rp = at("q_rp", M0 + 42 * KB, 2 * T)
        k_sq = at("k_sq", M0 + 46 * KB, TK)
        k_r = at("k_r", M0 + 49 * KB, TK)
        q_tmp = at("q_tmp", HH0 + 24 * KB, T)
        c_hi = at("c_hi", HH0, KT * TC, F32R)
        c_lo = at("c_lo", HH0 + 8 * KB, KT * TC, F32R)
        qn = at("qn", XH0, MLA_HEADS * T)
        qr = at("qr", XH0 + 16 * KB, 4 * T)
        kr_a = at("kr_a", XH0 + 24 * KB, 2 * TK)
        kn = at("kn", HH0, MLA_HEADS * TK)
        kr_b = at("kr_b", HH0 + 24 * KB, 2 * TK)
        at_p = at("at_p", M0, 2 * TK)
        at_pt = at("at_pt", M0 + 6 * KB, 6 * T)
        o_hi = at("o_hi", XH0, KT * T, F32R)
        o_lo = at("o_lo", M0 + 18 * KB, KT * T, F32R)
        gv = at("gv", M0, 4 * 2048)
        wst = at("wst", M0 + 32 * KB, KT * P)
        rs_b = at("rs_b", M0 + 36 * KB, KT * P)
        bs_b = at("bs_b", M0 + 40 * KB, KT * P)
        extra = at("extra", M0 + 44 * KB, 16 * P)
        g_u = at("g_u", M0 + 52 * KB, T)
        g_t = at("g_t", M0 + 54 * KB, T)
        g_s = at("g_s", M0 + 56 * KB, T)
        g_st = at("g_st", M0 + 58 * KB, 64)
        bs_row = at("bs_row", M0 + 52 * KB, KT * P)

        ps = ctx.enter_context(nc.psum_tensor("ps", [P, 8, T], F32))

        names = (
            ["raw_in%d" % i for i in range(RAW_SLOTS)]
            + ["split_turn", "w_high", "w_ready", "unit_started", "a_full", "a_free", "d_full", "d_free"]
            + ["x_loaded", "small_loaded", "ones_set", "act_order", "dve_order"]
            + ["n_squared", "n_added", "n_total", "n_log", "n_scale", "n_scaled", "n_high", "n_done"]
            + ["sp_scores", "sp_log", "sp_soft", "sp_decay", "sp_weights", "sp_out", "sp_high", "sp_low"]
            + ["hp_zero", "lb_diff", "lb_ready", "silu_c", "silu_done", "hf_sig", "hf_f", "hf_k", "hf_qs", "hf_log", "hf_b"]
            + ["lv_diff", "lv_exp", "lv_pair", "lv_score", "lv_kept", "off_diff", "off_exp", "ho_ready",
               "off_score", "off_kept", "ho_out", "ho_sq", "ho_total", "ho_log", "ho_scale", "ho_norm",
               "hg_sig", "hg_gate", "ho_high", "ho_low"]
            + ["mg_gate", "mg_sum", "mg_high", "mg_low"]
            + ["f_square", "f_high", "f_low", "ada_in0", "ada_in1", "ada_used", "ada_step", "ada_cols",
               "bank7_free", "mod_ready"]
            + ["ctx_loaded", "cstb_loaded", "qb_copy", "qb_sums", "qb_rot", "qb_rope", "rq_log", "rq_exp",
               "rq_ready", "kpe_scaled", "kpe_squared", "kpe_rot", "kpe_done", "kb_copy", "kb_sum", "kb_r",
               "kb_norm"]
            + ["s_full", "s_max", "s_exp", "p_norm", "t_full", "t_copied", "o_full", "o_high", "o_low"]
            + ["gm_loaded", "gm_rows", "gm_copy", "gm_extra", "gv_var", "gv_log", "gv_rstd", "gv_norm", "gu_gelu",
               "gu_mul", "gu_high", "gu_low", "stored"]
        )
        sem = {n: ctx.enter_context(nc.semaphore(n)) for n in names}

        def v(name, j=0, n=1):
            o = VECS[name][0] + j
            return vecs[:, o:o + n]

        def tile(t, j, w=T):
            return t[:, j * w:(j + 1) * w]

        D_C, D_CC, D_LB, D_OLB, D_GAIN, D_RQ, D_AT = 0, 8, 16, 20, 24, 64, 96

        def dcol(o, n=1):
            return derived[:, o:o + n]

        def mod_col(layer, part, j):
            fb = part * KT + j
            chunk = fb // 4
            return (layer * 2 + chunk // 6) * 4 * ADA_PER_IT + (chunk % 6) * 4 + fb % 4

        def ctx_col(part, j):
            fb = part * KT + j
            return (fb // 4) * 4 * ADA_PER_IT + 24 + fb % 4

        def mcol(c):
            return mods[:, c:c + 1]

        A_TILES = [("sb_qk", 8), ("sb_v", 4), ("hg_f", 4), ("hg_i", 4), ("merge", 16), ("ff0", 32),
                   ("q_a", 3), ("kv_a", 6), ("q_b", 12), ("k_b", 16), ("v_b", 12), ("ff1", 32),
                   ("gm_v", 16), ("gm_u", 16), ("ff2", 32)]
        D_TILES = [("hg_q", 4), ("hg_g", 4), ("merge", 16), ("w_out", 8), ("ff0", 32), ("mla_o", 8),
                   ("ff1", 32), ("gm_u", 32), ("ff2", 32)]

        def firsts(table):
            n, found = 0, {}
            for name, k in table:
                found[name] = n
                n += k
            found["end"] = n
            return found

        A = firsts(A_TILES)
        D = firsts(D_TILES)
        NORMS = [("norm1", 8), ("norm2", 8), ("final", 8), ("mix0", 8), ("ctx", 8), ("cq", 3), ("ck", 2),
                 ("ffn0", 8), ("mix1", 8), ("ffn1", 8)]
        NSQ = firsts([(n, k - 1) for n, k in NORMS])
        NT = firsts(NORMS)
        NI = {n: i for i, (n, _) in enumerate(NORMS)}

        def wait_pos(eng, s, value):
            if not isinstance(value, int) or value > 0:
                eng.wait_ge(sem[s], value)

        block = ctx.enter_context(nc.Block())

        @block.sync
        def _(sp):
            sp.dma_start(hres[:, :], x_t).then_inc(sem["x_loaded"], 16)

            def load_chunk(c, slot):
                sp.dma_start(raw[:, slot * 2 * UNIT:(slot + 1) * 2 * UNIT], weights[c, :, :])\
                    .then_inc(sem["raw_in%d" % slot], 16)

            load_chunk(0, 0)
            sp.dma_start(vecs[:, :], vecs_in).then_inc(sem["small_loaded"], 16)
            sp.dma_start(ident[:, :], ident_in).then_inc(sem["small_loaded"], 16)
            sp.dma_start(cst_a[:, :], const_a).then_inc(sem["small_loaded"], 16)
            for c in range(1, RAW_SLOTS):
                load_chunk(c, c)
            n_chunks = (N_UNITS + 1) // CHUNK_UNITS
            rounds = n_chunks // RAW_SLOTS
            with sp.Fori(1, rounds) as r:
                for s in range(RAW_SLOTS):
                    sp.wait_ge(sem["w_ready"], r * 8 - 8 + 2 * s + 2)
                    load_chunk(r * RAW_SLOTS + s, s)
            for c in range(rounds * RAW_SLOTS, n_chunks):
                sp.wait_ge(sem["w_ready"], 2 * (c - RAW_SLOTS) + 2)
                load_chunk(c, c % RAW_SLOTS)

        @block.gpsimd
        def _(pool):
            def split_unit(u, k, first=False):
                if k % 2 == 0:
                    slot = k // 2
                    pool.wait_ge(sem["raw_in%d" % slot], (u - k) * 2 + 16)
                src = raw[:, k * UNIT:(k + 1) * UNIT]
                s = k % W_SLOTS
                if not first:
                    pool.wait_ge(sem["unit_started"], u - W_SLOTS + 2)
                pool.sem_inc(sem["split_turn"], 1)
                pool.tensor_scalar(tile(w_hi, s, UNIT), src, 1.0, 1.0, ALU.mult, ALU.mult)\
                    .then_inc(sem["w_high"], 1)
                pool.wait_ge(sem["w_high"], u + 1)
                pool.tensor_tensor(tile(w_lo, s, UNIT), src, tile(w_hi, s, UNIT).bitcast(F32), ALU.subtract)\
                    .then_inc(sem["w_ready"], 1)

            for u in range(8):
                split_unit(u, u, u < W_SLOTS)
            with pool.Fori(1, N_UNITS // 8) as r:
                for k in range(8):
                    split_unit(r * 8 + k, k)
            for u in range(N_UNITS // 8 * 8, N_UNITS):
                split_unit(u, u % 8)

        @block.tensor
        def _(pe):
            def w(t, u, j):
                return t[:, (u % W_SLOTS) * UNIT + j * P:(u % W_SLOTS) * UNIT + (j + 1) * P]

            class Units:
                now = -1

            def start_unit(u, ready=None):
                pe.wait_ge(sem["w_ready"], (u if ready is None else ready) + 1)

            def group(dst, u, parts, first=True, last=True, new_unit=True, each=None, ready=None):
                if new_unit:
                    start_unit(u, ready)
                n = len(parts)
                for i, (j, hi, lo) in enumerate(parts):
                    if each is not None:
                        each(i)
                    m = pe.matmul(dst, w(w_hi, u, j), lo, start=first and i == 0, stop=False)
                    if new_unit and i == 0:
                        m.then_inc(sem["unit_started"], 1)
                    pe.matmul(dst, w(w_hi, u, j), hi, start=False, stop=False)
                    m = pe.matmul(dst, w(w_lo, u, j), hi, start=False, stop=last and i == n - 1)
                return m

            def a_bank(n):
                wait_pos(pe, "a_free", n - 3)
                return ps[:, n % 4, :]

            def d_bank(n):
                wait_pos(pe, "d_free", n - 1)
                return ps[:, 4 + n % 2, :]

            def x_parts(hi=x_hi, lo=x_lo, k=KT, w_=T, first_tile=0):
                return [(first_tile + j, tile(hi, j, w_), tile(lo, j, w_)) for j in range(k)]

            def stat(name, w_=T):
                i = NI[name]
                pe.wait_ge(sem["n_added"], NSQ[name] + dict(NORMS)[name] - 1)
                if i:
                    pe.wait_ge(sem["n_scale"], i)
                if w_ > T:
                    pe.matmul(ps[:, 6, :], ones[:, :], n_acc[:, 0:T], start=True, stop=True)
                    m = pe.matmul(ps[:, 7, 0:w_ - T], ones[:, :], n_acc[:, T:w_], start=True, stop=True)
                else:
                    m = pe.matmul(ps[:, 6, 0:w_], ones[:, :], n_acc[:, 0:w_], start=True, stop=True)
                m.then_inc(sem["n_total"], 1)

            def norm_waits(name):
                def each(i):
                    pe.wait_ge(sem["n_done"], NT[name] + i + 1)
                return each

            def feature_major(first_u, n, a0_, pool="a", each=None):
                for j in range(n):
                    dst = a_bank(a0_ + j) if pool == "a" else d_bank(a0_ + j)
                    group(dst, first_u + j, x_parts(), each=each if j == 0 else None)\
                        .then_inc(sem[pool + "_full"], 1)

            def token_major(first_u, a0_, n_cols=1):
                for cb in range(n_cols):
                    for uu in range(4):
                        u = first_u + cb * 4 + uu
                        start_unit(u)
                        s0 = (u % W_SLOTS) * UNIT
                        for c in range(NC4):
                            n = a0_ + cb * 4 + c
                            dst = a_bank(n) if uu == 0 else ps[:, n % 4, :]
                            for kk in range(2):
                                k = uu * 2 + kk
                                xh = x_hi[:, k * T + c * P:k * T + (c + 1) * P]
                                xl = x_lo[:, k * T + c * P:k * T + (c + 1) * P]
                                wh = w_hi[:, s0 + kk * T:s0 + (kk + 1) * T]
                                wl = w_lo[:, s0 + kk * T:s0 + (kk + 1) * T]
                                m = pe.matmul(dst, xl, wh, start=k == 0, stop=False)
                                if c == 0 and kk == 0:
                                    m.then_inc(sem["unit_started"], 1)
                                pe.matmul(dst, xh, wh, start=False, stop=False)
                                m = pe.matmul(dst, xh, wl, start=False, stop=k == KT - 1)
                            if uu == 3:
                                m.then_inc(sem["a_full"], 1)

            pe.wait_ge(sem["ones_set"], 2)
            stat("norm1")
            feature_major(FIRST["sb_q"], 8, A["sb_qk"], each=norm_waits("norm1"))
            token_major(FIRST["sb_v"], A["sb_v"])

            def z(h, i):
                b = (h % 2) * 3
                if i == 3:
                    return ps[:, b + 1, 0:P]
                return ps[:, b + i, i * P:T]

            def head_half(h):
                return slice(64 * (h % 2), 64 * (h % 2) + 64)

            def sb_scores(h):
                hp = head_half(h)
                if h < 2:
                    pe.wait_ge(sem["a_free"], A["hg_f"])
                else:
                    pe.wait_ge(sem["sp_weights"], 4 * (h - 1))
                for i in (0, 1, 2, 3):
                    m = pe.matmul(z(h, i), sb_k[hp, (h // 2) * T + i * P:(h // 2) * T + (i + 1) * P],
                                  sb_q[hp, (h // 2) * T + i * P:(h // 2 + 1) * T], start=i != 3, stop=True,
                                  skip_group_check=True)
                m.then_inc(sem["sp_scores"], 1)

            def sb_decay(h):
                seg = [0, 512, 896, 1152]
                buf = (h % 2) * 1280
                pe.wait_ge(sem["sp_soft"], 4 * h + 4)
                for i in range(4):
                    zi = z(h, i)
                    pe.matmul(zi[:, 0:P], ident[:, :], cst("big_neg"), start=False, stop=True,
                              skip_group_check=True)
                    m = pe.matmul(zi, cst("neg_tri"), sb_sp[:, buf + seg[i]:buf + seg[i] + T - i * P],
                                  start=False, stop=True, skip_group_check=True)
                    for i2 in range(i + 1, 4):
                        m = pe.matmul(zi[:, (i2 - i) * P:T - i * P], cst("neg_one"),
                                      sb_sp[:, buf + seg[i2]:buf + seg[i2] + T - i2 * P],
                                      start=False, stop=True, skip_group_check=True)
                m.then_inc(sem["sp_decay"], 1)

            def sb_values(h):
                seg = [0, 512, 896, 1152]
                dst = ps[head_half(h), 6 + h % 2, :]
                if h >= 2:
                    pe.wait_ge(sem["sp_low"], h - 1)
                for i in range(4):
                    pe.wait_ge(sem["sp_weights"], 4 * h + i + 1)
                    m = pe.matmul(dst[:, i * P:T], sb_v[:, i * T + h * 64:i * T + (h + 1) * 64],
                                  sb_w[:, seg[i]:seg[i] + T - i * P], start=i == 0, stop=i == 3,
                                  skip_group_check=True)
                m.then_inc(sem["sp_out"], 1)

            def cst(name, j=0, n=P):
                if name == "neg_one":
                    return neg_ones[:, :]
                o = CONSTS[name][0] + j
                return cst_a[:, o:o + n]

            sb_scores(0)
            for h in range(SB_HEADS):
                if h + 1 < SB_HEADS:
                    sb_scores(h + 1)
                sb_decay(h)
                sb_values(h)

            pe.wait_ge(sem["sp_weights"], 4 * SB_HEADS)
            for j in range(4):
                group(a_bank(A["hg_f"] + j), FIRST["hg_f"] + j, x_parts()).then_inc(sem["a_full"], 1)
            token_major(FIRST["hg_i"], A["hg_i"])
            for j in range(4):
                group(d_bank(D["hg_q"] + j), FIRST["hg_q"] + j, x_parts()).then_inc(sem["d_full"], 1)

            pe.wait_ge(sem["a_free"], A["merge"])
            pe.wait_ge(sem["d_free"], D["hg_g"])
            pe.wait_ge(sem["sp_low"], SB_HEADS)
            for lv in range(len(HGRN_LEVELS) + 1):
                for h in range(HG_HEADS):
                    bank = (lv % 2) * 4 + h
                    if lv >= 2:
                        pe.wait_ge(sem["lv_kept"], (lv - 2) * 4 + h + 1)
                    if lv == 0:
                        pe.wait_ge(sem["hf_k"], 4)
                        pe.wait_ge(sem["d_free"], D["hg_q"] + 4)
                    else:
                        pe.wait_ge(sem["lv_pair"], ((lv - 1) * 2 + h // 2 + 1))
                    for c in range(NC4):
                        o = h * T + c * P
                        if lv == 0:
                            l, r = hg_k[:, o:o + P], hg_q[:, o:o + P]
                        else:
                            l = r = hg_a[:, o:o + P]
                        m = pe.matmul(ps[:, bank, c * P:(c + 1) * P], l, r, start=True, stop=True)
                    m.then_inc(sem["lv_score"], 1)
            for h in range(HG_HEADS):
                pe.wait_ge(sem["ho_ready"], h + 1)
                b = (h % 2) * 2
                if h < 2:
                    pe.wait_ge(sem["lv_kept"], 4 * len(HGRN_LEVELS))
                else:
                    pe.wait_ge(sem["off_kept"], h - 1)
                km = lambda c: hg_k[:, h * T + c * P:h * T + (c + 1) * P]
                qp = lambda c: hg_q[:, h * T + c * P:h * T + (c + 1) * P]
                k0 = hg_edge[:, h * P:(h + 1) * P]
                q3 = hg_edge[:, (4 + h) * P:(5 + h) * P]
                pairs = [(km(0), qp(1)), (km(2), qp(3)), (k0, qp(2)), (k0, q3), (km(1), qp(2)), (km(1), q3)]
                for n, (l, r) in enumerate(pairs):
                    bank, o = b + n // 4, (n % 4) * P
                    m = pe.matmul(ps[:, bank, o:o + P], l, r, start=True, stop=True)
                m.then_inc(sem["off_score"], 1)
            pe.wait_ge(sem["lv_kept"], 4 * (len(HGRN_LEVELS) + 1))
            OFF = {(0, 1): 0, (2, 3): 1, (0, 2): 2, (0, 3): 3, (1, 2): 4, (1, 3): 5}
            for h in range(HG_HEADS):
                pe.wait_ge(sem["off_kept"], h + 1)
                for tc in range(NC4):
                    for sc in range(tc + 1):
                        if sc == tc:
                            r = hg_p[:, h * T + tc * P:h * T + (tc + 1) * P]
                        else:
                            o = (h * 6 + OFF[(sc, tc)]) * P
                            r = hg_off[:, o:o + P]
                        m = pe.matmul(ps[:, 4 + h, tc * P:(tc + 1) * P],
                                      hg_v[:, sc * T + h * P:sc * T + (h + 1) * P], r,
                                      start=sc == 0, stop=sc == tc)
                m.then_inc(sem["ho_out"], 1)
            for h in range(HG_HEADS):
                pe.wait_ge(sem["ho_sq"], h + 1)
                if h == 0:
                    pe.wait_ge(sem["off_kept"], HG_HEADS)
                pe.matmul(ps[:, h, :], ones[:, :], tile(hg_b, h), start=True, stop=True)\
                    .then_inc(sem["ho_total"], 1)
            pe.wait_ge(sem["ho_norm"], HG_HEADS)
            for j in range(4):
                group(d_bank(D["hg_g"] + j), FIRST["hg_g"] + j, x_parts()).then_inc(sem["d_full"], 1)

            pe.wait_ge(sem["ho_log"], HG_HEADS)
            for j in range(KT):
                u = FIRST["merge"] + 3 * j
                for g in range(2):
                    group(a_bank(A["merge"] + 2 * j + g), u + g, x_parts()).then_inc(sem["a_full"], 1)
                if j == 0:
                    pe.wait_ge(sem["sp_low"], SB_HEADS)
                    pe.wait_ge(sem["ho_low"], HG_HEADS)
                branch = lambda g: [(4 * g + k, tile(h_hi, 4 * g + k), tile(h_lo, 4 * g + k)) for k in range(4)]
                group(d_bank(D["merge"] + 2 * j), u + 2, branch(0)).then_inc(sem["d_full"], 1)
                group(d_bank(D["merge"] + 2 * j + 1), u + 2, branch(1), new_unit=False)\
                    .then_inc(sem["d_full"], 1)

            def merged(i):
                pe.wait_ge(sem["mg_low"], i + 1)
            for j in range(KT):
                group(d_bank(D["w_out"] + j), FIRST["w_out"] + j, x_parts(m_hi, m_lo),
                      each=merged if j == 0 else None).then_inc(sem["d_full"], 1)

            def feed_forward(name, norm, n_ff, with_ada):
                u0, a0_, d0_ = FIRST[name], A[name], D[name]
                with pe.Fori(0, 4) as it:
                    for j in range(8):
                        n = a0_ + it * 8 + j
                        pe.wait_ge(sem["a_free"], n - 3)
                        parts = x_parts()
                        group(ps[:, (a0_ + j) % 4, :], u0 + j, parts, ready=u0 + it * 16 + j,
                              each=norm_waits(norm) if j == 0 else None).then_inc(sem["a_full"], 1)
                    for j in range(8):
                        n = d0_ + it * 8 + j
                        pe.wait_ge(sem["d_free"], n - 1)

                        def hidden(i):
                            pe.wait_ge(sem["f_low"], it * 8 + n_ff * 32 + i + 1)
                        group(ps[:, 4 + (d0_ + j) % 2, :], u0 + 8 + j, x_parts(h_hi, h_lo),
                              ready=u0 + it * 16 + 8 + j, each=hidden if j == 0 else None)\
                            .then_inc(sem["d_full"], 1)
                    if with_ada:
                        pe.wait_ge(sem["ada_step"], it * 8 * ADA_PER_IT + 8 * ADA_PER_IT)
                        pe.wait_ge(sem["bank7_free"], it + 1)
                        for c in range(4 * ADA_PER_IT):
                            m = pe.matmul(ps[:, 7, c:c + 1], ada_acc[:, c * P:(c + 1) * P], ones[:, 0:1],
                                          start=True, stop=True)
                        m.then_inc(sem["ada_cols"], 1)

            stat("norm2")
            feed_forward("ff0", "norm2", 0, True)
            stat("final")

            stat("mix0")
            stat("ctx", TC)
            for j in range(3):
                group(a_bank(A["q_a"] + j), FIRST["q_a"] + j, x_parts(), each=norm_waits("mix0") if j == 0 else None)\
                    .then_inc(sem["a_full"], 1)
            for j in range(3):
                n = A["kv_a"] + 2 * j
                group(a_bank(n), FIRST["kv_a"] + j, x_parts()).then_inc(sem["a_full"], 1)
                group(a_bank(n + 1)[:, 0:TC], FIRST["kv_a"] + j, x_parts(c_hi, c_lo, w_=TC), new_unit=False,
                      each=norm_waits("ctx") if j == 0 else None).then_inc(sem["a_full"], 1)
            pe.wait_ge(sem["kpe_scaled"], 1)
            pe.wait_ge(sem["cstb_loaded"], 16)
            pe.matmul(ps[:, 4, :], cst_b[:, 0:P], kpe[:, TC:TK], start=True, stop=True).then_inc(sem["kpe_rot"], 1)
            stat("cq")
            stat("ck", TK)
            for b in range(12):
                pr, w_in = b // 3, b % 3
                dst = a_bank(A["q_b"] + b)
                m = None
                for k in range(3):
                    t = 3 * b + k
                    u = FIRST["q_b"] + t // 8
                    if b == 0:
                        pe.wait_ge(sem["n_done"], NT["cq"] + k + 1)
                    m = group(dst, u, [(t % 8, tile(cq_hi, k), tile(cq_lo, k))], first=k == 0, last=k == 2,
                              new_unit=t % 8 == 0)
                m.then_inc(sem["a_full"], 1)
                if w_in == 2:
                    pe.wait_ge(sem["a_free"], A["q_b"] + 3 * pr + 3)
                    for hh in range(2):
                        own = cst_b[:, CONSTS["half"][0] + hh:CONSTS["half"][0] + hh + 1]
                        for c in range(NC4):
                            col = (pr * 2 + hh) * 4 + c
                            o = c * P
                            pe.matmul(ps[:, 6, col:col + 1], q_sq[:, hh * T + o:hh * T + o + P], ones[:, 0:1],
                                      start=True, stop=False, skip_group_check=True)
                            m = pe.matmul(ps[:, 6, col:col + 1], q_sq[:, 2 * T + o:2 * T + o + P], own,
                                          start=False, stop=True, skip_group_check=True)
                    m.then_inc(sem["qb_sums"], 1)
                    pe.wait_ge(sem["qb_copy"], 3 * pr + 3)
                    if pr >= 1:
                        pe.wait_ge(sem["qb_rope"], pr)
                    pe.matmul(ps[:, 5, :], cst_b[:, 0:P], tile(q_rp, pr % 2), start=True, stop=True)\
                        .then_inc(sem["qb_rot"], 1)
            for h in range(MLA_HEADS):
                n = A["k_b"] + 2 * h
                for half, (lo_, hi_) in enumerate(((0, T), (T, TK))):
                    dst = a_bank(n + half)[:, 0:hi_ - lo_]
                    parts = [((2 * h + k) % 8, ck_hi[:, k * TK + lo_:k * TK + hi_],
                              ck_lo[:, k * TK + lo_:k * TK + hi_]) for k in range(2)]
                    if h == 0 and half == 0:
                        pe.wait_ge(sem["n_done"], NT["ck"] + 2)
                    group(dst, FIRST["k_b"] + h // 4, parts, new_unit=(h % 4 == 0 and half == 0))\
                        .then_inc(sem["a_full"], 1)
                pe.wait_ge(sem["a_free"], A["k_b"] + 2 * h + 2)
                if h >= 1:
                    pe.wait_ge(sem["kb_r"], h)
                else:
                    pe.wait_ge(sem["kpe_squared"], 1)
                    pe.wait_ge(sem["kpe_done"], 1)
                for bank, lo_, hi_ in ((4, 0, T), (7, T, TK)):
                    pe.matmul(ps[:, bank, 0:hi_ - lo_], ones[:, :], k_sq[:, lo_:hi_], start=True, stop=False)
                    m = pe.matmul(ps[:, bank, 0:hi_ - lo_], ones[0:64, :], kpe_sq[0:64, lo_:hi_], start=False,
                                  stop=True)
                m.then_inc(sem["kb_sum"], 1)
            for cb in range(2):
                u = FIRST["v_b"] + cb
                s0 = (u % W_SLOTS) * UNIT
                for c in range(6):
                    if c == 0:
                        start_unit(u)
                    n = A["v_b"] + cb * 6 + c
                    dst = a_bank(n)
                    for k in range(2):
                        kh = ck_hi[:, k * TK + c * P:k * TK + (c + 1) * P]
                        kl = ck_lo[:, k * TK + c * P:k * TK + (c + 1) * P]
                        wh = w_hi[:, s0 + k * T:s0 + (k + 1) * T]
                        wl = w_lo[:, s0 + k * T:s0 + (k + 1) * T]
                        m = pe.matmul(dst, kl, wh, start=k == 0, stop=False)
                        if c == 0 and k == 0:
                            m.then_inc(sem["unit_started"], 1)
                        pe.matmul(dst, kh, wh, start=False, stop=False)
                        m = pe.matmul(dst, kh, wl, start=False, stop=k == 1)
                    m.then_inc(sem["a_full"], 1)

            def at_scores(s):
                h, c = divmod(s, 4)
                b = (s % 2) * 2
                if s >= 2:
                    pe.wait_ge(sem["s_exp"], s - 1)
                if s == 0:
                    pe.wait_ge(sem["a_free"], A["ff1"])
                    pe.wait_ge(sem["kb_norm"], MLA_HEADS)
                    pe.wait_ge(sem["qb_rope"], 4)
                hp = head_half(h)
                pair = h // 2
                krt, kro = (kr_a, pair * TK) if pair < 2 else (kr_b, (pair - 2) * TK)
                for half, (lo_, hi_) in enumerate(((0, T), (T, TK))):
                    dst = ps[:, b + half, 0:hi_ - lo_]
                    pe.matmul(dst, qn[:, h * T + c * P:h * T + (c + 1) * P],
                              kn[:, h * TK + lo_:h * TK + hi_], start=True, stop=False)
                    m = pe.matmul(dst, qr[hp, pair * T + c * P:pair * T + (c + 1) * P],
                                  krt[hp, kro + lo_:kro + hi_], start=False, stop=True)
                m.then_inc(sem["s_full"], 1)

            def at_turn(s):
                pe.wait_ge(sem["p_norm"], s + 1)
                for half in range(2):
                    if s >= 1:
                        pe.wait_ge(sem["t_copied"], 2 * (s - 1) + half + 1)
                    elif half == 0:
                        pe.wait_ge(sem["kb_r"], MLA_HEADS)
                    for k in range(3):
                        o = (s % 2) * TK + (half * 3 + k) * P
                        m = pe.transpose(ps[:, 4 + half, k * P:(k + 1) * P], at_p[:, o:o + P], ident[:, :])
                    m.then_inc(sem["t_full"], 1)

            def at_values(h):
                pe.wait_ge(sem["t_copied"], 8 * (h + 1))
                if h >= 2:
                    pe.wait_ge(sem["o_low"], h - 1)
                for k in range(6):
                    m = pe.matmul(ps[:, 6 + h % 2, :], ml_v[:, k * 1024 + h * P:k * 1024 + (h + 1) * P],
                                  tile(at_pt, k), start=k == 0, stop=k == 5)
                m.then_inc(sem["o_full"], 1)

            at_scores(0)
            for s in range(4 * MLA_HEADS):
                if s + 1 < 4 * MLA_HEADS:
                    at_scores(s + 1)
                if s % 4 == 0 and s > 0:
                    at_values(s // 4 - 1)
                at_turn(s)
            at_values(MLA_HEADS - 1)

            def attended(i):
                pe.wait_ge(sem["o_low"], i + 1)
            pe.wait_ge(sem["t_copied"], 8 * MLA_HEADS)
            for j in range(KT):
                group(d_bank(D["mla_o"] + j), FIRST["mla_o"] + j, x_parts(o_hi, o_lo),
                      each=attended if j == 0 else None).then_inc(sem["d_full"], 1)
            pe.wait_ge(sem["o_low"], MLA_HEADS)
            stat("ffn0")
            feed_forward("ff1", "ffn0", 1, False)

            stat("mix1")
            pe.wait_ge(sem["gm_loaded"], 32)
            for i in range(2):
                pe.wait_ge(sem["n_scale"], NI["mix1"] + 1)
                pe.matmul(ps[:, 6 + i, :], ones[:, :], wst[:, i * T:(i + 1) * T], start=True, stop=True)\
                    .then_inc(sem["gm_rows"], 1)
            for i in range(2):
                pe.wait_ge(sem["gm_copy"], i + 1)
                pe.matmul(ps[:, 6 + i, :], ones[0:1, :], bs_row[0:1, i * T:(i + 1) * T], start=True, stop=True)\
                    .then_inc(sem["gm_rows"], 1)
            for k in range(KT):
                pe.wait_ge(sem["n_done"], NT["mix1"] + k + 1)
            token_major(FIRST["gm_v"], A["gm_v"], 4)
            for half in range(2):
                for j in range(8):
                    f = half * 8 + j
                    group(a_bank(A["gm_u"] + f), FIRST["gm_u"] + half * 16 + j, x_parts()).then_inc(sem["a_full"], 1)
                    dst = d_bank(D["gm_u"] + half * 16 + j)
                    if f == 0:
                        pe.wait_ge(sem["gv_norm"], 4)
                    for c in range(NC4):
                        m = pe.matmul(dst[:, c * P:(c + 1) * P],
                                      gv[:, c * 2048 + f * P:c * 2048 + (f + 1) * P],
                                      wst[:, (f // 2) * P:(f // 2 + 1) * P], start=True, stop=True)
                    m.then_inc(sem["d_full"], 1)

                def mixed(i, half=half):
                    pe.wait_ge(sem["gu_low"], half * 8 + i + 1)
                for j in range(8):
                    group(d_bank(D["gm_u"] + half * 16 + 8 + j), FIRST["gm_u"] + half * 16 + 8 + j,
                          x_parts(h_hi, h_lo), each=mixed if j == 0 else None).then_inc(sem["d_full"], 1)
            pe.wait_ge(sem["gm_copy"], 4)
            stat("ffn1")
            feed_forward("ff2", "ffn1", 2, False)

        NH = firsts([(n, 0 if n == "final" else k) for n, k in NORMS])
        NK = dict(NORMS)

        def norm_spec(name):
            main = lambda j: tile(hres, j)
            xs = (lambda j: tile(x_hi, j), lambda j: tile(x_lo, j))
            gain = lambda n: (lambda j: dcol(D_GAIN + 8 * n + j))
            return {
                "norm1": (main, T, 1024, lambda j: v("norm1", j), None, xs),
                "norm2": (main, T, 1024, lambda j: v("norm2", j), None, xs),
                "final": (main, T, 1024, lambda j: v("final", j), None, None),
                "mix0": (main, T, 1024, gain(0), lambda j: mcol(mod_col(0, 0, j)), xs),
                "ctx": (lambda j: tile(ctxx, j, TC), TC, 1024, gain(1), lambda j: mcol(ctx_col(0, j)),
                        (lambda j: tile(c_hi, j, TC), lambda j: tile(c_lo, j, TC))),
                "cq": (lambda j: tile(cq_raw, j), T, 384, lambda j: v("q_a_norm", j), None,
                       (lambda j: tile(cq_hi, j), lambda j: tile(cq_lo, j))),
                "ck": (lambda j: tile(ck_raw, j, TK), TK, 256, lambda j: v("kv_a_norm", j), None,
                       (lambda j: tile(ck_hi, j, TK), lambda j: tile(ck_lo, j, TK))),
                "ffn0": (main, T, 1024, gain(2), lambda j: mcol(mod_col(0, 3, j)), xs),
                "mix1": (main, T, 1024, gain(3), lambda j: mcol(mod_col(1, 0, j)), xs),
                "ffn1": (main, T, 1024, gain(4), lambda j: mcol(mod_col(1, 3, j)), xs),
            }[name]

        def norm_t(name, j):
            return tile(n_sq, j % 2, TK) if name == "ck" else n_t[:, (j % 2) * T:(j % 2) * T + norm_spec(name)[1]]

        seg = [0, 512, 896, 1152]
        AX_X = mybir.AxisListType.X

        def ps_pair(b):
            return ps[:, b:b + 2, :].rearrange("p b t -> p (b t)")

        def zt(h, i):
            b = (h % 2) * 3
            return ps[:, b + 1, 0:P] if i == 3 else ps[:, b + i, i * P:T]

        def half_of(h):
            return slice(64 * (h % 2), 64 * (h % 2) + 64)

        @block.scalar
        def _(act):
            def ordered(s, value):
                act.wait_ge(sem[s], value)

            def copy(out_, in_):
                return act.activation(out_, in_, ACT.Copy)

            def exp_tables():
                act.preload_act_table_set("natural_log_exp_and_others")

            def norm(name, ready):
                src, w_, feats, _, shift, dst = norm_spec(name)
                i, k = NI[name], NK[name]
                for j in range(k):
                    ready(j)
                    if j == 0:
                        if i:
                            act.wait_ge(sem["n_total"], i)
                        buf = n_acc[:, 0:w_]
                    else:
                        if j >= 3:
                            act.wait_ge(sem["n_added"], NSQ[name] + j - 2)
                        buf = n_sq[:, ((j - 1) % 2) * TK:((j - 1) % 2) * TK + w_]
                    act.activation(buf, src(j), ACT.Square).then_inc(sem["n_squared"], 1)
                act.wait_ge(sem["n_total"], i + 1)
                if i:
                    act.wait_ge(sem["n_done"], NT[name])
                pieces = [(6, 0, min(w_, T))] + ([(7, T, w_)] if w_ > T else [])
                for bank, lo_, hi_ in pieces:
                    m = act.activation(n_r[:, lo_:hi_], ps[:, bank, 0:hi_ - lo_], ACT.Ln, bias=EPS,
                                       scale=1.0 / feats)
                m.then_inc(sem["n_log"], 1)
                ordered("n_log", i + 1)
                act.activation(n_r[:, 0:w_], n_r[:, 0:w_], ACT.Exp, scale=-0.5).then_inc(sem["n_scale"], 1)
                if dst is None:
                    return
                for j in range(k):
                    act.wait_ge(sem["n_scaled"], NH[name] + j + 1)
                    t = norm_t(name, j)
                    if shift is None:
                        m = copy(dst[0](j), t)
                    else:
                        m = act.activation(dst[0](j), t, ACT.Identity, bias=shift(j))
                    m.then_inc(sem["n_high"], 1)

            def a_tile(n):
                act.wait_ge(sem["a_full"], n + 1)
                return ps[:, n % 4, :]

            def d_tile(n):
                act.wait_ge(sem["d_full"], n + 1)
                return ps[:, 4 + n % 2, :]

            def copy_out(n, dst, scale=None):
                t = a_tile(n)
                if scale is None:
                    m = copy(dst, t)
                else:
                    m = act.activation(dst, t, ACT.Copy, scale=scale)
                m.then_inc(sem["a_free"], 1)

            exp_tables()
            norm("norm1", lambda j: (act.wait_ge(sem["x_loaded"], 16), act.wait_ge(sem["small_loaded"], 48)))
            for j in range(4):
                copy_out(A["sb_qk"] + j, tile(sb_q, j), scale=0.125)
            for j in range(4):
                copy_out(A["sb_qk"] + 4 + j, tile(sb_k, j))
            for c in range(NC4):
                copy_out(A["sb_v"] + c, tile(sb_v, c))

            def softplus(h):
                act.wait_ge(sem["sp_scores"], h + 1)
                if h:
                    ordered("sp_log", h)
                for i in range(4):
                    m = act.activation(sb_e[:, seg[i]:seg[i] + T - i * P], zt(h, i), ACT.Abs)
                m.then_inc(sem["act_order"], 1)
                ordered("act_order", 2 * h + 1)
                act.activation(sb_e[:, :], sb_e[:, :], ACT.Exp, scale=-1.0).then_inc(sem["act_order"], 1)
                ordered("act_order", 2 * h + 2)
                if h:
                    act.wait_ge(sem["sp_soft"], 4 * h)
                act.activation(sb_l[:, :], sb_e[:, :], ACT.Ln, bias=1.0).then_inc(sem["sp_log"], 1)

            def weights_of(h):
                act.wait_ge(sem["sp_decay"], h + 1)
                if h:
                    act.wait_ge(sem["sp_out"], h)
                for i in range(4):
                    act.activation(sb_w[:, seg[i]:seg[i] + T - i * P], zt(h, i), ACT.Exp)\
                        .then_inc(sem["sp_weights"], 1)

            def sb_high(h):
                act.wait_ge(sem["sp_out"], h + 1)
                copy(h_hi[half_of(h), (h // 2) * T:(h // 2 + 1) * T], ps[half_of(h), 6 + h % 2, :])\
                    .then_inc(sem["sp_high"], 1)

            softplus(0)
            for h in range(SB_HEADS):
                if h + 1 < SB_HEADS:
                    softplus(h + 1)
                weights_of(h)
                if h:
                    sb_high(h - 1)
            sb_high(SB_HEADS - 1)

            act.wait_ge(sem["lb_diff"], 1)
            act.activation(dcol(D_OLB, 4), dcol(D_LB, 4), ACT.Sigmoid, scale=-1.0).then_inc(sem["act_order"], 1)
            ordered("act_order", 2 * SB_HEADS + 1)
            act.activation(dcol(D_LB, 4), dcol(D_LB, 4), ACT.Sigmoid).then_inc(sem["lb_ready"], 1)
            act.activation(dcol(D_C, 16), vecs[:, VECS["c"][0]:VECS["c"][0] + 16], ACT.Sigmoid)\
                .then_inc(sem["silu_c"], 1)
            for j in range(4):
                t = a_tile(A["hg_f"] + j)
                act.activation(tile(hg_b, j), t, ACT.Sigmoid).then_inc(sem["hf_sig"], 1)
                act.activation(tile(hg_k, j), t, ACT.Sigmoid, scale=-1.0).then_inc(sem["a_free"], 1)
            for c in range(NC4):
                copy_out(A["hg_i"] + c, tile(hg_v, c))
            for j in range(4):
                act.activation(tile(hg_a, j), d_tile(D["hg_q"] + j), ACT.Sigmoid).then_inc(sem["hf_qs"], 1)
            exp_tables()
            act.wait_ge(sem["hf_f"], 4)
            for j in range(4):
                act.wait_ge(sem["d_free"], D["hg_q"] + j + 1)
                act.activation(tile(hg_a, j), tile(hg_b, j), ACT.Ln).then_inc(sem["hf_log"], 1)
            for lv, m_ in enumerate(HGRN_LEVELS):
                for pr in range(2):
                    act.wait_ge(sem["lv_diff"], 2 * lv + pr + 1)
                    vw = hg_a[:, pr * 2 * T:(pr + 1) * 2 * T].rearrange("p (g s m) -> p g s m", s=2, m=m_)
                    act.activation(vw[:, :, 0, :], vw[:, :, 0, :], ACT.Exp, scale=-1.0)
                    act.activation(vw[:, :, 1, :], vw[:, :, 1, :], ACT.Exp).then_inc(sem["lv_exp"], 1)
            for h in range(HG_HEADS):
                act.wait_ge(sem["off_diff"], h + 1)
                act.activation(tile(hg_a, h), tile(hg_a, h), ACT.Exp)
                if h >= 2:
                    act.wait_ge(sem["ho_ready"], h - 1)
                act.activation(tile(hg_s, h % 2), tile(hg_b, h), ACT.Exp).then_inc(sem["off_exp"], 1)
            for h in range(HG_HEADS):
                act.wait_ge(sem["off_score"], h + 1)
                b = (h % 2) * 2
                copy(hg_off[:, h * 768:h * 768 + T], ps[:, b, :])
                copy(hg_off[:, h * 768 + T:(h + 1) * 768], ps[:, b + 1, 0:2 * P]).then_inc(sem["off_kept"], 1)
            for h in range(HG_HEADS):
                act.wait_ge(sem["ho_out"], h + 1)
                act.activation(tile(hg_b, h), ps[:, 4 + h, :], ACT.Square).then_inc(sem["ho_sq"], 1)
            act.dma_start(hres[:, :], x_t).then_inc(sem["x_loaded"], 16)
            for h in range(HG_HEADS):
                act.wait_ge(sem["ho_total"], h + 1)
                act.activation(tile(hg_a, h), ps[:, h, :], ACT.Ln, bias=EPS, scale=1.0 / P)\
                    .then_inc(sem["ho_log"], 1)
                ordered("ho_log", h + 1)
                act.activation(tile(hg_a, h), tile(hg_a, h), ACT.Exp, scale=-0.5).then_inc(sem["ho_scale"], 1)
            for j in range(4):
                if j >= 2:
                    act.wait_ge(sem["d_free"], D["hg_g"] + j - 1)
                act.activation(tile(hg_s, j % 2), d_tile(D["hg_g"] + j), ACT.Sigmoid).then_inc(sem["hg_sig"], 1)
                act.wait_ge(sem["hg_gate"], j + 1)
                copy(tile(h_hi, 4 + j), tile(hg_k, j)).then_inc(sem["ho_high"], 1)

            for j in range(KT):
                for g, name in enumerate(("gate_a", "gate_b")):
                    n = A["merge"] + 2 * j + g
                    t = a_tile(n)
                    if j == 0:
                        act.wait_ge(sem["ho_low"], HG_HEADS)
                    if j >= 2:
                        act.wait_ge(sem["d_free"], D["merge"] + 2 * (j - 2) + g + 1)
                    act.activation(tile(m_t, (j % 2) * 2 + g), t, ACT.Sigmoid, bias=v(name, j))\
                        .then_inc(sem["a_free"], 1)
                act.wait_ge(sem["mg_sum"], j + 1)
                copy(tile(m_hi, j), tile(m_t, 4)).then_inc(sem["mg_high"], 1)
            exp_tables()

            def load_ada(chunk, slot):
                act.dma_start(tile(ada_w, slot, 4096), ada[bass.ds(chunk, 1), :, :].rearrange("a p n -> (a p) n"))\
                    .then_inc(sem["ada_in%d" % slot], 16)

            def feed_forward(name, n_ff, with_ada):
                a0_, d0_ = A[name], D[name]
                with act.Fori(0, 4) as it:
                    for j in range(8):
                        if with_ada:
                            r = 0 if j == 0 else (j + 1) // 2 if j % 2 else None
                            if r is not None:
                                act.wait_ge(sem["ada_used"], it * 7 + max(r - 2, -1) + 2)
                                load_ada(it * 7 + r, r % 2)
                        n = it * 8 + j
                        act.wait_ge(sem["a_full"], n + a0_ + 1)
                        act.wait_ge(sem["f_square"], n + n_ff * 32 + 1)
                        act.activation(tile(f_r, j % 2), ps[:, (a0_ + j) % 4, :], ACT.Relu)\
                            .then_inc(sem["a_free"], 1)
                        act.wait_ge(sem["a_free"], n + a0_ + 1)
                        act.wait_ge(sem["d_full"], it * 8 + d0_)
                        act.activation(tile(h_hi, j), tile(f_r, j % 2), ACT.Square).then_inc(sem["f_high"], 1)
                    if with_ada:
                        for r in (5, 6):
                            act.wait_ge(sem["ada_used"], it * 7 + r)
                            load_ada(it * 7 + r, r % 2)

            norm("norm2", lambda j: act.wait_ge(sem["d_free"], D["w_out"] + j + 1))
            feed_forward("ff0", 0, True)
            act.wait_ge(sem["ada_used"], ADA_CHUNKS + 1)
            act.dma_start(cst_b[:, :], const_b).then_inc(sem["cstb_loaded"], 16)
            act.wait_ge(sem["ada_cols"], 4)
            act.dma_start(ctxx[:, :], ctx_t).then_inc(sem["ctx_loaded"], 16)
            norm("final", lambda j: act.wait_ge(sem["d_free"], D["mla_o"]))
            norm("mix0", lambda j: act.wait_ge(sem["n_done"], NT["final"] + j + 1))
            norm("ctx", lambda j: act.wait_ge(sem["ctx_loaded"], 16))
            for j in range(3):
                copy_out(A["q_a"] + j, tile(cq_raw, j))
            for j in range(3):
                n = A["kv_a"] + 2 * j
                dst = kpe_raw if j == 2 else ck_raw[:, j * TK:(j + 1) * TK]
                copy(dst[:, TC:TK], a_tile(n)).then_inc(sem["a_free"], 1)
                copy(dst[:, 0:TC], a_tile(n + 1)[:, 0:TC]).then_inc(sem["a_free"], 1)
            ordered("a_free", A["q_b"])
            act.activation(kpe[:, :], kpe_raw[:, :], ACT.Copy, scale=v("k_rope")).then_inc(sem["kpe_scaled"], 1)
            act.activation(kpe_sq[:, :], kpe_raw[:, :], ACT.Square).then_inc(sem["kpe_squared"], 1)
            norm("cq", lambda j: None)
            norm("ck", lambda j: None)
            for b in range(12):
                pr, w_in = b // 3, b % 3
                t = a_tile(A["q_b"] + b)
                if w_in < 2:
                    dst, g = tile(qn, 2 * pr + w_in), "q_nope"
                else:
                    dst, g = tile(q_rp, pr % 2), "q_rope"
                    if pr >= 2:
                        act.wait_ge(sem["qb_rope"], pr - 1)
                act.activation(dst, t, ACT.Copy, scale=v(g)).then_inc(sem["qb_copy"], 1)
                if pr:
                    act.wait_ge(sem["qb_sums"], pr)
                act.activation(tile(q_sq, w_in), t, ACT.Square).then_inc(sem["a_free"], 1)
            for h in range(MLA_HEADS):
                if h == 0:
                    act.wait_ge(sem["qb_rope"], 4)
                else:
                    act.wait_ge(sem["kb_sum"], h)
                for half, (lo_, hi_) in enumerate(((0, T), (T, TK))):
                    t = a_tile(A["k_b"] + 2 * h + half)[:, 0:hi_ - lo_]
                    act.activation(kn[:, h * TK + lo_:h * TK + hi_], t, ACT.Copy, scale=v("k_nope"))\
                        .then_inc(sem["kb_copy"], 1)
                    act.activation(k_sq[:, lo_:hi_], t, ACT.Square).then_inc(sem["a_free"], 1)
                act.wait_ge(sem["kb_sum"], h + 1)
                if h:
                    act.wait_ge(sem["kb_norm"], h)
                act.activation(k_r[:, 0:T], ps[:, 4, :], ACT.Ln, bias=EPS, scale=1.0 / 192)
                act.activation(k_r[:, T:TK], ps[:, 7, 0:TC], ACT.Ln, bias=EPS, scale=1.0 / 192)\
                    .then_inc(sem["act_order"], 1)
                ordered("act_order", 2 * SB_HEADS + 1 + h + 1)
                act.activation(k_r[:, :], k_r[:, :], ACT.Exp, scale=-0.5).then_inc(sem["kb_r"], 1)
            act.wait_ge(sem["qb_sums"], 4)
            act.activation(dcol(D_RQ, 32), ps[:, 6, 0:32], ACT.Ln, bias=EPS, scale=1.0 / 192)\
                .then_inc(sem["rq_log"], 1)
            ordered("rq_log", 1)
            act.activation(dcol(D_RQ, 32), dcol(D_RQ, 32), ACT.Exp, scale=-0.5).then_inc(sem["rq_exp"], 1)
            act.wait_ge(sem["kb_norm"], MLA_HEADS)
            for cb in range(2):
                for c in range(6):
                    copy_out(A["v_b"] + cb * 6 + c, ml_v[:, c * 1024 + cb * T:c * 1024 + (cb + 1) * T])

            def at_exp(s):
                h, c = divmod(s, 4)
                act.wait_ge(sem["s_max"], s + 1)
                if s >= 2:
                    act.wait_ge(sem["t_full"], 2 * (s - 1))
                b = (s % 2) * 2
                act.activation(tile(at_p, s % 2, TK), ps_pair(b)[:, 0:TK], ACT.Exp,
                               bias=dcol(D_AT + 4 * (s % 2) + 1), scale=dcol(D_RQ + s),
                               accum_out=dcol(D_AT + 4 * (s % 2) + 2)).then_inc(sem["s_exp"], 1)

            def at_copy(s):
                h, c = divmod(s, 4)
                if s % 4 == 0 and h:
                    act.wait_ge(sem["o_full"], h)
                for half in range(2):
                    act.wait_ge(sem["t_full"], 2 * s + half + 1)
                    dst = at_pt[:, half * 3 * T:(half + 1) * 3 * T].rearrange("p (k t) -> p k t", k=3)
                    src = ps[:, 4 + half, 0:3 * P].rearrange("p (k t) -> p k t", k=3)
                    copy(dst[:, :, c * P:(c + 1) * P], src).then_inc(sem["t_copied"], 1)

            def o_high_of(h):
                act.wait_ge(sem["o_full"], h + 1)
                copy(tile(o_hi, h), ps[:, 6 + h % 2, :]).then_inc(sem["o_high"], 1)

            at_exp(0)
            for s in range(4 * MLA_HEADS):
                if s + 1 < 4 * MLA_HEADS:
                    at_exp(s + 1)
                at_copy(s)
                if s % 4 == 1 and s > 4:
                    o_high_of(s // 4 - 1)
            o_high_of(MLA_HEADS - 1)
            norm("ffn0", lambda j: act.wait_ge(sem["d_free"], D["mla_o"] + j + 1))
            feed_forward("ff1", 1, False)
            act.wait_ge(sem["d_free"], D["gm_u"])
            act.dma_start(wst[:, :], ws_t).then_inc(sem["gm_loaded"], 16)
            act.dma_start(bs_row[0:1, :], bs_in).then_inc(sem["gm_loaded"], 16)
            norm("mix1", lambda j: None)
            act.preload_act_table(ACT.Gelu)
            for cb in range(4):
                for c in range(NC4):
                    n = A["gm_v"] + cb * 4 + c
                    act.activation(gv[:, c * 2048 + cb * T:c * 2048 + (cb + 1) * T], a_tile(n), ACT.Gelu)\
                        .then_inc(sem["a_free"], 1)
            act.wait_ge(sem["gv_var"], 4)
            exp_tables()
            var = g_st[:, 56:64].rearrange("p (c s) -> p c s", s=2)[:, :, 1]
            act.activation(var, var, ACT.Ln, bias=EPS).then_inc(sem["gv_log"], 1)
            ordered("gv_log", 1)
            act.activation(var, var, ACT.Exp, scale=-0.5).then_inc(sem["gv_rstd"], 1)
            for half in range(2):
                for j in range(8):
                    f = half * 8 + j
                    t = a_tile(A["gm_u"] + f)
                    if f == 0:
                        act.wait_ge(sem["gm_extra"], 16)
                    else:
                        act.wait_ge(sem["gu_mul"], f)
                    act.activation(g_u[:, :], t, ACT.Gelu).then_inc(sem["a_free"], 1)
                    act.wait_ge(sem["gu_mul"], f + 1)
                    act.wait_ge(sem["d_full"], D["gm_u"] + half * 16)
                    copy(tile(h_hi, j), g_s[:, :]).then_inc(sem["gu_high"], 1)
            exp_tables()
            norm("ffn1", lambda j: act.wait_ge(sem["d_free"], D["ff2"]))
            feed_forward("ff2", 2, False)
            for j in range(KT):
                act.wait_ge(sem["d_free"], D["end"] - 8 + j + 1)
                act.dma_start(out[:, j * T:(j + 1) * T], tile(hres, j)).then_inc(sem["stored"], 16)
            act.wait_ge(sem["stored"], 16 * KT)

        @block.vector
        def _(dve):
            class Order:
                n = 0

            def ordered(ins):
                Order.n += 1
                ins.then_inc(sem["dve_order"], 1)
                dve.wait_ge(sem["dve_order"], Order.n)

            def norm(name):
                src, w_, _, gain, shift, dst = norm_spec(name)
                i, k = NI[name], NK[name]
                for j in range(1, k):
                    dve.wait_ge(sem["n_squared"], NT[name] + j + 1)
                    if j > 1:
                        dve.wait_ge(sem["n_added"], NSQ[name] + j - 1)
                    sq = n_sq[:, ((j - 1) % 2) * TK:((j - 1) % 2) * TK + w_]
                    dve.tensor_tensor(n_acc[:, 0:w_], n_acc[:, 0:w_], sq, ALU.add).then_inc(sem["n_added"], 1)
                dve.wait_ge(sem["n_scale"], i + 1)
                if dst is None:
                    for j in range(k):
                        dve.scalar_tensor_tensor(src(j), src(j), gain(j), n_r[:, 0:w_], ALU.mult, ALU.mult)\
                            .then_inc(sem["n_done"], 1)
                    return

                def scaled(j):
                    if j >= 2:
                        dve.wait_ge(sem["n_high"], NH[name] + j - 1)
                        dve.wait_ge(sem["n_done"], NT[name] + j - 1)
                    dve.scalar_tensor_tensor(norm_t(name, j), src(j), gain(j), n_r[:, 0:w_], ALU.mult, ALU.mult)\
                        .then_inc(sem["n_scaled"], 1)

                scaled(0)
                for j in range(k):
                    if j + 1 < k:
                        scaled(j + 1)
                    dve.wait_ge(sem["n_high"], NH[name] + j + 1)
                    high = dst[0](j).bitcast(F32)
                    if shift is None:
                        m = dve.tensor_tensor(dst[1](j), norm_t(name, j), high, ALU.subtract)
                    else:
                        m = dve.scalar_tensor_tensor(dst[1](j), norm_t(name, j), shift(j), high, ALU.add,
                                                     ALU.subtract)
                    m.then_inc(sem["n_done"], 1)

            def d_tile(n):
                dve.wait_ge(sem["d_full"], n + 1)
                return ps[:, 4 + n % 2, :]

            dve.memset(ones[:, :], 1.0).then_inc(sem["ones_set"], 1)
            dve.memset(neg_ones[:, :], -1.0).then_inc(sem["ones_set"], 1)
            dve.sem_inc(sem["f_square"], 2)
            dve.sem_inc(sem["ada_used"], 1)
            dve.sem_inc(sem["bank7_free"], 1)
            norm("norm1")

            def soft(h):
                dve.wait_ge(sem["sp_log"], h + 1)
                if h >= 2:
                    dve.wait_ge(sem["sp_decay"], h - 1)
                o = (h % 2) * 1280
                for i in range(4):
                    m = dve.scalar_tensor_tensor(sb_sp[:, o + seg[i]:o + seg[i] + T - i * P], zt(h, i), 0.0,
                                                 sb_l[:, seg[i]:seg[i] + T - i * P], ALU.max, ALU.add)
                ordered(m)
                for i in range(4):
                    d = sb_sp[:, o + seg[i]:o + seg[i] + P]
                    dve.tensor_tensor(d, d, cst_a[:, CONSTS["strict"][0]:CONSTS["strict"][0] + P], ALU.mult)\
                        .then_inc(sem["sp_soft"], 1)

            def sb_low(h):
                dve.wait_ge(sem["sp_high"], h + 1)
                c0 = (h // 2) * T
                dve.tensor_tensor(h_lo[half_of(h), c0:c0 + T], ps[half_of(h), 6 + h % 2, :],
                                  h_hi[half_of(h), c0:c0 + T].bitcast(F32), ALU.subtract)\
                    .then_inc(sem["sp_low"], 1)

            soft(0)
            for h in range(SB_HEADS):
                if h + 1 < SB_HEADS:
                    soft(h + 1)
                if h:
                    sb_low(h - 1)
            sb_low(SB_HEADS - 1)

            dve.tensor_tensor(dcol(D_LB, 4), v("lb0", 0, 4), v("lb1", 0, 4), ALU.subtract).then_inc(sem["lb_diff"], 1)
            dve.memset(hg_p[:, :], 0.0).then_inc(sem["hp_zero"], 1)
            dve.wait_ge(sem["lb_ready"], 1)
            dve.wait_ge(sem["silu_c"], 1)
            dve.tensor_tensor(dcol(D_C, 16), dcol(D_C, 16), vecs[:, VECS["c"][0]:VECS["c"][0] + 16], ALU.mult)\
                .then_inc(sem["silu_done"], 1)
            for j in range(4):
                dve.wait_ge(sem["hf_sig"], j + 1)
                dve.tensor_scalar(tile(hg_b, j), tile(hg_b, j), dcol(D_OLB + j), dcol(D_LB + j), ALU.mult,
                                  ALU.add).then_inc(sem["hf_f"], 1)
                dve.wait_ge(sem["a_free"], A["hg_f"] + j + 1)
                dve.tensor_scalar(tile(hg_k, j), tile(hg_k, j), dcol(D_OLB + j), None, ALU.mult)\
                    .then_inc(sem["hf_k"], 1)
            for j in range(4):
                dve.wait_ge(sem["hf_qs"], j + 1)
                dve.tensor_tensor(tile(hg_q, j), d_tile(D["hg_q"] + j), tile(hg_a, j), ALU.mult)\
                    .then_inc(sem["d_free"], 1)
            restart = cst_a[:, CONSTS["restart"][0]:CONSTS["restart"][0] + T]
            for j in range(4):
                dve.wait_ge(sem["hf_log"], j + 1)
                dve.tensor_tensor_scan(tile(hg_b, j), restart, tile(hg_a, j), 0.0, ALU.mult, ALU.add)\
                    .then_inc(sem["hf_b"], 1)

            def keep(lv):
                o = CONSTS["levels"][0] + lv * P
                mask = cst_a[:, o:o + P].bitcast(I32).unsqueeze(1).broadcast_to([P, NC4, P])
                for h in range(HG_HEADS):
                    bank = (lv % 2) * 4 + h
                    dve.wait_ge(sem["lv_score"], lv * 4 + h + 1)
                    if lv:
                        dve.wait_ge(sem["lv_kept"], (lv - 1) * 4 + h + 1)
                    else:
                        dve.wait_ge(sem["hp_zero"], 1)
                    dve.copy_predicated(tile(hg_p, h).rearrange("p (c t) -> p c t", c=NC4), mask,
                                        ps[:, bank, :].rearrange("p (c t) -> p c t", c=NC4))\
                        .then_inc(sem["lv_kept"], 1)

            dve.wait_ge(sem["hf_b"], 4)
            for lv, m_ in enumerate(HGRN_LEVELS):
                view = lambda t, pr: t[:, pr * 2 * T:(pr + 1) * 2 * T].rearrange("p (g s m) -> p g s m", s=2, m=m_)
                for pr in range(2):
                    if lv:
                        dve.wait_ge(sem["lv_score"], lv * 4 + 2 * pr + 2)
                    b = view(hg_b, pr)
                    ref = b[:, :, 0:1, m_ - 1:m_].broadcast_to([P, T // m_, 2, m_])
                    dve.tensor_tensor(view(hg_a, pr), b, ref, ALU.subtract).then_inc(sem["lv_diff"], 1)
                keep(lv)
                for pr in range(2):
                    dve.wait_ge(sem["lv_exp"], 2 * lv + pr + 1)
                    a = view(hg_a, pr)
                    dve.tensor_tensor(a[:, :, 0, :], a[:, :, 0, :], view(hg_k, pr)[:, :, 0, :], ALU.mult)
                    dve.tensor_tensor(a[:, :, 1, :], a[:, :, 1, :], view(hg_q, pr)[:, :, 1, :], ALU.mult)\
                        .then_inc(sem["lv_pair"], 1)
            dve.wait_ge(sem["lv_score"], 4 * 8)
            for h in range(HG_HEADS):
                b = tile(hg_b, h).rearrange("p (c t) -> p c t", c=NC4)
                dve.tensor_tensor(tile(hg_a, h).rearrange("p (c t) -> p c t", c=NC4),
                                  b[:, :, P - 1:P].broadcast_to([P, NC4, P]), b, ALU.subtract)\
                    .then_inc(sem["off_diff"], 1)
            for h in range(HG_HEADS):
                dve.wait_ge(sem["off_exp"], h + 1)
                k, q, ep = tile(hg_k, h), tile(hg_q, h), tile(hg_s, h % 2)
                dve.tensor_tensor(k, k, tile(hg_a, h), ALU.mult)
                ordered(dve.tensor_tensor(q, q, ep, ALU.mult))
                dve.tensor_scalar(hg_edge[:, h * P:(h + 1) * P], k[:, 0:P], ep[:, 2 * P - 1:2 * P], None, ALU.mult)
                dve.tensor_scalar(hg_edge[:, (4 + h) * P:(5 + h) * P], q[:, 3 * P:T], ep[:, 3 * P - 1:3 * P],
                                  None, ALU.mult).then_inc(sem["ho_ready"], 1)
            keep(len(HGRN_LEVELS))
            for h in range(HG_HEADS):
                dve.wait_ge(sem["ho_scale"], h + 1)
                dve.scalar_tensor_tensor(tile(hg_p, h), ps[:, 4 + h, :], v("hg_norm", h), tile(hg_a, h),
                                         ALU.mult, ALU.mult).then_inc(sem["ho_norm"], 1)
            for j in range(4):
                dve.wait_ge(sem["hg_sig"], j + 1)
                dve.tensor_tensor(tile(hg_q, j), d_tile(D["hg_g"] + j), tile(hg_s, j % 2), ALU.mult)\
                    .then_inc(sem["d_free"], 1)
                dve.wait_ge(sem["d_free"], D["hg_g"] + j + 1)
                dve.tensor_tensor(tile(hg_k, j), tile(hg_p, j), tile(hg_q, j), ALU.mult).then_inc(sem["hg_gate"], 1)
                dve.wait_ge(sem["ho_high"], j + 1)
                dve.tensor_tensor(tile(h_lo, 4 + j), tile(hg_k, j), tile(h_hi, 4 + j).bitcast(F32), ALU.subtract)\
                    .then_inc(sem["ho_low"], 1)

            for j in range(KT):
                for g in range(2):
                    n = 2 * j + g
                    dve.wait_ge(sem["a_free"], A["merge"] + n + 1)
                    if g == 0 and j:
                        dve.wait_ge(sem["mg_high"], j)
                        dve.wait_ge(sem["mg_low"], j)
                    dve.tensor_tensor(tile(m_t, 4 + g), d_tile(D["merge"] + n), tile(m_t, (j % 2) * 2 + g), ALU.mult)\
                        .then_inc(sem["d_free"], 1)
                dve.wait_ge(sem["d_free"], D["merge"] + 2 * j + 2)
                dve.tensor_tensor(tile(m_t, 4), tile(m_t, 4), tile(m_t, 5), ALU.add).then_inc(sem["mg_sum"], 1)
                dve.wait_ge(sem["mg_high"], j + 1)
                dve.tensor_tensor(tile(m_lo, j), tile(m_t, 4), tile(m_hi, j).bitcast(F32), ALU.subtract)\
                    .then_inc(sem["mg_low"], 1)

            def add_out(n, j, gate, bank=None):
                dve.wait_ge(sem["d_full"], n + 1)
                src = ps[:, bank if bank is not None else 4 + n % 2, :]
                dve.scalar_tensor_tensor(tile(hres, j), src, gate, tile(hres, j), ALU.mult, ALU.add)\
                    .then_inc(sem["d_free"], 1)

            dve.wait_ge(sem["x_loaded"], 32)
            for j in range(KT):
                add_out(D["w_out"] + j, j, 1.0)
            norm("norm2")

            def feed_forward(name, n_ff, gate, with_ada):
                a0_, d0_ = A[name], D[name]
                with dve.Fori(0, 4) as it:
                    def ada_part(slot_no):
                        if not with_ada or not 1 <= slot_no <= 14:
                            return
                        r, part = divmod(slot_no - 1, 2)
                        cvec = D_CC if r == 6 else D_C
                        acc = tile(ada_acc, r)
                        if part == 0:
                            dve.wait_ge(sem["ada_in%d" % (r % 2)], it * (64 if r % 2 == 0 else 48) + 16 * (r // 2) + 16)
                            if r == 0:
                                dve.wait_ge(sem["bank7_free"], it + 1)
                        for k in range(4 * part, 4 * part + 4):
                            wk = ada_w[:, (r % 2) * 4096 + k * T:(r % 2) * 4096 + (k + 1) * T]
                            if k == 0:
                                m = dve.tensor_scalar(acc, wk, dcol(cvec + k), None, ALU.mult)
                            else:
                                dve.wait_ge(sem["ada_step"], it * 56 + r * 8 + k)
                                m = dve.scalar_tensor_tensor(acc, wk, dcol(cvec + k), acc, ALU.mult, ALU.add)
                            m.then_inc(sem["ada_step"], 1)
                        if part == 1:
                            dve.wait_ge(sem["ada_step"], it * 56 + r * 8 + 8)
                            dve.sem_inc(sem["ada_used"], 1)

                    for j in range(8):
                        n = it * 8 + j
                        dve.wait_ge(sem["a_free"], n + a0_ + 1)
                        dve.tensor_tensor(tile(f_s, j % 2), tile(f_r, j % 2), tile(f_r, j % 2), ALU.mult)\
                            .then_inc(sem["f_square"], 1)
                        dve.wait_ge(sem["f_square"], n + n_ff * 32 + 3)
                        dve.wait_ge(sem["f_high"], n + n_ff * 32 + 1)
                        dve.tensor_tensor(tile(h_lo, j), tile(f_s, j % 2), tile(h_hi, j).bitcast(F32), ALU.subtract)\
                            .then_inc(sem["f_low"], 1)
                        ada_part(j)
                    for j in range(8):
                        dve.wait_ge(sem["d_full"], it * 8 + d0_ + j + 1)
                        dve.scalar_tensor_tensor(tile(hres, j), ps[:, 4 + (d0_ + j) % 2, :], gate(j), tile(hres, j),
                                                 ALU.mult, ALU.add).then_inc(sem["d_free"], 1)
                        ada_part(8 + j)
                    if with_ada:
                        dve.wait_ge(sem["ada_cols"], it + 1)
                        dve.tensor_copy(mods[:, bass.ds(it * 28, 28)], ps[:, 7, 0:28]).then_inc(sem["bank7_free"], 1)

            dve.wait_ge(sem["silu_done"], 1)
            feed_forward("ff0", 0, lambda j: 1.0, True)
            dve.wait_ge(sem["bank7_free"], 5)
            ordered(dve.tensor_tensor(mods[:, :], mods[:, :], v("ada_b", 0, 4 * ADA_CHUNKS), ALU.add))
            for n, (name, cols) in enumerate((("mix0", lambda j: mod_col(0, 1, j)), ("mix0", lambda j: ctx_col(1, j)),
                                              ("ffn0", lambda j: mod_col(0, 4, j)), ("mix1", lambda j: mod_col(1, 1, j)),
                                              ("ffn1", lambda j: mod_col(1, 4, j)))):
                for j in (0, 4):
                    m = dve.scalar_tensor_tensor(dcol(D_GAIN + 8 * n + j, 4), mods[:, cols(j):cols(j) + 4], 1.0,
                                                 v(name, j, 4), ALU.add, ALU.mult)
            m.then_inc(sem["mod_ready"], 1)
            norm("final")
            dve.wait_ge(sem["mod_ready"], 1)
            norm("mix0")
            norm("ctx")
            cos = cst_b[:, P:P + T]
            sin = cst_b[:, P + T:P + 2 * T]
            dve.wait_ge(sem["kpe_rot"], 1)
            dve.tensor_tensor(q_tmp[:, :], ps[:, 4, :], sin, ALU.mult)
            ordered(dve.tensor_tensor(kpe[:, TC:TK], kpe[:, TC:TK], cos, ALU.mult))
            dve.tensor_tensor(kpe[:, TC:TK], kpe[:, TC:TK], q_tmp[:, :], ALU.add).then_inc(sem["kpe_done"], 1)
            norm("cq")
            norm("ck")
            for pr in range(4):
                dve.wait_ge(sem["qb_rot"], pr + 1)
                if pr:
                    dve.wait_ge(sem["qb_rope"], pr)
                dve.tensor_tensor(q_tmp[:, :], ps[:, 5, :], sin, ALU.mult)
                ordered(dve.tensor_tensor(tile(qr, pr), tile(q_rp, pr % 2), cos, ALU.mult))
                dve.tensor_tensor(tile(qr, pr), tile(qr, pr), q_tmp[:, :], ALU.add).then_inc(sem["qb_rope"], 1)
            for h in range(MLA_HEADS):
                hp, pair = half_of(h), h // 2
                krt, kro = (kr_a, pair * TK) if pair < 2 else (kr_b, (pair - 2) * TK)
                dve.wait_ge(sem["kb_r"], h + 1)
                dve.tensor_tensor(kn[:, h * TK:(h + 1) * TK], kn[:, h * TK:(h + 1) * TK], k_r[:, :], ALU.mult)
                dve.tensor_tensor(krt[hp, kro:kro + TK], kpe[hp, :], k_r[hp, :], ALU.mult)\
                    .then_inc(sem["kb_norm"], 1)
            dve.wait_ge(sem["rq_exp"], 1)
            dve.tensor_scalar(dcol(D_RQ, 32), dcol(D_RQ, 32), 192.0 ** -0.5, None, ALU.mult)\
                .then_inc(sem["rq_ready"], 1)
            dve.wait_ge(sem["rq_ready"], 1)

            def at_max(s):
                b = (s % 2) * 2
                o = D_AT + 4 * (s % 2)
                dve.wait_ge(sem["s_full"], s + 1)
                if s >= 2:
                    dve.wait_ge(sem["p_norm"], s - 1)
                ordered(dve.tensor_reduce(dcol(o), ps_pair(b)[:, 0:TK], AX_X, ALU.max))
                dve.tensor_scalar(dcol(o + 1), dcol(o), dcol(D_RQ + s), -1.0, ALU.mult, ALU.mult)\
                    .then_inc(sem["s_max"], 1)

            def at_norm(s):
                o = D_AT + 4 * (s % 2)
                dve.wait_ge(sem["s_exp"], s + 1)
                ordered(dve.reciprocal(dcol(o + 3), dcol(o + 2)))
                p = tile(at_p, s % 2, TK)
                dve.tensor_scalar(p, p, dcol(o + 3), None, ALU.mult).then_inc(sem["p_norm"], 1)

            def o_low_of(h):
                dve.wait_ge(sem["o_high"], h + 1)
                dve.tensor_tensor(tile(o_lo, h), ps[:, 6 + h % 2, :], tile(o_hi, h).bitcast(F32), ALU.subtract)\
                    .then_inc(sem["o_low"], 1)

            at_max(0)
            for s in range(4 * MLA_HEADS):
                if s + 1 < 4 * MLA_HEADS:
                    at_max(s + 1)
                at_norm(s)
                if s % 4 == 2 and s > 4:
                    o_low_of(s // 4 - 1)
            o_low_of(MLA_HEADS - 1)
            for j in range(KT):
                add_out(D["mla_o"] + j, j, mcol(mod_col(0, 2, j)))
            norm("ffn0")
            feed_forward("ff1", 1, lambda j: mcol(mod_col(0, 5, j)), False)

            norm("mix1")
            for i in range(4):
                dve.wait_ge(sem["gm_rows"], i + 1)
                dst = (rs_b if i < 2 else bs_b)[:, (i % 2) * T:(i % 2 + 1) * T]
                dve.tensor_copy(dst, ps[:, 6 + i % 2, :]).then_inc(sem["gm_copy"], 1)
            dve.wait_ge(sem["gm_copy"], 4)
            for f in range(16):
                g = f // 2
                dve.scalar_tensor_tensor(extra[:, f * P:(f + 1) * P], rs_b[:, g * P:(g + 1) * P], v("ln_b", f),
                                         bs_b[:, g * P:(g + 1) * P], ALU.mult, ALU.add)\
                    .then_inc(sem["gm_extra"], 1)
            dve.wait_ge(sem["a_free"], A["gm_u"])
            for c in range(NC4):
                for q in range(4):
                    m = dve.bn_stats(g_st[:, (c % 2) * 24 + q * 6:(c % 2) * 24 + q * 6 + 6],
                                     gv[:, c * 2048 + q * T:c * 2048 + (q + 1) * T])
                ordered(m)
                dve.bn_aggr(g_st[:, 56 + 2 * c:58 + 2 * c], g_st[:, (c % 2) * 24:(c % 2) * 24 + 24])\
                    .then_inc(sem["gv_var"], 1)
                if c < 3:
                    dve.wait_ge(sem["gv_var"], c + 1)
            dve.wait_ge(sem["gv_rstd"], 1)
            for c in range(NC4):
                g = gv[:, c * 2048:(c + 1) * 2048]
                dve.tensor_scalar(g, g, g_st[:, 56 + 2 * c:57 + 2 * c], g_st[:, 57 + 2 * c:58 + 2 * c],
                                  ALU.subtract, ALU.mult).then_inc(sem["gv_norm"], 1)
            for half in range(2):
                for j in range(8):
                    f = half * 8 + j
                    n = D["gm_u"] + half * 16 + j
                    dve.wait_ge(sem["d_full"], n + 1)
                    ex = extra[:, f * P:(f + 1) * P].unsqueeze(1).broadcast_to([P, NC4, P])
                    src = ps[:, 4 + n % 2, :].rearrange("p (c t) -> p c t", c=NC4)
                    if f:
                        dve.wait_ge(sem["gu_mul"], f)
                    dve.scalar_tensor_tensor(g_t[:, :].rearrange("p (c t) -> p c t", c=NC4), src, v("ln_g", f), ex,
                                             ALU.mult, ALU.add).then_inc(sem["d_free"], 1)
                    dve.wait_ge(sem["d_free"], n + 1)
                    dve.wait_ge(sem["a_free"], A["gm_u"] + f + 1)
                    if f:
                        dve.wait_ge(sem["gu_high"], f)
                        dve.wait_ge(sem["gu_low"], f)
                    dve.tensor_tensor(g_s[:, :], g_t[:, :], g_u[:, :], ALU.mult).then_inc(sem["gu_mul"], 1)
                    dve.wait_ge(sem["gu_high"], f + 1)
                    dve.tensor_tensor(tile(h_lo, j), g_s[:, :], tile(h_hi, j).bitcast(F32), ALU.subtract)\
                        .then_inc(sem["gu_low"], 1)
                for j in range(8):
                    add_out(D["gm_u"] + half * 16 + 8 + j, j, mcol(mod_col(1, 2, j)))
            norm("ffn1")
            feed_forward("ff2", 2, lambda j: mcol(mod_col(1, 5, j)), False)


def _units(w, k_tiles, m_tiles):
    t = w.reshape(k_tiles, P, m_tiles, P).transpose(2, 0, 1, 3).reshape(k_tiles * m_tiles, P, P)
    return _pack(t)


def _pack(tiles):
    import numpy as np
    n = tiles.shape[0]
    if n % 8:
        tiles = np.concatenate([tiles, np.zeros((8 - n % 8, P, P), tiles.dtype)])
    return tiles.reshape(-1, 8, P, P).transpose(0, 2, 1, 3).reshape(-1, P, UNIT)


def _moving(w, k_tiles):
    n = w.shape[1] // T
    return w.reshape(k_tiles // 2, 2, P, n, T).transpose(3, 0, 2, 1, 4).reshape(-1, P, UNIT)


def _half_first(w1, w2, up_cols=8):
    import numpy as np
    parts = []
    for g in range(w2.shape[0] // (8 * P)):
        s = slice(g * 8 * P, (g + 1) * 8 * P)
        parts += [_units(w1[:, s], 8, 8), _units(w2[s, :], 8, 8)]
    return np.concatenate(parts)


def _stream(i):
    import numpy as np
    a = {k: np.asarray(x) for k, x in i.items()}
    w = a["w_in"][0]
    cut = lambda o, n: w[:, o:o + n]
    parts = [_units(cut(0, 512), 8, 4), _units(cut(512, 512), 8, 4), _moving(cut(1024, 512), 8),
             _units(cut(1536, 512), 8, 4), _moving(cut(2048, 512), 8), _units(cut(2560, 512), 8, 4),
             _units(cut(3072, 512), 8, 4)]
    ga, gb = _units(cut(3584, 1024), 8, 8), _units(cut(4608, 1024), 8, 8)
    both = np.concatenate([a["w_o_sb"][0], a["w_o_hg"][0]])
    o = _units(both, 8, 8)
    parts.append(np.stack([ga, gb, o], 1).reshape(24, P, UNIT))
    parts.append(_units(a["w_out"][0], 8, 8))
    parts.append(_half_first(a["w_ff1"][0], a["w_ff2"][0]))
    parts.append(_units(a["mla_wq_a_2"][0], 8, 3))
    kva = a["mla_wkv_a_2"][0]
    parts.append(_units(np.concatenate([kva, kva[:, 256:320]], 1), 8, 3))
    qb = a["mla_wq_b_2"][0].reshape(384, MLA_HEADS, 192)
    blocks = []
    for pr in range(4):
        blocks += [qb[:, 2 * pr, 0:128], qb[:, 2 * pr + 1, 0:128],
                   np.concatenate([qb[:, 2 * pr, 128:192], qb[:, 2 * pr + 1, 128:192]], 1)]
    parts.append(_units(np.concatenate(blocks, 1), 3, 12))
    kvb = a["mla_wkv_b_2"][0].reshape(256, MLA_HEADS, 256)
    parts.append(_units(np.ascontiguousarray(kvb[:, :, 0:128]).reshape(256, 1024), 2, 8))
    parts.append(_moving(np.ascontiguousarray(kvb[:, :, 128:256]).reshape(256, 1024), 2))
    parts.append(_units(a["mla_wo_2"][0], 8, 8))
    parts.append(_half_first(a["ffn_w1_2"][0], a["ffn_w2_2"][0]))
    gi = a["gm_w_in_2"][0]
    parts.append(_moving(gi[:, 2048:4096], 8))
    parts.append(_half_first(gi[:, 0:2048], a["gm_w_out_2"][0]))
    parts.append(_half_first(a["ffn_w1_2"][1], a["ffn_w2_2"][1]))
    s = np.concatenate(parts)
    assert s.shape[0] == N_UNITS, s.shape
    if N_UNITS % 2:
        s = np.concatenate([s, np.zeros((1, P, UNIT), s.dtype)])
    return np.ascontiguousarray(s.reshape(-1, 2, P, UNIT).transpose(0, 2, 1, 3)).reshape(-1, P, 2 * UNIT)


def _cols(x):
    import numpy as np
    return np.asarray(x).reshape(-1, P).T


def _ada(i):
    import numpy as np
    w, b = np.asarray(i["ada_w_2"]), np.asarray(i["ada_b_2"])
    chunks, bias = [], []
    for it in range(4):
        layer = it // 2
        todo = [(layer, (it % 2) * 6 + r) for r in range(6)] + [(0, it)]
        for l, c in todo:
            chunks.append(w[l][:, c * T:(c + 1) * T].reshape(KT, P, T).transpose(1, 0, 2).reshape(P, KT * T))
            bias.append(_cols(b[l][c * T:(c + 1) * T]))
    return np.stack(chunks), np.concatenate(bias, 1)


def _vectors(i, ada_bias):
    import numpy as np
    a = {k: np.asarray(x) for k, x in i.items()}
    twice = lambda x: np.concatenate([x, x])
    got = {
        "norm1": a["norm1_g"][0], "gate_a": a["b_gate"][0][:1024], "gate_b": a["b_gate"][0][1024:],
        "lb0": a["lb_logits"][0], "lb1": a["lb_logits"][1], "hg_norm": a["hg_norm_g"][0],
        "norm2": a["norm2_g"][0], "final": a["final_g"], "mix0": a["norm_mix_g_2"][0],
        "ffn0": a["norm_ffn_g_2"][0], "mix1": a["norm_mix_g_2"][1], "ffn1": a["norm_ffn_g_2"][1],
        "q_a_norm": a["mla_q_a_norm_2"][0], "kv_a_norm": a["mla_kv_a_norm_2"][0],
        "q_nope": a["mla_q_norm_2"][0][:128], "q_rope": twice(a["mla_q_norm_2"][0][128:]),
        "k_nope": a["mla_k_norm_2"][0][:128], "k_rope": twice(a["mla_k_norm_2"][0][128:]),
        "ln_g": a["gm_ln_g_2"][0], "ln_b": a["gm_ln_b_2"][0], "c": a["c_2"][0], "c_ctx": a["c_ctx_2"],
    }
    cols = [ada_bias if n == "ada_b" else _cols(got[n]) for n in VECS]
    return np.ascontiguousarray(np.concatenate(cols, 1))


def _constants():
    import numpy as np
    s, t = np.arange(P)[:, None], np.arange(P)[None, :]
    f = lambda x: x.astype(np.float32)
    levels = [f(s == t)]
    for m in HGRN_LEVELS:
        same = s // (2 * m) == t // (2 * m)
        levels.append(f(same & (s // m % 2 == 0) & (t // m % 2 == 1)))
    restart = np.ones((P, T), np.float32)
    restart[:, ::P] = 0
    a = np.concatenate([-f(s >= t), f(s >= t) * np.float32(-1e30), f(s < t)] + levels + [restart], 1)
    rot = np.zeros((P, P), np.float32)
    for base in (0, 64):
        for half in (0, 32):
            for j in range(16):
                o = base + half + j
                rot[o + 16, o] = -1
                rot[o, o + 16] = 1
    rows = T // 64
    row = np.repeat(np.arange(rows, dtype=np.float32), 64)
    col = np.tile(np.arange(64, dtype=np.float32), rows)
    inv = np.float32(10000.0) ** (-np.arange(0, 32, 2, dtype=np.float32) / np.float32(32))
    ar, ac = row[:, None] * inv[None, :], col[:, None] * inv[None, :]
    ang = np.concatenate([ar, ar, ac, ac], -1)
    ang = np.concatenate([ang, ang], -1).T
    half = np.stack([np.arange(P) < 64, np.arange(P) >= 64], 1)
    b = np.concatenate([rot, np.cos(ang), np.sin(ang), half], 1).astype(np.float32)
    return np.ascontiguousarray(a), np.ascontiguousarray(b), np.eye(P, dtype=np.float32)


def _arrays(inputs):
    import numpy as np
    ada, ada_bias = _ada(inputs)
    ca, cb, ident = _constants()
    fm = lambda x, n: np.ascontiguousarray(np.asarray(x)[0].T.reshape(KT, P, n).transpose(1, 0, 2)).reshape(P, KT * n)
    ws = np.asarray(inputs["gm_ws_2"])[0]
    return {
        "weights": _stream(inputs), "ada": ada, "x_t": fm(inputs["x"], T), "ctx_t": fm(inputs["ctx_2"], TC),
        "vecs_in": _vectors(inputs, ada_bias), "const_a": ca, "const_b": cb, "ident_in": ident,
        "ws_t": np.ascontiguousarray(ws.transpose(2, 0, 1)).reshape(P, KT * P),
        "bs_in": np.ascontiguousarray(np.asarray(inputs["gm_bs_2"])[0]).reshape(1, KT * P),
    }


def kernel(**inputs):
    import numpy as np
    import concourse.bacc as bacc
    from concourse.bass_utils import run_bass_kernel_spmd

    nc = bacc.Bacc("TRN2", target_bir_lowering=False, num_devices=1)
    arrays = _arrays(inputs)
    aps = {n: nc.dram_tensor(n, a.shape, mybir.dt.from_np(a.dtype), kind="ExternalInput").ap()
           for n, a in arrays.items()}
    out = nc.dram_tensor("out", (P, KT * T), F32, kind="ExternalOutput").ap()
    build_program(nc, out=out, **aps)
    r = run_bass_kernel_spmd(nc, [arrays], core_ids=[0])
    got = np.asarray(r.results[0]["out"]).reshape(P, KT, T)
    return np.ascontiguousarray(got.transpose(2, 1, 0)).reshape(1, T, D_MODEL)
```

```python
from contextlib import ExitStack

import concourse.bass as bass
from concourse import mybir

P = 128
T = 512
TC = 256
TK = T + TC
KT = 8
NC4 = T // P
SB_HEADS = 8
HG_HEADS = 4
MLA_HEADS = 8
EPS = 1e-6
D_MODEL = 1024
UNIT = 1024
W_SLOTS = 4
RAW_SLOTS = 4
CHUNK_UNITS = 2
HGRN_LEVELS = (64, 32, 16, 8, 4, 2, 1)
ADA_CHUNKS = 28
ADA_PER_IT = 7

F32 = mybir.dt.float32
F32R = mybir.dt.float32r
I32 = mybir.dt.int32
ALU = mybir.AluOpType
ACT = mybir.ActivationFunctionType

STREAM = [
    ("sb_q", 4), ("sb_k", 4), ("sb_v", 4), ("hg_f", 4), ("hg_i", 4), ("hg_q", 4), ("hg_g", 4),
    ("merge", 24), ("w_out", 8), ("ff0", 64),
    ("q_a", 3), ("kv_a", 3), ("q_b", 5), ("k_b", 2), ("v_b", 2), ("mla_o", 8), ("ff1", 64),
    ("gm_v", 16), ("gm_u", 32), ("ff2", 64),
]
N_UNITS = sum(n for _, n in STREAM)
FIRST = {}
_at = 0
for _name, _n in STREAM:
    FIRST[_name] = _at
    _at += _n

VECS = {}
_at = 0
for _name, _n in [
    ("norm1", 8), ("gate_a", 8), ("gate_b", 8), ("lb0", 4), ("lb1", 4), ("hg_norm", 4), ("norm2", 8),
    ("final", 8), ("mix0", 8), ("ffn0", 8), ("mix1", 8), ("ffn1", 8), ("q_a_norm", 3),
    ("kv_a_norm", 2), ("q_nope", 1), ("q_rope", 1), ("k_nope", 1), ("k_rope", 1), ("ln_g", 16),
    ("ln_b", 16), ("ada_b", 4 * ADA_CHUNKS), ("c", 8), ("c_ctx", 8),
]:
    VECS[_name] = (_at, _n)
    _at += _n
N_VECS = _at

CONSTS = {}
_at = 0
for _name, _n in [("neg_tri", P), ("big_neg", P), ("strict", P), ("levels", 8 * P), ("restart", T)]:
    CONSTS[_name] = (_at, _n)
    _at += _n
N_CONST_A = _at
_at = 0
for _name, _n in [("rot", P), ("cos", T), ("sin", T), ("half", 2)]:
    CONSTS[_name] = (_at, _n)
    _at += _n
N_CONST_B = _at


def build_program(nc, weights, ada, x_t, ctx_t, vecs_in, const_a, const_b, ident_in, ws_t, bs_in, out):
    ctx = ExitStack()
    with ctx:
        KB = 1024
        a0 = (nc.sbuf_base + 31) // 32 * 32

        def at(name, off, cols, dt=F32):
            return nc.alloc_sbuf_tensor_at(name, [P, cols], dt, offset=a0 + off)

        raw = at("raw", 0, RAW_SLOTS * 2 * UNIT)
        w_hi = at("w_hi", 32 * KB, W_SLOTS * UNIT, F32R)
        w_lo = at("w_lo", 48 * KB, W_SLOTS * UNIT, F32R)
        XH0, HH0, HL0, H0 = 64 * KB, 96 * KB, 112 * KB, 128 * KB
        M0 = 144 * KB
        x_hi = at("x_hi", XH0, KT * T, F32R)
        x_lo = at("x_lo", XH0 + 16 * KB, KT * T, F32R)
        h_hi = at("h_hi", HH0, KT * T, F32R)
        h_lo = at("h_lo", HL0, KT * T, F32R)
        hres = at("hres", H0, KT * T)
        n_sq = at("n_sq", M0 + 54 * KB, 2 * T)
        n_acc = at("n_acc", M0 + 58 * KB, T)
        l_sq = at("l_sq", HL0, 2 * TK)
        l_acc = at("l_acc", HL0 + 6 * KB, TK)
        g_sq = at("g_sq", M0 + 46 * KB, 2 * T)
        g_acc = at("g_acc", M0 + 50 * KB, T)
        g_x = at("g_x", HL0, 2 * T)
        n_r = at("n_r", HL0 + 9 * KB, TK)
        n_t = at("n_t", HL0 + 12 * KB, 2 * T)
        S0 = M0 + 60 * KB
        ones = at("ones", S0, P)
        ident = at("ident", S0 + 512, P)
        neg_ones = at("neg_ones", S0 + 1024, P)
        vecs = at("vecs", S0 + 1536, N_VECS)
        mods = at("mods", S0 + 1536 + 4 * N_VECS + 12, 4 * ADA_CHUNKS)
        derived = at("derived", S0 + 1536 + 4 * N_VECS + 12 + 448, 120)

        cst_a = at("cst_a", M0, N_CONST_A)
        sb_q = at("sb_q", M0 + 8 * KB, 4 * T)
        sb_k = at("sb_k", M0 + 16 * KB, 4 * T)
        sb_v = at("sb_v", M0 + 24 * KB, 4 * T)
        sb_e = at("sb_e", M0 + 32 * KB, 1280)
        sb_l = at("sb_l", M0 + 37 * KB, 1280)
        sb_sp = at("sb_sp", M0 + 42 * KB, 2 * 1280)
        sb_w = at("sb_w", M0 + 52 * KB, 1280)
        hg_b = at("hg_b", M0 + 8 * KB, 4 * T)
        hg_k = at("hg_k", M0 + 16 * KB, 4 * T)
        hg_q = at("hg_q", M0 + 24 * KB, 4 * T)
        hg_v = at("hg_v", M0 + 32 * KB, 4 * T)
        hg_a = at("hg_a", M0 + 40 * KB, 4 * T)
        hg_p = at("hg_p", M0 + 48 * KB, 4 * T)
        hg_s = at("hg_s", M0 + 56 * KB, 2 * T)
        hg_off = at("hg_off", H0, 4 * 6 * P)
        hg_edge = at("hg_edge", H0 + 12 * KB, 2 * 4 * P)
        m_hi = at("m_hi", M0, KT * T, F32R)
        m_lo = at("m_lo", M0 + 16 * KB, KT * T, F32R)
        m_t = at("m_t", M0 + 32 * KB, 6 * T)
        ada_w = at("ada_w", M0, 2 * 4096)
        ada_acc = at("ada_acc", M0 + 32 * KB, ADA_PER_IT * T)
        f_r = at("f_r", M0 + 46 * KB, 2 * T)
        f_s = at("f_s", M0 + 50 * KB, 2 * T)
        cst_b = at("cst_b", M0, N_CONST_B)
        cq_hi = at("cq_hi", M0 + 5 * KB, 3 * T, F32R)
        cq_lo = at("cq_lo", M0 + 11 * KB, 3 * T, F32R)
        ck_hi = at("ck_hi", M0 + 17 * KB, 2 * TK, F32R)
        ck_lo = at("ck_lo", M0 + 23 * KB, 2 * TK, F32R)
        kpe = at("kpe", M0 + 29 * KB, TK)
        ml_v = at("ml_v", M0 + 36 * KB, 6 * 1024)
        ctxx = at("ctxx", M0 + 36 * KB, KT * TC)
        cq_raw = at("cq_raw", M0 + 44 * KB, 3 * T)
        ck_raw = at("ck_raw", M0 + 50 * KB, 2 * TK)
        kpe_raw = at("kpe_raw", M0 + 56 * KB, TK)
        kpe_sq = at("kpe_sq", M0 + 32 * KB, TK)
        q_sq = at("q_sq", M0 + 36 * KB, 6 * T)
        q_rp = at("q_rp", M0 + 48 * KB, 2 * T)
        k_sq = at("k_sq", M0 + 5 * KB, 2 * TK)
        k_r = at("k_r", M0 + 11 * KB, 2 * TK)
        q_tmp = at("q_tmp", XH0 + 30 * KB, T)
        c_hi = at("c_hi", HH0, KT * TC, F32R)
        c_lo = at("c_lo", HH0 + 8 * KB, KT * TC, F32R)
        qn = at("qn", XH0, MLA_HEADS * T)
        qr = at("qr", XH0 + 16 * KB, 4 * T)
        kr_a = at("kr_a", XH0 + 24 * KB, 2 * TK)
        kn = at("kn", HH0, MLA_HEADS * TK)
        kr_b = at("kr_b", HH0 + 24 * KB, 2 * TK)
        at_p = at("at_p", M0, 2 * TK)
        at_pt = at("at_pt", M0 + 6 * KB, 12 * T)
        o_hi = at("o_hi", XH0, KT * T, F32R)
        o_lo = at("o_lo", HH0, KT * T, F32R)
        gv = at("gv", M0, 4 * 2048)
        wst = at("wst", M0 + 32 * KB, KT * P)
        rs_b = at("rs_b", M0 + 36 * KB, KT * P)
        bs_b = at("bs_b", M0 + 40 * KB, KT * P)
        extra = at("extra", M0 + 44 * KB, 16 * P)
        g_u = at("g_u", M0 + 52 * KB, T)
        g_t = at("g_t", M0 + 54 * KB, T)
        g_s = at("g_s", M0 + 56 * KB, T)
        g_st = at("g_st", M0 + 58 * KB, 64)
        bs_row = at("bs_row", M0, KT * P)

        ps = ctx.enter_context(nc.psum_tensor("ps", [P, 8, T], F32))

        names = (
            ["raw_in%d" % i for i in range(RAW_SLOTS)] + ["x_in%d" % i for i in range(4)]
            + ["split_turn", "w_high", "w_ready", "unit_started", "a_full", "a_free", "d_full", "d_free"]
            + ["x_loaded", "vecs_loaded", "small_loaded", "ones_set", "act_order", "dve_order"]
            + ["n_squared", "n_added", "n_total", "n_log", "n_scale", "n_scaled", "n_high", "n_done"]
            + ["g_squared", "g_added", "g_inverse", "g_sum", "g_log", "g_scale", "final_done"]
            + ["sp_scores", "sp_log", "sp_soft", "sp_decay", "sp_weights", "sp_out", "sp_high", "sp_low"]
            + ["hp_zero", "lb_diff", "lb_ready", "silu_c", "silu_done", "hf_sig", "hf_f", "hf_k", "hf_qs", "hf_log", "hf_b"]
            + ["lv_diff", "lv_exp", "lv_pair", "lv_score", "lv_kept", "off_diff", "off_exp", "ho_ready",
               "off_score", "off_kept", "ho_out", "ho_sq", "ho_total", "ho_log", "ho_scale", "ho_norm",
               "hg_sig", "hg_gate", "ho_high", "ho_low"]
            + ["mg_gate", "mg_sum", "mg_high", "mg_low"]
            + ["f_square", "f_high", "f_low", "ada_in0", "ada_in1", "ada_used", "ada_step", "ada_cols",
               "bank7_free", "mod_ready"]
            + ["ctx_loaded", "cstb_loaded", "qb_copy", "qb_sums", "qb_rot", "qb_rope", "rq_log", "rq_exp",
               "rq_ready", "kpe_scaled", "kpe_squared", "kpe_rot", "kpe_done", "kb_copy", "kb_sum", "kb_r",
               "kb_norm"]
            + ["s_full", "s_max", "s_exp", "p_norm", "t_full", "t_copied", "o_full", "o_high", "o_low"]
            + ["gm_loaded", "gm_rows", "gm_copy", "gm_extra", "gv_var", "gv_log", "gv_rstd", "gv_norm", "gu_gelu",
               "gu_mul", "gu_high", "gu_low", "stored"]
        )
        sem = {n: ctx.enter_context(nc.semaphore(n)) for n in names}

        def v(name, j=0, n=1):
            o = VECS[name][0] + j
            return vecs[:, o:o + n]

        def tile(t, j, w=T):
            return t[:, j * w:(j + 1) * w]

        D_C, D_CC, D_LB, D_OLB, D_GAIN, D_RQ, D_AT = 0, 8, 16, 20, 24, 64, 96

        def dcol(o, n=1):
            return derived[:, o:o + n]

        def mod_col(layer, part, j):
            fb = part * KT + j
            chunk = fb // 4
            return (layer * 2 + chunk // 6) * 4 * ADA_PER_IT + (chunk % 6) * 4 + fb % 4

        def ctx_col(part, j):
            fb = part * KT + j
            return (fb // 4) * 4 * ADA_PER_IT + 24 + fb % 4

        def mcol(c):
            return mods[:, c:c + 1]

        A_TILES = [("sb_qk", 8), ("sb_v", 4), ("hg_f", 4), ("hg_i", 4), ("merge", 16), ("ff0", 32),
                   ("q_a", 3), ("kv_a", 6), ("q_b", 12), ("kv_b", 28), ("ff1", 32),
                   ("gm_v", 16), ("gm_u", 16), ("ff2", 32)]
        D_TILES = [("hg_q", 4), ("hg_g", 4), ("merge", 16), ("w_out", 8), ("ff0", 32), ("mla_o", 8),
                   ("ff1", 32), ("gm_u", 32), ("ff2", 32)]

        def firsts(table):
            n, found = 0, {}
            for name, k in table:
                found[name] = n
                n += k
            found["end"] = n
            return found

        A = firsts(A_TILES)
        D = firsts(D_TILES)
        NORMS = [("norm1", 8), ("norm2", 8), ("final", 8), ("ctx", 8), ("cq", 3), ("ck", 2),
                 ("ffn0", 8), ("mix1", 8), ("ffn1", 8)]
        NSQ = firsts([(n, k - 1) for n, k in NORMS])
        NT = firsts(NORMS)
        NI = {n: i for i, (n, _) in enumerate(NORMS)}

        V_AFTER = (2, 1, 2, 1, 2, 1, 2, 1)
        V_FIRST = [sum(V_AFTER[:h]) for h in range(MLA_HEADS)]

        def k_tile(h):
            return A["kv_b"] + 2 * h + V_FIRST[h]

        def v_tile(i):
            h = max(g for g in range(MLA_HEADS) if V_FIRST[g] <= i)
            return A["kv_b"] + 2 * (h + 1) + i

        def squares_at(name):
            return (l_sq, l_acc) if name in ("cq", "ck") else (n_sq, n_acc)

        def wait_pos(eng, s, value):
            if not isinstance(value, int) or value > 0:
                eng.wait_ge(sem[s], value)

        block = ctx.enter_context(nc.Block())

        @block.sync
        def _(sp):
            for i in range(4):
                sp.dma_start(hres[:, 2 * i * T:2 * (i + 1) * T], x_t[:, 2 * i * T:2 * (i + 1) * T])\
                    .then_inc(sem["x_in%d" % i], 16)

            def load_chunk(c, slot):
                sp.dma_start(raw[:, slot * 2 * UNIT:(slot + 1) * 2 * UNIT], weights[c, :, :])\
                    .then_inc(sem["raw_in%d" % slot], 16)

            sp.dma_start(vecs[:, :], vecs_in).then_inc(sem["vecs_loaded"], 16)
            for c in range(RAW_SLOTS):
                load_chunk(c, c)
                if c == 1:
                    sp.dma_start(ident[:, :], ident_in).then_inc(sem["small_loaded"], 16)
                    sp.dma_start(cst_a[:, :], const_a).then_inc(sem["small_loaded"], 16)
            n_chunks = (N_UNITS + 1) // CHUNK_UNITS
            rounds = n_chunks // RAW_SLOTS
            with sp.Fori(1, rounds) as r:
                for s in range(RAW_SLOTS):
                    sp.wait_ge(sem["w_ready"], r * 8 - 8 + 2 * s + 2)
                    load_chunk(r * RAW_SLOTS + s, s)
            for c in range(rounds * RAW_SLOTS, n_chunks):
                sp.wait_ge(sem["w_ready"], 2 * (c - RAW_SLOTS) + 2)
                load_chunk(c, c % RAW_SLOTS)

        @block.gpsimd
        def _(pool):
            def split_unit(u, k, first=False):
                if k % 2 == 0:
                    slot = k // 2
                    pool.wait_ge(sem["raw_in%d" % slot], (u - k) * 2 + 16)
                src = raw[:, k * UNIT:(k + 1) * UNIT]
                s = k % W_SLOTS
                if not first:
                    pool.wait_ge(sem["unit_started"], u - W_SLOTS + 2)
                pool.sem_inc(sem["split_turn"], 1)
                pool.tensor_scalar(tile(w_hi, s, UNIT), src, 1.0, 1.0, ALU.mult, ALU.mult)\
                    .then_inc(sem["w_high"], 1)
                pool.wait_ge(sem["w_high"], u + 1)
                pool.tensor_tensor(tile(w_lo, s, UNIT), src, tile(w_hi, s, UNIT).bitcast(F32), ALU.subtract)\
                    .then_inc(sem["w_ready"], 1)

            for u in range(8):
                split_unit(u, u, u < W_SLOTS)
            with pool.Fori(1, N_UNITS // 8) as r:
                for k in range(8):
                    split_unit(r * 8 + k, k)
            for u in range(N_UNITS // 8 * 8, N_UNITS):
                split_unit(u, u % 8)

        @block.tensor
        def _(pe):
            def w(t, u, j):
                return t[:, (u % W_SLOTS) * UNIT + j * P:(u % W_SLOTS) * UNIT + (j + 1) * P]

            class Units:
                now = -1

            def start_unit(u, ready=None):
                pe.wait_ge(sem["w_ready"], (u if ready is None else ready) + 1)

            def group(dst, u, parts, first=True, last=True, new_unit=True, each=None, ready=None):
                if new_unit:
                    start_unit(u, ready)
                n = len(parts)
                for i, (j, hi, lo) in enumerate(parts):
                    if each is not None:
                        each(i)
                    m = pe.matmul(dst, w(w_hi, u, j), lo, start=first and i == 0, stop=False)
                    if new_unit and i == 0:
                        m.then_inc(sem["unit_started"], 1)
                    pe.matmul(dst, w(w_hi, u, j), hi, start=False, stop=False)
                    m = pe.matmul(dst, w(w_lo, u, j), hi, start=False, stop=last and i == n - 1)
                return m

            def a_bank(n):
                wait_pos(pe, "a_free", n - 3)
                return ps[:, n % 4, :]

            def d_bank(n):
                wait_pos(pe, "d_free", n - 1)
                return ps[:, 4 + n % 2, :]

            def x_parts(hi=x_hi, lo=x_lo, k=KT, w_=T, first_tile=0):
                return [(first_tile + j, tile(hi, j, w_), tile(lo, j, w_)) for j in range(k)]

            def stat(name, w_=T):
                i = NI[name]
                pe.wait_ge(sem["n_added"], NSQ[name] + dict(NORMS)[name] - 1)
                if i:
                    pe.wait_ge(sem["n_scale"], i)
                acc = squares_at(name)[1]
                m = pe.matmul(ps[:, 6, 0:min(w_, T)], ones[:, :], acc[:, 0:min(w_, T)], start=True, stop=True)
                if w_ > T:
                    m = pe.matmul(ps[:, 7, 0:w_ - T], ones[:, :], acc[:, T:w_], start=True, stop=True)
                if name == "final":
                    pe.wait_ge(sem["bank7_free"], 5)
                    pe.wait_ge(sem["g_added"], KT - 1)
                    m = pe.matmul(ps[:, 7, :], ones[:, :], g_acc[:, :], start=True, stop=True)
                m.then_inc(sem["n_total"], 1)

            def norm_waits(name):
                def each(i):
                    pe.wait_ge(sem["n_done"], NT[name] + i + 1)
                return each

            def feature_major(first_u, n, a0_, pool="a", each=None):
                for j in range(n):
                    dst = a_bank(a0_ + j) if pool == "a" else d_bank(a0_ + j)
                    group(dst, first_u + j, x_parts(), each=each if j == 0 else None)\
                        .then_inc(sem[pool + "_full"], 1)

            def token_major(first_u, a0_, n_cols=1):
                for cb in range(n_cols):
                    for uu in range(4):
                        u = first_u + cb * 4 + uu
                        start_unit(u)
                        s0 = (u % W_SLOTS) * UNIT
                        for c in range(NC4):
                            n = a0_ + cb * 4 + c
                            dst = a_bank(n) if uu == 0 else ps[:, n % 4, :]
                            for kk in range(2):
                                k = uu * 2 + kk
                                xh = x_hi[:, k * T + c * P:k * T + (c + 1) * P]
                                xl = x_lo[:, k * T + c * P:k * T + (c + 1) * P]
                                wh = w_hi[:, s0 + kk * T:s0 + (kk + 1) * T]
                                wl = w_lo[:, s0 + kk * T:s0 + (kk + 1) * T]
                                m = pe.matmul(dst, xl, wh, start=k == 0, stop=False)
                                if c == 0 and kk == 0:
                                    m.then_inc(sem["unit_started"], 1)
                                pe.matmul(dst, xh, wh, start=False, stop=False)
                                m = pe.matmul(dst, xh, wl, start=False, stop=k == KT - 1)
                            if uu == 3:
                                m.then_inc(sem["a_full"], 1)

            pe.wait_ge(sem["ones_set"], 2)
            stat("norm1")
            feature_major(FIRST["sb_q"], 8, A["sb_qk"], each=norm_waits("norm1"))
            token_major(FIRST["sb_v"], A["sb_v"])

            def z(h, i):
                b = (h % 2) * 3
                if i == 3:
                    return ps[:, b + 1, 0:P]
                return ps[:, b + i, i * P:T]

            def head_half(h):
                return slice(64 * (h % 2), 64 * (h % 2) + 64)

            def sb_scores(h):
                hp = head_half(h)
                if h < 2:
                    pe.wait_ge(sem["a_free"], A["hg_f"])
                else:
                    pe.wait_ge(sem["sp_weights"], 4 * (h - 1))
                for i in (0, 1, 2, 3):
                    m = pe.matmul(z(h, i), sb_k[hp, (h // 2) * T + i * P:(h // 2) * T + (i + 1) * P],
                                  sb_q[hp, (h // 2) * T + i * P:(h // 2 + 1) * T], start=i != 3, stop=True,
                                  skip_group_check=True)
                m.then_inc(sem["sp_scores"], 1)

            def sb_decay(h):
                seg = [0, 512, 896, 1152]
                buf = (h % 2) * 1280
                pe.wait_ge(sem["sp_soft"], 4 * h + 4)
                for i in range(4):
                    zi = z(h, i)
                    pe.matmul(zi[:, 0:P], ident[:, :], cst("big_neg"), start=False, stop=True,
                              skip_group_check=True)
                    m = pe.matmul(zi, cst("neg_tri"), sb_sp[:, buf + seg[i]:buf + seg[i] + T - i * P],
                                  start=False, stop=True, skip_group_check=True)
                    for i2 in range(i + 1, 4):
                        m = pe.matmul(zi[:, (i2 - i) * P:T - i * P], cst("neg_one"),
                                      sb_sp[:, buf + seg[i2]:buf + seg[i2] + T - i2 * P],
                                      start=False, stop=True, skip_group_check=True)
                m.then_inc(sem["sp_decay"], 1)

            def sb_values(h):
                seg = [0, 512, 896, 1152]
                dst = ps[head_half(h), 6 + h % 2, :]
                if h >= 2:
                    pe.wait_ge(sem["sp_low"], h - 1)
                for i in range(4):
                    pe.wait_ge(sem["sp_weights"], 4 * h + i + 1)
                    m = pe.matmul(dst[:, i * P:T], sb_v[:, i * T + h * 64:i * T + (h + 1) * 64],
                                  sb_w[:, seg[i]:seg[i] + T - i * P], start=i == 0, stop=i == 3,
                                  skip_group_check=True)
                m.then_inc(sem["sp_out"], 1)

            def cst(name, j=0, n=P):
                if name == "neg_one":
                    return neg_ones[:, :]
                o = CONSTS[name][0] + j
                return cst_a[:, o:o + n]

            pe.wait_ge(sem["small_loaded"], 32)
            sb_scores(0)
            for h in range(SB_HEADS):
                if h + 1 < SB_HEADS:
                    sb_scores(h + 1)
                sb_decay(h)
                sb_values(h)

            pe.wait_ge(sem["sp_weights"], 4 * SB_HEADS)
            for j in range(4):
                group(a_bank(A["hg_f"] + j), FIRST["hg_f"] + j, x_parts()).then_inc(sem["a_full"], 1)
            token_major(FIRST["hg_i"], A["hg_i"])
            for j in range(4):
                group(d_bank(D["hg_q"] + j), FIRST["hg_q"] + j, x_parts()).then_inc(sem["d_full"], 1)

            pe.wait_ge(sem["a_free"], A["merge"])
            pe.wait_ge(sem["d_free"], D["hg_g"])
            pe.wait_ge(sem["sp_low"], SB_HEADS)
            for lv in range(len(HGRN_LEVELS) + 1):
                for h in range(HG_HEADS):
                    bank = (lv % 2) * 4 + h
                    if lv >= 2:
                        pe.wait_ge(sem["lv_kept"], (lv - 2) * 4 + h + 1)
                    if lv == 0:
                        pe.wait_ge(sem["hf_k"], 4)
                        pe.wait_ge(sem["d_free"], D["hg_q"] + 4)
                    else:
                        pe.wait_ge(sem["lv_pair"], ((lv - 1) * 2 + h // 2 + 1))
                    for c in range(NC4):
                        o = h * T + c * P
                        if lv == 0:
                            l, r = hg_k[:, o:o + P], hg_q[:, o:o + P]
                        else:
                            l = r = hg_a[:, o:o + P]
                        m = pe.matmul(ps[:, bank, c * P:(c + 1) * P], l, r, start=True, stop=True)
                    m.then_inc(sem["lv_score"], 1)
            for h in range(HG_HEADS):
                pe.wait_ge(sem["ho_ready"], h + 1)
                b = (h % 2) * 2
                if h < 2:
                    pe.wait_ge(sem["lv_kept"], 4 * len(HGRN_LEVELS))
                else:
                    pe.wait_ge(sem["off_kept"], h - 1)
                km = lambda c: hg_k[:, h * T + c * P:h * T + (c + 1) * P]
                qp = lambda c: hg_q[:, h * T + c * P:h * T + (c + 1) * P]
                k0 = hg_edge[:, h * P:(h + 1) * P]
                q3 = hg_edge[:, (4 + h) * P:(5 + h) * P]
                pairs = [(km(0), qp(1)), (km(2), qp(3)), (k0, qp(2)), (k0, q3), (km(1), qp(2)), (km(1), q3)]
                for n, (l, r) in enumerate(pairs):
                    bank, o = b + n // 4, (n % 4) * P
                    m = pe.matmul(ps[:, bank, o:o + P], l, r, start=True, stop=True)
                m.then_inc(sem["off_score"], 1)
            pe.wait_ge(sem["lv_kept"], 4 * (len(HGRN_LEVELS) + 1))
            OFF = {(0, 1): 0, (2, 3): 1, (0, 2): 2, (0, 3): 3, (1, 2): 4, (1, 3): 5}
            for h in range(HG_HEADS):
                pe.wait_ge(sem["off_kept"], h + 1)
                for tc in range(NC4):
                    for sc in range(tc + 1):
                        if sc == tc:
                            r = hg_p[:, h * T + tc * P:h * T + (tc + 1) * P]
                        else:
                            o = (h * 6 + OFF[(sc, tc)]) * P
                            r = hg_off[:, o:o + P]
                        m = pe.matmul(ps[:, 4 + h, tc * P:(tc + 1) * P],
                                      hg_v[:, sc * T + h * P:sc * T + (h + 1) * P], r,
                                      start=sc == 0, stop=sc == tc)
                m.then_inc(sem["ho_out"], 1)
            for h in range(HG_HEADS):
                pe.wait_ge(sem["ho_sq"], h + 1)
                if h == 0:
                    pe.wait_ge(sem["off_kept"], HG_HEADS)
                pe.matmul(ps[:, h, :], ones[:, :], tile(hg_b, h), start=True, stop=True)\
                    .then_inc(sem["ho_total"], 1)
            pe.wait_ge(sem["ho_norm"], HG_HEADS)
            for j in range(4):
                group(d_bank(D["hg_g"] + j), FIRST["hg_g"] + j, x_parts()).then_inc(sem["d_full"], 1)

            pe.wait_ge(sem["ho_log"], HG_HEADS)
            for j in range(KT):
                u = FIRST["merge"] + 3 * j
                for g in range(2):
                    group(a_bank(A["merge"] + 2 * j + g), u + g, x_parts()).then_inc(sem["a_full"], 1)
                if j == 0:
                    pe.wait_ge(sem["sp_low"], SB_HEADS)
                    pe.wait_ge(sem["ho_low"], HG_HEADS)
                branch = lambda g: [(4 * g + k, tile(h_hi, 4 * g + k), tile(h_lo, 4 * g + k)) for k in range(4)]
                group(d_bank(D["merge"] + 2 * j), u + 2, branch(0)).then_inc(sem["d_full"], 1)
                group(d_bank(D["merge"] + 2 * j + 1), u + 2, branch(1), new_unit=False)\
                    .then_inc(sem["d_full"], 1)

            def merged(i):
                pe.wait_ge(sem["mg_low"], i + 1)
            for j in range(KT):
                group(d_bank(D["w_out"] + j), FIRST["w_out"] + j, x_parts(m_hi, m_lo),
                      each=merged if j == 0 else None).then_inc(sem["d_full"], 1)

            def feed_forward(name, norm, n_ff, with_ada):
                u0, a0_, d0_ = FIRST[name], A[name], D[name]
                with pe.Fori(0, 4) as it:
                    for j in range(8):
                        n = a0_ + it * 8 + j
                        pe.wait_ge(sem["a_free"], n - 3)
                        parts = x_parts()
                        group(ps[:, (a0_ + j) % 4, :], u0 + j, parts, ready=u0 + it * 16 + j,
                              each=norm_waits(norm) if j == 0 else None).then_inc(sem["a_full"], 1)
                    for j in range(8):
                        n = d0_ + it * 8 + j
                        pe.wait_ge(sem["d_free"], n - 1)

                        def hidden(i):
                            pe.wait_ge(sem["f_low"], it * 8 + n_ff * 32 + i + 1)
                        group(ps[:, 4 + (d0_ + j) % 2, :], u0 + 8 + j, x_parts(h_hi, h_lo),
                              ready=u0 + it * 16 + 8 + j, each=hidden if j == 0 else None)\
                            .then_inc(sem["d_full"], 1)
                    if with_ada:
                        pe.wait_ge(sem["ada_step"], it * 8 * ADA_PER_IT + 8 * ADA_PER_IT)
                        pe.wait_ge(sem["bank7_free"], it + 1)
                        for c in range(4 * ADA_PER_IT):
                            m = pe.matmul(ps[:, 7, c:c + 1], ada_acc[:, c * P:(c + 1) * P], ones[:, 0:1],
                                          start=True, stop=True)
                        m.then_inc(sem["ada_cols"], 1)

            stat("norm2")
            feed_forward("ff0", "norm2", 0, True)
            stat("final")

            for j in range(3):
                group(a_bank(A["q_a"] + j), FIRST["q_a"] + j, x_parts(), each=norm_waits("final") if j == 0 else None)\
                    .then_inc(sem["a_full"], 1)
            stat("ctx", TC)
            for j in range(3):
                n = A["kv_a"] + 2 * j
                group(a_bank(n), FIRST["kv_a"] + j, x_parts()).then_inc(sem["a_full"], 1)
                group(a_bank(n + 1)[:, 0:TC], FIRST["kv_a"] + j, x_parts(c_hi, c_lo, w_=TC), new_unit=False,
                      each=norm_waits("ctx") if j == 0 else None).then_inc(sem["a_full"], 1)
                if j == 0:
                    stat("cq")
            pe.wait_ge(sem["kpe_scaled"], 1)
            pe.wait_ge(sem["cstb_loaded"], 16)
            pe.matmul(ps[:, 4, :], cst_b[:, 0:P], kpe[:, TC:TK], start=True, stop=True).then_inc(sem["kpe_rot"], 1)
            def query_sums(pr):
                pe.wait_ge(sem["a_free"], A["q_b"] + 3 * pr + 3)
                sq = lambda i, o: q_sq[:, ((pr % 2) * 3 + i) * T + o:((pr % 2) * 3 + i) * T + o + P]
                for hh in range(2):
                    own = cst_b[:, CONSTS["half"][0] + hh:CONSTS["half"][0] + hh + 1]
                    for c in range(NC4):
                        col = (pr * 2 + hh) * 4 + c
                        pe.matmul(ps[:, 6, col:col + 1], sq(hh, c * P), ones[:, 0:1], start=True, stop=False,
                                  skip_group_check=True)
                        m = pe.matmul(ps[:, 6, col:col + 1], sq(2, c * P), own, start=False, stop=True,
                                      skip_group_check=True)
                m.then_inc(sem["qb_sums"], 1)
                pe.wait_ge(sem["qb_copy"], 3 * pr + 3)
                if pr >= 1:
                    pe.wait_ge(sem["qb_rope"], pr)
                pe.matmul(ps[:, 5, :], cst_b[:, 0:P], tile(q_rp, pr % 2), start=True, stop=True)\
                    .then_inc(sem["qb_rot"], 1)

            for b in range(12):
                pr = b // 3
                dst = a_bank(A["q_b"] + b)
                for k in range(3):
                    t = 3 * b + k
                    u = FIRST["q_b"] + t // 8
                    if b == 0:
                        pe.wait_ge(sem["n_done"], NT["cq"] + k + 1)
                    m = group(dst, u, [(t % 8, tile(cq_hi, k), tile(cq_lo, k))], first=k == 0, last=k == 2,
                              new_unit=t % 8 == 0)
                m.then_inc(sem["a_full"], 1)
                if b == 2:
                    stat("ck", TK)
                if b % 3 == 2 and pr >= 1:
                    query_sums(pr - 1)

            def key_tiles(h):
                u = FIRST["k_b"] + h // 4
                for half, (lo_, hi_) in enumerate(((0, T), (T, TK))):
                    dst = a_bank(k_tile(h) + half)[:, 0:hi_ - lo_]
                    parts = [((2 * h + k) % 8, ck_hi[:, k * TK + lo_:k * TK + hi_],
                              ck_lo[:, k * TK + lo_:k * TK + hi_]) for k in range(2)]
                    if h == 0 and half == 0:
                        pe.wait_ge(sem["n_done"], NT["ck"] + 2)
                    group(dst, u, parts, new_unit=(h % 4 == 0 and half == 0)).then_inc(sem["a_full"], 1)

            def value_tile(i):
                u = FIRST["v_b"] + i // 6
                if i % 6 == 0:
                    start_unit(u)
                dst, c = a_bank(v_tile(i)), i % 6
                s0 = (u % W_SLOTS) * UNIT
                for k in range(2):
                    kh = ck_hi[:, k * TK + c * P:k * TK + (c + 1) * P]
                    kl = ck_lo[:, k * TK + c * P:k * TK + (c + 1) * P]
                    wh = w_hi[:, s0 + k * T:s0 + (k + 1) * T]
                    wl = w_lo[:, s0 + k * T:s0 + (k + 1) * T]
                    pe.matmul(dst, kl, wh, start=k == 0, stop=False)
                    pe.matmul(dst, kh, wh, start=False, stop=False)
                    m = pe.matmul(dst, kh, wl, start=False, stop=k == 1)
                m.then_inc(sem["a_full"], 1)

            def key_sums(h):
                pe.wait_ge(sem["a_free"], k_tile(h) + 2)
                if h >= 1:
                    pe.wait_ge(sem["kb_r"], h)
                else:
                    pe.wait_ge(sem["kpe_squared"], 1)
                    pe.wait_ge(sem["kpe_done"], 1)
                sq = (h % 2) * TK
                for bank, lo_, hi_ in ((4, 0, T), (7, T, TK)):
                    m = pe.matmul(ps[:, bank, 0:hi_ - lo_], ones[:, :], k_sq[:, sq + lo_:sq + hi_], start=True,
                                  stop=False)
                    if h == MLA_HEADS - 1:
                        m.then_inc(sem["unit_started"], 1)
                    m = pe.matmul(ps[:, bank, 0:hi_ - lo_], ones[0:64, :], kpe_sq[0:64, lo_:hi_], start=False,
                                  stop=True)
                m.then_inc(sem["kb_sum"], 1)

            key_tiles(0)
            query_sums(3)
            for h in range(MLA_HEADS):
                for i in range(V_FIRST[h], V_FIRST[h] + V_AFTER[h]):
                    value_tile(i)
                if h + 1 < MLA_HEADS and h != 3:
                    key_tiles(h + 1)
                key_sums(h)
                if h == 3:
                    key_tiles(4)

            def at_scores(s, half):
                h, c = divmod(s, 4)
                b = (s % 3) * 2
                if half == 0:
                    if s >= 3:
                        pe.wait_ge(sem["s_exp"], s - 2)
                    if s % 4 == 0:
                        pe.wait_ge(sem["kb_norm"], h + 1)
                    if s == 0:
                        pe.wait_ge(sem["a_free"], A["ff1"])
                        pe.wait_ge(sem["qb_rope"], 4)
                    if s == 2:
                        pe.wait_ge(sem["kb_r"], MLA_HEADS)
                hp = head_half(h)
                pair = h // 2
                krt, kro = (kr_a, pair * TK) if pair < 2 else (kr_b, (pair - 2) * TK)
                lo_, hi_ = ((0, T), (T, TK))[half]
                dst = ps[:, b + half, 0:hi_ - lo_]
                pe.matmul(dst, qn[:, h * T + c * P:h * T + (c + 1) * P],
                          kn[:, h * TK + lo_:h * TK + hi_], start=True, stop=False)
                m = pe.matmul(dst, qr[hp, pair * T + c * P:pair * T + (c + 1) * P],
                              krt[hp, kro + lo_:kro + hi_], start=False, stop=True)
                if half == 1:
                    m.then_inc(sem["s_full"], 1)

            def at_turn(s, half):
                if half == 0:
                    pe.wait_ge(sem["p_norm"], s + 1)
                if s == 0 and half == 0:
                    pe.wait_ge(sem["rq_log"], 1)
                else:
                    pe.wait_ge(sem["t_copied"], 2 * s + half)
                for k in range(3):
                    o = (s % 2) * TK + (half * 3 + k) * P
                    m = pe.transpose(ps[:, 6, k * P:(k + 1) * P], at_p[:, o:o + P], ident[:, :])
                m.then_inc(sem["t_full"], 1)

            def at_values(h):
                pe.wait_ge(sem["t_copied"], 8 * (h + 1))
                if h >= 1:
                    pe.wait_ge(sem["o_low"], h)
                for k in range(6):
                    m = pe.matmul(ps[:, 7, :], ml_v[:, k * 1024 + h * P:k * 1024 + (h + 1) * P],
                                  tile(at_pt, (h % 2) * 6 + k), start=k == 0, stop=k == 5)
                m.then_inc(sem["o_full"], 1)

            for s in range(2):
                at_scores(s, 0)
                at_scores(s, 1)
            for s in range(4 * MLA_HEADS):
                for half in range(2):
                    at_turn(s, half)
                    if s + 2 < 4 * MLA_HEADS:
                        at_scores(s + 2, half)
                if s % 4 == 0 and s > 0:
                    at_values(s // 4 - 1)
            at_values(MLA_HEADS - 1)

            def attended(i):
                pe.wait_ge(sem["o_low"], i + 1)
            pe.wait_ge(sem["t_copied"], 8 * MLA_HEADS)
            for j in range(KT):
                group(d_bank(D["mla_o"] + j), FIRST["mla_o"] + j, x_parts(o_hi, o_lo),
                      each=attended if j == 0 else None).then_inc(sem["d_full"], 1)
            pe.wait_ge(sem["o_low"], MLA_HEADS)
            stat("ffn0")
            feed_forward("ff1", "ffn0", 1, False)

            stat("mix1")
            pe.wait_ge(sem["gm_loaded"], 32)
            pe.wait_ge(sem["d_free"], D["gm_u"])
            for i in range(2):
                pe.matmul(ps[:, 4 + i, :], ones[:, :], wst[:, i * T:(i + 1) * T], start=True, stop=True)\
                    .then_inc(sem["gm_rows"], 1)
            pe.wait_ge(sem["n_scale"], NI["mix1"] + 1)
            for i in range(2):
                pe.matmul(ps[:, 6 + i, :], ones[0:1, :], bs_row[0:1, i * T:(i + 1) * T], start=True, stop=True)\
                    .then_inc(sem["gm_rows"], 1)
            for k in range(KT):
                pe.wait_ge(sem["n_done"], NT["mix1"] + k + 1)
            token_major(FIRST["gm_v"], A["gm_v"], 4)
            for half in range(2):
                for j in range(8):
                    f = half * 8 + j
                    group(a_bank(A["gm_u"] + f), FIRST["gm_u"] + half * 16 + j, x_parts()).then_inc(sem["a_full"], 1)
                    dst = d_bank(D["gm_u"] + half * 16 + j)
                    if f == 0:
                        pe.wait_ge(sem["gm_copy"], 4)
                        pe.wait_ge(sem["gv_norm"], 4)
                    for c in range(NC4):
                        m = pe.matmul(dst[:, c * P:(c + 1) * P],
                                      gv[:, c * 2048 + f * P:c * 2048 + (f + 1) * P],
                                      wst[:, (f // 2) * P:(f // 2 + 1) * P], start=True, stop=True)
                    m.then_inc(sem["d_full"], 1)

                def mixed(i, half=half):
                    pe.wait_ge(sem["gu_low"], half * 8 + i + 1)
                for j in range(8):
                    group(d_bank(D["gm_u"] + half * 16 + 8 + j), FIRST["gm_u"] + half * 16 + 8 + j,
                          x_parts(h_hi, h_lo), each=mixed if j == 0 else None).then_inc(sem["d_full"], 1)
            stat("ffn1")
            feed_forward("ff2", "ffn1", 2, False)

        NH = NT
        NK = dict(NORMS)

        def norm_spec(name):
            main = lambda j: tile(hres, j)
            xs = (lambda j: tile(x_hi, j), lambda j: tile(x_lo, j))
            gain = lambda n: (lambda j: dcol(D_GAIN + 8 * n + j))
            return {
                "norm1": (main, T, 1024, lambda j: v("norm1", j), None, xs),
                "norm2": (main, T, 1024, lambda j: v("norm2", j), None, xs),
                "final": (main, T, 1024, gain(0), lambda j: mcol(mod_col(0, 0, j)), xs),
                "ctx": (lambda j: tile(ctxx, j, TC), TC, 1024, gain(1), lambda j: mcol(ctx_col(0, j)),
                        (lambda j: tile(c_hi, j, TC), lambda j: tile(c_lo, j, TC))),
                "cq": (lambda j: tile(cq_raw, j), T, 384, lambda j: v("q_a_norm", j), None,
                       (lambda j: tile(cq_hi, j), lambda j: tile(cq_lo, j))),
                "ck": (lambda j: tile(ck_raw, j, TK), TK, 256, lambda j: v("kv_a_norm", j), None,
                       (lambda j: tile(ck_hi, j, TK), lambda j: tile(ck_lo, j, TK))),
                "ffn0": (main, T, 1024, gain(2), lambda j: mcol(mod_col(0, 3, j)), xs),
                "mix1": (main, T, 1024, gain(3), lambda j: mcol(mod_col(1, 0, j)), xs),
                "ffn1": (main, T, 1024, gain(4), lambda j: mcol(mod_col(1, 3, j)), xs),
            }[name]

        def square_of(name, j):
            squares, w_ = squares_at(name)[0], norm_spec(name)[1]
            step = TK if squares is l_sq else T
            return squares[:, ((j - 1) % 2) * step:((j - 1) % 2) * step + w_]

        def norm_t(name, j):
            return tile(l_sq, j % 2, TK) if name == "ck" else n_t[:, (j % 2) * T:(j % 2) * T + norm_spec(name)[1]]

        seg = [0, 512, 896, 1152]
        AX_X = mybir.AxisListType.X

        def ps_pair(b):
            return ps[:, b:b + 2, :].rearrange("p b t -> p (b t)")

        def zt(h, i):
            b = (h % 2) * 3
            return ps[:, b + 1, 0:P] if i == 3 else ps[:, b + i, i * P:T]

        def half_of(h):
            return slice(64 * (h % 2), 64 * (h % 2) + 64)

        @block.scalar
        def _(act):
            def ordered(s, value):
                act.wait_ge(sem[s], value)

            def copy(out_, in_):
                return act.activation(out_, in_, ACT.Copy)

            def exp_tables():
                act.preload_act_table_set("natural_log_exp_and_others")

            def load_ada(chunk, slot):
                act.dma_start(tile(ada_w, slot, 4096), ada[bass.ds(chunk, 1), :, :].rearrange("a p n -> (a p) n"))\
                    .then_inc(sem["ada_in%d" % slot], 16)

            def norm(name, ready):
                src, w_, feats, _, shift, dst = norm_spec(name)
                i, k = NI[name], NK[name]
                squares, acc = squares_at(name)
                for j in range(k):
                    ready(j)
                    if j == 0:
                        if i:
                            act.wait_ge(sem["n_total"], i)
                        buf = acc[:, 0:w_]
                    else:
                        if j >= 3:
                            act.wait_ge(sem["n_added"], NSQ[name] + j - 2)
                        buf = square_of(name, j)
                    act.activation(buf, src(j), ACT.Square).then_inc(sem["n_squared"], 1)
                    if name == "final":
                        if j >= 3:
                            act.wait_ge(sem["g_added"], j - 2)
                        act.activation(tile(g_sq, (j - 1) % 2) if j else g_acc[:, :], src(j), ACT.Square,
                                       scale=v("final", j)).then_inc(sem["g_squared"], 1)
                if name == "norm2":
                    for chunk in range(2):
                        load_ada(chunk, chunk)
                if name == "final":
                    act.wait_ge(sem["ada_used"], ADA_CHUNKS + 1)
                    act.dma_start(cst_b[:, :], const_b).then_inc(sem["cstb_loaded"], 16)
                    act.wait_ge(sem["ada_cols"], 4)
                    act.dma_start(ctxx[:, :], ctx_t).then_inc(sem["ctx_loaded"], 16)
                act.wait_ge(sem["n_total"], i + 1)
                if i:
                    act.wait_ge(sem["n_done"], NT[name])
                pieces = [(6, 0, min(w_, T))] + ([(7, T, w_)] if w_ > T else [])
                for bank, lo_, hi_ in pieces:
                    m = act.activation(n_r[:, lo_:hi_], ps[:, bank, 0:hi_ - lo_], ACT.Ln, bias=EPS,
                                       scale=1.0 / feats)
                m.then_inc(sem["n_log"], 1)
                ordered("n_log", i + 1)
                if name == "final":
                    act.activation(g_x[:, 0:T], n_r[:, 0:w_], ACT.Exp, scale=-1.0).then_inc(sem["g_inverse"], 1)
                    ordered("g_inverse", 1)
                act.activation(n_r[:, 0:w_], n_r[:, 0:w_], ACT.Exp, scale=-0.5).then_inc(sem["n_scale"], 1)
                if name == "final":
                    act.wait_ge(sem["g_sum"], 1)
                    act.activation(g_x[:, T:2 * T], g_x[:, 0:T], ACT.Ln, bias=EPS, scale=1.0 / feats)\
                        .then_inc(sem["g_log"], 1)
                    ordered("g_log", 1)
                    act.activation(g_x[:, T:2 * T], g_x[:, T:2 * T], ACT.Exp, scale=-0.5)\
                        .then_inc(sem["g_scale"], 1)
                for j in range(k):
                    act.wait_ge(sem["n_scaled"], NH[name] + j + 1)
                    t = norm_t(name, j)
                    if shift is None:
                        m = copy(dst[0](j), t)
                    else:
                        m = act.activation(dst[0](j), t, ACT.Identity, bias=shift(j))
                    m.then_inc(sem["n_high"], 1)

            def a_tile(n):
                act.wait_ge(sem["a_full"], n + 1)
                return ps[:, n % 4, :]

            def d_tile(n):
                act.wait_ge(sem["d_full"], n + 1)
                return ps[:, 4 + n % 2, :]

            def copy_out(n, dst, scale=None):
                t = a_tile(n)
                if scale is None:
                    m = copy(dst, t)
                else:
                    m = act.activation(dst, t, ACT.Copy, scale=scale)
                m.then_inc(sem["a_free"], 1)

            exp_tables()
            norm("norm1", lambda j: act.wait_ge(sem["x_in%d" % (j // 2)], 16))
            for j in range(4):
                copy_out(A["sb_qk"] + j, tile(sb_q, j), scale=0.125)
            for j in range(4):
                copy_out(A["sb_qk"] + 4 + j, tile(sb_k, j))
            for c in range(NC4):
                copy_out(A["sb_v"] + c, tile(sb_v, c))

            def softplus(h):
                act.wait_ge(sem["sp_scores"], h + 1)
                if h:
                    ordered("sp_log", h)
                for i in range(4):
                    m = act.activation(sb_e[:, seg[i]:seg[i] + T - i * P], zt(h, i), ACT.Abs)
                m.then_inc(sem["act_order"], 1)
                ordered("act_order", 2 * h + 1)
                act.activation(sb_e[:, :], sb_e[:, :], ACT.Exp, scale=-1.0).then_inc(sem["act_order"], 1)
                ordered("act_order", 2 * h + 2)
                if h:
                    act.wait_ge(sem["sp_soft"], 4 * h)
                act.activation(sb_l[:, :], sb_e[:, :], ACT.Ln, bias=1.0).then_inc(sem["sp_log"], 1)

            def weights_of(h):
                act.wait_ge(sem["sp_decay"], h + 1)
                if h:
                    act.wait_ge(sem["sp_out"], h)
                for i in range(4):
                    act.activation(sb_w[:, seg[i]:seg[i] + T - i * P], zt(h, i), ACT.Exp)\
                        .then_inc(sem["sp_weights"], 1)

            def sb_high(h):
                act.wait_ge(sem["sp_out"], h + 1)
                copy(h_hi[half_of(h), (h // 2) * T:(h // 2 + 1) * T], ps[half_of(h), 6 + h % 2, :])\
                    .then_inc(sem["sp_high"], 1)

            softplus(0)
            for h in range(SB_HEADS):
                if h + 1 < SB_HEADS:
                    softplus(h + 1)
                weights_of(h)
                if h:
                    sb_high(h - 1)
            sb_high(SB_HEADS - 1)

            act.wait_ge(sem["lb_diff"], 1)
            act.activation(dcol(D_OLB, 4), dcol(D_LB, 4), ACT.Sigmoid, scale=-1.0).then_inc(sem["act_order"], 1)
            ordered("act_order", 2 * SB_HEADS + 1)
            act.activation(dcol(D_LB, 4), dcol(D_LB, 4), ACT.Sigmoid).then_inc(sem["lb_ready"], 1)
            act.activation(dcol(D_C, 16), vecs[:, VECS["c"][0]:VECS["c"][0] + 16], ACT.Sigmoid)\
                .then_inc(sem["silu_c"], 1)
            for j in range(4):
                t = a_tile(A["hg_f"] + j)
                act.activation(tile(hg_b, j), t, ACT.Sigmoid).then_inc(sem["hf_sig"], 1)
                act.activation(tile(hg_k, j), t, ACT.Sigmoid, scale=-1.0).then_inc(sem["a_free"], 1)
            for c in range(NC4):
                copy_out(A["hg_i"] + c, tile(hg_v, c))
            for j in range(4):
                act.activation(tile(hg_a, j), d_tile(D["hg_q"] + j), ACT.Sigmoid).then_inc(sem["hf_qs"], 1)
            exp_tables()
            act.wait_ge(sem["hf_f"], 4)
            for j in range(4):
                act.wait_ge(sem["d_free"], D["hg_q"] + j + 1)
                act.activation(tile(hg_a, j), tile(hg_b, j), ACT.Ln).then_inc(sem["hf_log"], 1)
            for lv, m_ in enumerate(HGRN_LEVELS):
                for pr in range(2):
                    act.wait_ge(sem["lv_diff"], 2 * lv + pr + 1)
                    vw = hg_a[:, pr * 2 * T:(pr + 1) * 2 * T].rearrange("p (g s m) -> p g s m", s=2, m=m_)
                    act.activation(vw[:, :, 0, :], vw[:, :, 0, :], ACT.Exp, scale=-1.0)
                    act.activation(vw[:, :, 1, :], vw[:, :, 1, :], ACT.Exp).then_inc(sem["lv_exp"], 1)
            for h in range(HG_HEADS):
                act.wait_ge(sem["off_diff"], h + 1)
                act.activation(tile(hg_a, h), tile(hg_a, h), ACT.Exp)
                if h >= 2:
                    act.wait_ge(sem["ho_ready"], h - 1)
                act.activation(tile(hg_s, h % 2), tile(hg_b, h), ACT.Exp).then_inc(sem["off_exp"], 1)
            for h in range(HG_HEADS):
                act.wait_ge(sem["off_score"], h + 1)
                b = (h % 2) * 2
                copy(hg_off[:, h * 768:h * 768 + T], ps[:, b, :])
                copy(hg_off[:, h * 768 + T:(h + 1) * 768], ps[:, b + 1, 0:2 * P]).then_inc(sem["off_kept"], 1)
            for h in range(HG_HEADS):
                act.wait_ge(sem["ho_out"], h + 1)
                act.activation(tile(hg_b, h), ps[:, 4 + h, :], ACT.Square).then_inc(sem["ho_sq"], 1)
            act.dma_start(hres[:, :], x_t).then_inc(sem["x_loaded"], 16)
            for h in range(HG_HEADS):
                act.wait_ge(sem["ho_total"], h + 1)
                act.activation(tile(hg_a, h), ps[:, h, :], ACT.Ln, bias=EPS, scale=1.0 / P)\
                    .then_inc(sem["ho_log"], 1)
                ordered("ho_log", h + 1)
                act.activation(tile(hg_a, h), tile(hg_a, h), ACT.Exp, scale=-0.5).then_inc(sem["ho_scale"], 1)
            for j in range(4):
                if j >= 2:
                    act.wait_ge(sem["d_free"], D["hg_g"] + j - 1)
                act.activation(tile(hg_s, j % 2), d_tile(D["hg_g"] + j), ACT.Sigmoid).then_inc(sem["hg_sig"], 1)
                act.wait_ge(sem["hg_gate"], j + 1)
                copy(tile(h_hi, 4 + j), tile(hg_k, j)).then_inc(sem["ho_high"], 1)

            for j in range(KT):
                for g, name in enumerate(("gate_a", "gate_b")):
                    n = A["merge"] + 2 * j + g
                    t = a_tile(n)
                    if j == 0:
                        act.wait_ge(sem["ho_low"], HG_HEADS)
                    if j >= 2:
                        act.wait_ge(sem["d_free"], D["merge"] + 2 * (j - 2) + g + 1)
                    act.activation(tile(m_t, (j % 2) * 2 + g), t, ACT.Sigmoid, bias=v(name, j))\
                        .then_inc(sem["a_free"], 1)
                act.wait_ge(sem["mg_sum"], j + 1)
                copy(tile(m_hi, j), tile(m_t, 4)).then_inc(sem["mg_high"], 1)
            exp_tables()

            def feed_forward(name, n_ff, with_ada):
                a0_, d0_ = A[name], D[name]

                def groups(it, last):
                    for j in range(8):
                        if with_ada and j in (3, 5, 7):
                            r = (j + 1) // 2
                            act.wait_ge(sem["ada_used"], it * 7 + r)
                            load_ada(it * 7 + r, r % 2)
                        n = it * 8 + j
                        act.wait_ge(sem["a_full"], n + a0_ + 1)
                        act.wait_ge(sem["f_square"], n + n_ff * 32 + 1)
                        act.activation(tile(f_r, j % 2), ps[:, (a0_ + j) % 4, :], ACT.Relu)\
                            .then_inc(sem["a_free"], 1)
                        act.wait_ge(sem["a_free"], n + a0_ + 1)
                        act.wait_ge(sem["d_full"], it * 8 + d0_)
                        act.activation(tile(h_hi, j), tile(f_r, j % 2), ACT.Square).then_inc(sem["f_high"], 1)
                    if with_ada:
                        for r in (5, 6):
                            act.wait_ge(sem["ada_used"], it * 7 + r)
                            load_ada(it * 7 + r, r % 2)
                        if not last:
                            for r in (1, 0):
                                act.wait_ge(sem["ada_used"], it * 7 + 8 - r)
                                load_ada(it * 7 + 7 + r, r)

                with act.Fori(0, 3) as it:
                    groups(it, False)
                groups(3, True)

            norm("norm2", lambda j: act.wait_ge(sem["d_free"], D["w_out"] + j + 1))
            feed_forward("ff0", 0, True)
            norm("final", lambda j: act.wait_ge(sem["d_free"], D["mla_o"] - 8 + j + 1))
            norm("ctx", lambda j: act.wait_ge(sem["ctx_loaded"], 16))
            for j in range(3):
                copy_out(A["q_a"] + j, tile(cq_raw, j))
            for j in range(3):
                n = A["kv_a"] + 2 * j
                dst = kpe_raw if j == 2 else ck_raw[:, j * TK:(j + 1) * TK]
                copy(dst[:, TC:TK], a_tile(n)).then_inc(sem["a_free"], 1)
                copy(dst[:, 0:TC], a_tile(n + 1)[:, 0:TC]).then_inc(sem["a_free"], 1)
                if j == 0:
                    ordered("a_free", A["kv_a"])
                    norm("cq", lambda j: None)
            ordered("a_free", A["q_b"])
            act.activation(kpe[:, :], kpe_raw[:, :], ACT.Copy, scale=v("k_rope")).then_inc(sem["kpe_scaled"], 1)
            act.activation(kpe_sq[:, :], kpe_raw[:, :], ACT.Square).then_inc(sem["kpe_squared"], 1)
            norm("ck", lambda j: None)
            for b in range(12):
                pr, w_in = b // 3, b % 3
                t = a_tile(A["q_b"] + b)
                if w_in < 2:
                    dst, g = tile(qn, 2 * pr + w_in), "q_nope"
                else:
                    dst, g = tile(q_rp, pr % 2), "q_rope"
                    if pr >= 2:
                        act.wait_ge(sem["qb_rope"], pr - 1)
                act.activation(dst, t, ACT.Copy, scale=v(g)).then_inc(sem["qb_copy"], 1)
                if pr >= 2:
                    act.wait_ge(sem["qb_sums"], pr - 1)
                act.activation(tile(q_sq, (pr % 2) * 3 + w_in), t, ACT.Square).then_inc(sem["a_free"], 1)
            def key_squares(h):
                if h >= 2:
                    act.wait_ge(sem["kb_sum"], h - 1)
                sq = (h % 2) * TK
                for half, (lo_, hi_) in enumerate(((0, T), (T, TK))):
                    t = a_tile(k_tile(h) + half)[:, 0:hi_ - lo_]
                    act.activation(kn[:, h * TK + lo_:h * TK + hi_], t, ACT.Copy, scale=v("k_nope"))\
                        .then_inc(sem["kb_copy"], 1)
                    act.activation(k_sq[:, sq + lo_:sq + hi_], t, ACT.Square).then_inc(sem["a_free"], 1)

            def key_scale(h):
                act.wait_ge(sem["kb_sum"], h + 1)
                if h >= 2:
                    act.wait_ge(sem["kb_norm"], h - 1)
                o = (h % 2) * TK
                act.activation(k_r[:, o:o + T], ps[:, 4, :], ACT.Ln, bias=EPS, scale=1.0 / 192)
                act.activation(k_r[:, o + T:o + TK], ps[:, 7, 0:TC], ACT.Ln, bias=EPS, scale=1.0 / 192)\
                    .then_inc(sem["act_order"], 1)
                ordered("act_order", 2 * SB_HEADS + 1 + h + 1)
                act.activation(k_r[:, o:o + TK], k_r[:, o:o + TK], ACT.Exp, scale=-0.5).then_inc(sem["kb_r"], 1)

            key_squares(0)
            act.wait_ge(sem["qb_sums"], 4)
            act.activation(dcol(D_RQ, 32), ps[:, 6, 0:32], ACT.Ln, bias=EPS, scale=1.0 / 192)\
                .then_inc(sem["rq_log"], 1)
            ordered("rq_log", 1)
            act.activation(dcol(D_RQ, 32), dcol(D_RQ, 32), ACT.Exp, scale=-0.5).then_inc(sem["rq_exp"], 1)
            act.wait_ge(sem["qb_rope"], 4)
            for h in range(MLA_HEADS):
                for i in range(V_FIRST[h], V_FIRST[h] + V_AFTER[h]):
                    cb, c = divmod(i, 6)
                    copy_out(v_tile(i), ml_v[:, c * 1024 + cb * T:c * 1024 + (cb + 1) * T])
                if h + 1 < MLA_HEADS and h != 3:
                    key_squares(h + 1)
                key_scale(h)
                if h == 3:
                    key_squares(4)

            def at_exp(s):
                act.wait_ge(sem["s_max"], s + 1)
                if s >= 2:
                    act.wait_ge(sem["t_full"], 2 * (s - 1))
                elif s == 0:
                    act.wait_ge(sem["kb_norm"], MLA_HEADS)
                b = (s % 3) * 2
                act.activation(tile(at_p, s % 2, TK), ps_pair(b)[:, 0:TK], ACT.Exp,
                               bias=dcol(D_AT + 4 * (s % 2) + 1), scale=dcol(D_RQ + s),
                               accum_out=dcol(D_AT + 4 * (s % 2) + 2)).then_inc(sem["s_exp"], 1)

            def at_copy(s, half):
                h, c = divmod(s, 4)
                if s % 4 == 0 and half == 0 and h >= 2:
                    act.wait_ge(sem["o_full"], h - 1)
                act.wait_ge(sem["t_full"], 2 * s + half + 1)
                o = ((h % 2) * 6 + half * 3) * T
                dst = at_pt[:, o:o + 3 * T].rearrange("p (k t) -> p k t", k=3)
                src = ps[:, 6, 0:3 * P].rearrange("p (k t) -> p k t", k=3)
                copy(dst[:, :, c * P:(c + 1) * P], src).then_inc(sem["t_copied"], 1)

            def o_high_of(h):
                act.wait_ge(sem["o_full"], h + 1)
                copy(tile(o_hi, h), ps[:, 7, :]).then_inc(sem["o_high"], 1)

            at_exp(0)
            for s in range(4 * MLA_HEADS):
                at_copy(s, 0)
                if s + 1 < 4 * MLA_HEADS:
                    at_exp(s + 1)
                at_copy(s, 1)
                if s % 4 == 1 and s > 4:
                    o_high_of(s // 4 - 1)
            o_high_of(MLA_HEADS - 1)
            norm("ffn0", lambda j: act.wait_ge(sem["d_free"], D["mla_o"] + j + 1))
            act.dma_start(wst[:, :], ws_t).then_inc(sem["gm_loaded"], 16)
            act.dma_start(bs_row[0:1, :], bs_in).then_inc(sem["gm_loaded"], 16)
            feed_forward("ff1", 1, False)
            norm("mix1", lambda j: act.wait_ge(sem["d_free"], D["gm_u"] - 8 + j + 1))
            act.preload_act_table(ACT.Gelu)
            for cb in range(4):
                for c in range(NC4):
                    n = A["gm_v"] + cb * 4 + c
                    act.activation(gv[:, c * 2048 + cb * T:c * 2048 + (cb + 1) * T], a_tile(n), ACT.Gelu)\
                        .then_inc(sem["a_free"], 1)
            act.wait_ge(sem["gv_var"], 4)
            exp_tables()
            var = g_st[:, 56:64].rearrange("p (c s) -> p c s", s=2)[:, :, 1]
            act.activation(var, var, ACT.Ln, bias=EPS).then_inc(sem["gv_log"], 1)
            ordered("gv_log", 1)
            act.activation(var, var, ACT.Exp, scale=-0.5).then_inc(sem["gv_rstd"], 1)
            for half in range(2):
                for j in range(8):
                    f = half * 8 + j
                    t = a_tile(A["gm_u"] + f)
                    if f == 0:
                        act.wait_ge(sem["gm_extra"], 16)
                    else:
                        act.wait_ge(sem["gu_mul"], f)
                    act.activation(g_u[:, :], t, ACT.Gelu).then_inc(sem["a_free"], 1)
                    act.wait_ge(sem["gu_mul"], f + 1)
                    act.wait_ge(sem["d_full"], D["gm_u"] + half * 16)
                    copy(tile(h_hi, j), g_s[:, :]).then_inc(sem["gu_high"], 1)
            exp_tables()
            norm("ffn1", lambda j: act.wait_ge(sem["d_free"], D["ff2"] - 8 + j + 1))
            feed_forward("ff2", 2, False)
            for j in range(KT):
                act.wait_ge(sem["d_free"], D["end"] - 8 + j + 1)
                act.dma_start(out[:, j * T:(j + 1) * T], tile(hres, j)).then_inc(sem["stored"], 16)
            act.wait_ge(sem["stored"], 16 * KT)

        @block.vector
        def _(dve):
            class Order:
                n = 0

            def ordered(ins):
                Order.n += 1
                ins.then_inc(sem["dve_order"], 1)
                dve.wait_ge(sem["dve_order"], Order.n)

            def add_square(name, j):
                w_ = norm_spec(name)[1]
                acc = squares_at(name)[1][:, 0:w_]
                dve.wait_ge(sem["n_squared"], NT[name] + j + 1)
                if j > 1:
                    dve.wait_ge(sem["n_added"], NSQ[name] + j - 1)
                dve.tensor_tensor(acc, acc, square_of(name, j), ALU.add).then_inc(sem["n_added"], 1)
                if name == "final":
                    dve.wait_ge(sem["g_squared"], j + 1)
                    if j > 1:
                        dve.wait_ge(sem["g_added"], j - 1)
                    dve.tensor_tensor(g_acc[:, :], g_acc[:, :], tile(g_sq, (j - 1) % 2), ALU.add)\
                        .then_inc(sem["g_added"], 1)

            def norm(name, added=0):
                src, w_, _, gain, shift, dst = norm_spec(name)
                i, k = NI[name], NK[name]
                for j in range(added + 1, k):
                    add_square(name, j)
                dve.wait_ge(sem["n_scale"], i + 1)
                scale = n_r[:, 0:w_]
                if name == "final":
                    dve.tensor_tensor(g_x[:, 0:T], ps[:, 7, :], g_x[:, 0:T], ALU.mult).then_inc(sem["g_sum"], 1)
                    dve.wait_ge(sem["g_scale"], 1)
                    scale = g_x[:, T:2 * T]
                    ordered(dve.tensor_tensor(scale, scale, n_r[:, :][:, 0:T], ALU.mult))

                def scaled(j):
                    if j >= 2:
                        dve.wait_ge(sem["n_high"], NH[name] + j - 1)
                        dve.wait_ge(sem["n_done"], NT[name] + j - 1)
                    dve.scalar_tensor_tensor(norm_t(name, j), src(j), gain(j), scale, ALU.mult, ALU.mult)\
                        .then_inc(sem["n_scaled"], 1)

                scaled(0)
                for j in range(k):
                    if j + 1 < k:
                        scaled(j + 1)
                    dve.wait_ge(sem["n_high"], NH[name] + j + 1)
                    high = dst[0](j).bitcast(F32)
                    if shift is None:
                        m = dve.tensor_tensor(dst[1](j), norm_t(name, j), high, ALU.subtract)
                    else:
                        m = dve.scalar_tensor_tensor(dst[1](j), norm_t(name, j), shift(j), high, ALU.add,
                                                     ALU.subtract)
                    m.then_inc(sem["n_done"], 1)
                if name == "final":
                    for j in range(KT):
                        dve.scalar_tensor_tensor(src(j), src(j), v("final", j), n_r[:, 0:T], ALU.mult, ALU.mult)\
                            .then_inc(sem["final_done"], 1)

            def d_tile(n):
                dve.wait_ge(sem["d_full"], n + 1)
                return ps[:, 4 + n % 2, :]

            dve.memset(ones[:, :], 1.0).then_inc(sem["ones_set"], 1)
            dve.memset(neg_ones[:, :], -1.0).then_inc(sem["ones_set"], 1)
            dve.sem_inc(sem["f_square"], 2)
            dve.sem_inc(sem["ada_used"], 1)
            dve.sem_inc(sem["bank7_free"], 1)
            dve.wait_ge(sem["vecs_loaded"], 16)
            norm("norm1")
            dve.wait_ge(sem["small_loaded"], 32)

            def soft(h):
                dve.wait_ge(sem["sp_log"], h + 1)
                if h >= 2:
                    dve.wait_ge(sem["sp_decay"], h - 1)
                o = (h % 2) * 1280
                for i in range(4):
                    m = dve.scalar_tensor_tensor(sb_sp[:, o + seg[i]:o + seg[i] + T - i * P], zt(h, i), 0.0,
                                                 sb_l[:, seg[i]:seg[i] + T - i * P], ALU.max, ALU.add)
                ordered(m)
                for i in range(4):
                    d = sb_sp[:, o + seg[i]:o + seg[i] + P]
                    dve.tensor_tensor(d, d, cst_a[:, CONSTS["strict"][0]:CONSTS["strict"][0] + P], ALU.mult)\
                        .then_inc(sem["sp_soft"], 1)

            def sb_low(h):
                dve.wait_ge(sem["sp_high"], h + 1)
                c0 = (h // 2) * T
                dve.tensor_tensor(h_lo[half_of(h), c0:c0 + T], ps[half_of(h), 6 + h % 2, :],
                                  h_hi[half_of(h), c0:c0 + T].bitcast(F32), ALU.subtract)\
                    .then_inc(sem["sp_low"], 1)

            soft(0)
            for h in range(SB_HEADS):
                if h + 1 < SB_HEADS:
                    soft(h + 1)
                if h:
                    sb_low(h - 1)
            sb_low(SB_HEADS - 1)

            dve.tensor_tensor(dcol(D_LB, 4), v("lb0", 0, 4), v("lb1", 0, 4), ALU.subtract).then_inc(sem["lb_diff"], 1)
            dve.memset(hg_p[:, :], 0.0).then_inc(sem["hp_zero"], 1)
            dve.wait_ge(sem["lb_ready"], 1)
            dve.wait_ge(sem["silu_c"], 1)
            dve.tensor_tensor(dcol(D_C, 16), dcol(D_C, 16), vecs[:, VECS["c"][0]:VECS["c"][0] + 16], ALU.mult)\
                .then_inc(sem["silu_done"], 1)
            for j in range(4):
                dve.wait_ge(sem["hf_sig"], j + 1)
                dve.tensor_scalar(tile(hg_b, j), tile(hg_b, j), dcol(D_OLB + j), dcol(D_LB + j), ALU.mult,
                                  ALU.add).then_inc(sem["hf_f"], 1)
                dve.wait_ge(sem["a_free"], A["hg_f"] + j + 1)
                dve.tensor_scalar(tile(hg_k, j), tile(hg_k, j), dcol(D_OLB + j), None, ALU.mult)\
                    .then_inc(sem["hf_k"], 1)
            for j in range(4):
                dve.wait_ge(sem["hf_qs"], j + 1)
                dve.tensor_tensor(tile(hg_q, j), d_tile(D["hg_q"] + j), tile(hg_a, j), ALU.mult)\
                    .then_inc(sem["d_free"], 1)
            restart = cst_a[:, CONSTS["restart"][0]:CONSTS["restart"][0] + T]
            for j in range(4):
                dve.wait_ge(sem["hf_log"], j + 1)
                dve.tensor_tensor_scan(tile(hg_b, j), restart, tile(hg_a, j), 0.0, ALU.mult, ALU.add)\
                    .then_inc(sem["hf_b"], 1)

            def keep(lv):
                o = CONSTS["levels"][0] + lv * P
                mask = cst_a[:, o:o + P].bitcast(I32).unsqueeze(1).broadcast_to([P, NC4, P])
                for h in range(HG_HEADS):
                    bank = (lv % 2) * 4 + h
                    dve.wait_ge(sem["lv_score"], lv * 4 + h + 1)
                    if lv:
                        dve.wait_ge(sem["lv_kept"], (lv - 1) * 4 + h + 1)
                    else:
                        dve.wait_ge(sem["hp_zero"], 1)
                    dve.copy_predicated(tile(hg_p, h).rearrange("p (c t) -> p c t", c=NC4), mask,
                                        ps[:, bank, :].rearrange("p (c t) -> p c t", c=NC4))\
                        .then_inc(sem["lv_kept"], 1)

            dve.wait_ge(sem["hf_b"], 4)
            for lv, m_ in enumerate(HGRN_LEVELS):
                view = lambda t, pr: t[:, pr * 2 * T:(pr + 1) * 2 * T].rearrange("p (g s m) -> p g s m", s=2, m=m_)
                for pr in range(2):
                    if lv:
                        dve.wait_ge(sem["lv_score"], lv * 4 + 2 * pr + 2)
                    b = view(hg_b, pr)
                    ref = b[:, :, 0:1, m_ - 1:m_].broadcast_to([P, T // m_, 2, m_])
                    dve.tensor_tensor(view(hg_a, pr), b, ref, ALU.subtract).then_inc(sem["lv_diff"], 1)
                keep(lv)
                for pr in range(2):
                    dve.wait_ge(sem["lv_exp"], 2 * lv + pr + 1)
                    a = view(hg_a, pr)
                    dve.tensor_tensor(a[:, :, 0, :], a[:, :, 0, :], view(hg_k, pr)[:, :, 0, :], ALU.mult)
                    dve.tensor_tensor(a[:, :, 1, :], a[:, :, 1, :], view(hg_q, pr)[:, :, 1, :], ALU.mult)\
                        .then_inc(sem["lv_pair"], 1)
            dve.wait_ge(sem["lv_score"], 4 * 8)
            for h in range(HG_HEADS):
                b = tile(hg_b, h).rearrange("p (c t) -> p c t", c=NC4)
                dve.tensor_tensor(tile(hg_a, h).rearrange("p (c t) -> p c t", c=NC4),
                                  b[:, :, P - 1:P].broadcast_to([P, NC4, P]), b, ALU.subtract)\
                    .then_inc(sem["off_diff"], 1)
            for h in range(HG_HEADS):
                dve.wait_ge(sem["off_exp"], h + 1)
                k, q, ep = tile(hg_k, h), tile(hg_q, h), tile(hg_s, h % 2)
                dve.tensor_tensor(k, k, tile(hg_a, h), ALU.mult)
                ordered(dve.tensor_tensor(q, q, ep, ALU.mult))
                dve.tensor_scalar(hg_edge[:, h * P:(h + 1) * P], k[:, 0:P], ep[:, 2 * P - 1:2 * P], None, ALU.mult)
                dve.tensor_scalar(hg_edge[:, (4 + h) * P:(5 + h) * P], q[:, 3 * P:T], ep[:, 3 * P - 1:3 * P],
                                  None, ALU.mult).then_inc(sem["ho_ready"], 1)
            keep(len(HGRN_LEVELS))
            for h in range(HG_HEADS):
                dve.wait_ge(sem["ho_scale"], h + 1)
                dve.scalar_tensor_tensor(tile(hg_p, h), ps[:, 4 + h, :], v("hg_norm", h), tile(hg_a, h),
                                         ALU.mult, ALU.mult).then_inc(sem["ho_norm"], 1)
            for j in range(4):
                dve.wait_ge(sem["hg_sig"], j + 1)
                dve.tensor_tensor(tile(hg_q, j), d_tile(D["hg_g"] + j), tile(hg_s, j % 2), ALU.mult)\
                    .then_inc(sem["d_free"], 1)
                dve.wait_ge(sem["d_free"], D["hg_g"] + j + 1)
                dve.tensor_tensor(tile(hg_k, j), tile(hg_p, j), tile(hg_q, j), ALU.mult).then_inc(sem["hg_gate"], 1)
                dve.wait_ge(sem["ho_high"], j + 1)
                dve.tensor_tensor(tile(h_lo, 4 + j), tile(hg_k, j), tile(h_hi, 4 + j).bitcast(F32), ALU.subtract)\
                    .then_inc(sem["ho_low"], 1)

            for j in range(KT):
                for g in range(2):
                    n = 2 * j + g
                    dve.wait_ge(sem["a_free"], A["merge"] + n + 1)
                    if g == 0 and j:
                        dve.wait_ge(sem["mg_high"], j)
                        dve.wait_ge(sem["mg_low"], j)
                    dve.tensor_tensor(tile(m_t, 4 + g), d_tile(D["merge"] + n), tile(m_t, (j % 2) * 2 + g), ALU.mult)\
                        .then_inc(sem["d_free"], 1)
                dve.wait_ge(sem["d_free"], D["merge"] + 2 * j + 2)
                dve.tensor_tensor(tile(m_t, 4), tile(m_t, 4), tile(m_t, 5), ALU.add).then_inc(sem["mg_sum"], 1)
                dve.wait_ge(sem["mg_high"], j + 1)
                dve.tensor_tensor(tile(m_lo, j), tile(m_t, 4), tile(m_hi, j).bitcast(F32), ALU.subtract)\
                    .then_inc(sem["mg_low"], 1)

            def add_out(n, j, gate, bank=None):
                dve.wait_ge(sem["d_full"], n + 1)
                src = ps[:, bank if bank is not None else 4 + n % 2, :]
                dve.scalar_tensor_tensor(tile(hres, j), src, gate, tile(hres, j), ALU.mult, ALU.add)\
                    .then_inc(sem["d_free"], 1)

            dve.wait_ge(sem["x_loaded"], 16)
            for j in range(KT):
                add_out(D["w_out"] + j, j, 1.0)
                if j >= 2:
                    add_square("norm2", j - 1)
            norm("norm2", KT - 2)

            def feed_forward(name, n_ff, gate, with_ada, next_norm):
                a0_, d0_ = A[name], D[name]

                def groups(it, last):
                    def ada_part(slot_no):
                        if not with_ada or not 1 <= slot_no <= 14:
                            return
                        r, part = divmod(slot_no - 1, 2)
                        cvec = D_CC if r == 6 else D_C
                        acc = tile(ada_acc, r)
                        if part == 0:
                            dve.wait_ge(sem["ada_in%d" % (r % 2)], it * (64 if r % 2 == 0 else 48) + 16 * (r // 2) + 16)
                            if r == 0:
                                dve.wait_ge(sem["bank7_free"], it + 1)
                        for k in range(4 * part, 4 * part + 4):
                            wk = ada_w[:, (r % 2) * 4096 + k * T:(r % 2) * 4096 + (k + 1) * T]
                            if k == 0:
                                m = dve.tensor_scalar(acc, wk, dcol(cvec + k), None, ALU.mult)
                            else:
                                dve.wait_ge(sem["ada_step"], it * 56 + r * 8 + k)
                                m = dve.scalar_tensor_tensor(acc, wk, dcol(cvec + k), acc, ALU.mult, ALU.add)
                            m.then_inc(sem["ada_step"], 1)
                        if part == 1:
                            dve.wait_ge(sem["ada_step"], it * 56 + r * 8 + 8)
                            dve.sem_inc(sem["ada_used"], 1)

                    for j in range(8):
                        n = it * 8 + j
                        dve.wait_ge(sem["a_free"], n + a0_ + 1)
                        dve.tensor_tensor(tile(f_s, j % 2), tile(f_r, j % 2), tile(f_r, j % 2), ALU.mult)\
                            .then_inc(sem["f_square"], 1)
                        dve.wait_ge(sem["f_square"], n + n_ff * 32 + 3)
                        dve.wait_ge(sem["f_high"], n + n_ff * 32 + 1)
                        dve.tensor_tensor(tile(h_lo, j), tile(f_s, j % 2), tile(h_hi, j).bitcast(F32), ALU.subtract)\
                            .then_inc(sem["f_low"], 1)
                        ada_part(j)
                    for j in range(8):
                        dve.wait_ge(sem["d_full"], it * 8 + d0_ + j + 1)
                        dve.scalar_tensor_tensor(tile(hres, j), ps[:, 4 + (d0_ + j) % 2, :], gate(j), tile(hres, j),
                                                 ALU.mult, ALU.add).then_inc(sem["d_free"], 1)
                        ada_part(8 + j)
                        if last and next_norm is not None and j >= 2:
                            add_square(next_norm, j - 1)
                    if with_ada:
                        dve.wait_ge(sem["ada_cols"], it + 1)
                        dve.tensor_copy(mods[:, bass.ds(it * 28, 28)], ps[:, 7, 0:28]).then_inc(sem["bank7_free"], 1)

                with dve.Fori(0, 3) as it:
                    groups(it, False)
                groups(3, True)

            dve.wait_ge(sem["silu_done"], 1)
            feed_forward("ff0", 0, lambda j: 1.0, True, "final")
            dve.wait_ge(sem["bank7_free"], 5)
            ordered(dve.tensor_tensor(mods[:, :], mods[:, :], v("ada_b", 0, 4 * ADA_CHUNKS), ALU.add))
            for n, (name, cols) in enumerate((("mix0", lambda j: mod_col(0, 1, j)), ("mix0", lambda j: ctx_col(1, j)),
                                              ("ffn0", lambda j: mod_col(0, 4, j)), ("mix1", lambda j: mod_col(1, 1, j)),
                                              ("ffn1", lambda j: mod_col(1, 4, j)))):
                for j in (0, 4):
                    m = dve.scalar_tensor_tensor(dcol(D_GAIN + 8 * n + j, 4), mods[:, cols(j):cols(j) + 4], 1.0,
                                                 v(name, j, 4), ALU.add, ALU.mult)
            ordered(m)
            dve.tensor_tensor(dcol(D_GAIN, 8), dcol(D_GAIN, 8), v("final", 0, 8), ALU.mult)\
                .then_inc(sem["mod_ready"], 1)
            dve.wait_ge(sem["mod_ready"], 1)
            norm("final", KT - 2)
            norm("ctx")
            norm("cq")
            cos = cst_b[:, P:P + T]
            sin = cst_b[:, P + T:P + 2 * T]
            dve.wait_ge(sem["kpe_rot"], 1)
            dve.tensor_tensor(q_tmp[:, :], ps[:, 4, :], sin, ALU.mult)
            ordered(dve.tensor_tensor(kpe[:, TC:TK], kpe[:, TC:TK], cos, ALU.mult))
            dve.tensor_tensor(kpe[:, TC:TK], kpe[:, TC:TK], q_tmp[:, :], ALU.add).then_inc(sem["kpe_done"], 1)
            norm("ck")
            for pr in range(4):
                dve.wait_ge(sem["qb_rot"], pr + 1)
                if pr:
                    dve.wait_ge(sem["qb_rope"], pr)
                dve.tensor_tensor(q_tmp[:, :], ps[:, 5, :], sin, ALU.mult)
                ordered(dve.tensor_tensor(tile(qr, pr), tile(q_rp, pr % 2), cos, ALU.mult))
                dve.tensor_tensor(tile(qr, pr), tile(qr, pr), q_tmp[:, :], ALU.add).then_inc(sem["qb_rope"], 1)
            for h in range(MLA_HEADS):
                hp, pair = half_of(h), h // 2
                krt, kro = (kr_a, pair * TK) if pair < 2 else (kr_b, (pair - 2) * TK)
                dve.wait_ge(sem["kb_r"], h + 1)
                o = (h % 2) * TK
                dve.tensor_tensor(kn[:, h * TK:(h + 1) * TK], kn[:, h * TK:(h + 1) * TK], k_r[:, o:o + TK], ALU.mult)
                dve.tensor_tensor(krt[hp, kro:kro + TK], kpe[hp, :], k_r[hp, o:o + TK], ALU.mult)\
                    .then_inc(sem["kb_norm"], 1)
            dve.wait_ge(sem["rq_exp"], 1)
            dve.tensor_scalar(dcol(D_RQ, 32), dcol(D_RQ, 32), 192.0 ** -0.5, None, ALU.mult)\
                .then_inc(sem["rq_ready"], 1)
            dve.wait_ge(sem["rq_ready"], 1)

            def at_max(s):
                b = (s % 3) * 2
                o = D_AT + 4 * (s % 2)
                dve.wait_ge(sem["s_full"], s + 1)
                if s >= 2:
                    dve.wait_ge(sem["p_norm"], s - 1)
                ordered(dve.tensor_reduce(dcol(o), ps_pair(b)[:, 0:TK], AX_X, ALU.max))
                dve.tensor_scalar(dcol(o + 1), dcol(o), dcol(D_RQ + s), -1.0, ALU.mult, ALU.mult)\
                    .then_inc(sem["s_max"], 1)

            def at_norm(s):
                o = D_AT + 4 * (s % 2)
                dve.wait_ge(sem["s_exp"], s + 1)
                ordered(dve.reciprocal(dcol(o + 3), dcol(o + 2)))
                p = tile(at_p, s % 2, TK)
                dve.tensor_scalar(p, p, dcol(o + 3), None, ALU.mult).then_inc(sem["p_norm"], 1)

            def o_low_of(h):
                dve.wait_ge(sem["o_high"], h + 1)
                dve.tensor_tensor(tile(o_lo, h), ps[:, 7, :], tile(o_hi, h).bitcast(F32), ALU.subtract)\
                    .then_inc(sem["o_low"], 1)

            at_max(0)
            at_norm(0)
            at_max(1)
            for s in range(4 * MLA_HEADS):
                if s + 1 < 4 * MLA_HEADS:
                    at_norm(s + 1)
                if s + 2 < 4 * MLA_HEADS:
                    at_max(s + 2)
                if s % 4 == 1 and s > 4:
                    o_low_of(s // 4 - 1)
            o_low_of(MLA_HEADS - 1)
            for j in range(KT):
                add_out(D["mla_o"] + j, j, mcol(mod_col(0, 2, j)))
                if j >= 2:
                    add_square("ffn0", j - 1)
            norm("ffn0", KT - 2)
            feed_forward("ff1", 1, lambda j: mcol(mod_col(0, 5, j)), False, "mix1")

            norm("mix1", KT - 2)
            for i in range(4):
                dve.wait_ge(sem["gm_rows"], i + 1)
                dst = (rs_b if i < 2 else bs_b)[:, (i % 2) * T:(i % 2 + 1) * T]
                dve.tensor_copy(dst, ps[:, 4 + i, :]).then_inc(sem["gm_copy"], 1)
            dve.wait_ge(sem["gm_copy"], 4)
            for f in range(16):
                g = f // 2
                dve.scalar_tensor_tensor(extra[:, f * P:(f + 1) * P], rs_b[:, g * P:(g + 1) * P], v("ln_b", f),
                                         bs_b[:, g * P:(g + 1) * P], ALU.mult, ALU.add)\
                    .then_inc(sem["gm_extra"], 1)
            dve.wait_ge(sem["a_free"], A["gm_u"])
            for c in range(NC4):
                for q in range(4):
                    m = dve.bn_stats(g_st[:, (c % 2) * 24 + q * 6:(c % 2) * 24 + q * 6 + 6],
                                     gv[:, c * 2048 + q * T:c * 2048 + (q + 1) * T])
                ordered(m)
                dve.bn_aggr(g_st[:, 56 + 2 * c:58 + 2 * c], g_st[:, (c % 2) * 24:(c % 2) * 24 + 24])\
                    .then_inc(sem["gv_var"], 1)
                if c < 3:
                    dve.wait_ge(sem["gv_var"], c + 1)
            dve.wait_ge(sem["gv_rstd"], 1)
            for c in range(NC4):
                g = gv[:, c * 2048:(c + 1) * 2048]
                dve.tensor_scalar(g, g, g_st[:, 56 + 2 * c:57 + 2 * c], g_st[:, 57 + 2 * c:58 + 2 * c],
                                  ALU.subtract, ALU.mult).then_inc(sem["gv_norm"], 1)
            for half in range(2):
                for j in range(8):
                    f = half * 8 + j
                    n = D["gm_u"] + half * 16 + j
                    dve.wait_ge(sem["d_full"], n + 1)
                    ex = extra[:, f * P:(f + 1) * P].unsqueeze(1).broadcast_to([P, NC4, P])
                    src = ps[:, 4 + n % 2, :].rearrange("p (c t) -> p c t", c=NC4)
                    if f:
                        dve.wait_ge(sem["gu_mul"], f)
                    dve.scalar_tensor_tensor(g_t[:, :].rearrange("p (c t) -> p c t", c=NC4), src, v("ln_g", f), ex,
                                             ALU.mult, ALU.add).then_inc(sem["d_free"], 1)
                    dve.wait_ge(sem["d_free"], n + 1)
                    dve.wait_ge(sem["a_free"], A["gm_u"] + f + 1)
                    if f:
                        dve.wait_ge(sem["gu_high"], f)
                        dve.wait_ge(sem["gu_low"], f)
                    dve.tensor_tensor(g_s[:, :], g_t[:, :], g_u[:, :], ALU.mult).then_inc(sem["gu_mul"], 1)
                    dve.wait_ge(sem["gu_high"], f + 1)
                    dve.tensor_tensor(tile(h_lo, j), g_s[:, :], tile(h_hi, j).bitcast(F32), ALU.subtract)\
                        .then_inc(sem["gu_low"], 1)
                for j in range(8):
                    add_out(D["gm_u"] + half * 16 + 8 + j, j, mcol(mod_col(1, 2, j)))
                    if half and j >= 2:
                        add_square("ffn1", j - 1)
            norm("ffn1", KT - 2)
            feed_forward("ff2", 2, lambda j: mcol(mod_col(1, 5, j)), False, None)


def _units(w, k_tiles, m_tiles):
    t = w.reshape(k_tiles, P, m_tiles, P).transpose(2, 0, 1, 3).reshape(k_tiles * m_tiles, P, P)
    return _pack(t)


def _pack(tiles):
    import numpy as np
    n = tiles.shape[0]
    if n % 8:
        tiles = np.concatenate([tiles, np.zeros((8 - n % 8, P, P), tiles.dtype)])
    return tiles.reshape(-1, 8, P, P).transpose(0, 2, 1, 3).reshape(-1, P, UNIT)


def _moving(w, k_tiles):
    n = w.shape[1] // T
    return w.reshape(k_tiles // 2, 2, P, n, T).transpose(3, 0, 2, 1, 4).reshape(-1, P, UNIT)


def _half_first(w1, w2, up_cols=8):
    import numpy as np
    parts = []
    for g in range(w2.shape[0] // (8 * P)):
        s = slice(g * 8 * P, (g + 1) * 8 * P)
        parts += [_units(w1[:, s], 8, 8), _units(w2[s, :], 8, 8)]
    return np.concatenate(parts)


def _stream(i):
    import numpy as np
    a = {k: np.asarray(x) for k, x in i.items()}
    w = a["w_in"][0]
    cut = lambda o, n: w[:, o:o + n]
    parts = [_units(cut(0, 512), 8, 4), _units(cut(512, 512), 8, 4), _moving(cut(1024, 512), 8),
             _units(cut(1536, 512), 8, 4), _moving(cut(2048, 512), 8), _units(cut(2560, 512), 8, 4),
             _units(cut(3072, 512), 8, 4)]
    ga, gb = _units(cut(3584, 1024), 8, 8), _units(cut(4608, 1024), 8, 8)
    both = np.concatenate([a["w_o_sb"][0], a["w_o_hg"][0]])
    o = _units(both, 8, 8)
    parts.append(np.stack([ga, gb, o], 1).reshape(24, P, UNIT))
    parts.append(_units(a["w_out"][0], 8, 8))
    parts.append(_half_first(a["w_ff1"][0], a["w_ff2"][0]))
    parts.append(_units(a["mla_wq_a_2"][0], 8, 3))
    kva = a["mla_wkv_a_2"][0]
    parts.append(_units(np.concatenate([kva, kva[:, 256:320]], 1), 8, 3))
    qb = a["mla_wq_b_2"][0].reshape(384, MLA_HEADS, 192)
    blocks = []
    for pr in range(4):
        blocks += [qb[:, 2 * pr, 0:128], qb[:, 2 * pr + 1, 0:128],
                   np.concatenate([qb[:, 2 * pr, 128:192], qb[:, 2 * pr + 1, 128:192]], 1)]
    parts.append(_units(np.concatenate(blocks, 1), 3, 12))
    kvb = a["mla_wkv_b_2"][0].reshape(256, MLA_HEADS, 256)
    parts.append(_units(np.ascontiguousarray(kvb[:, :, 0:128]).reshape(256, 1024), 2, 8))
    parts.append(_moving(np.ascontiguousarray(kvb[:, :, 128:256]).reshape(256, 1024), 2))
    parts.append(_units(a["mla_wo_2"][0], 8, 8))
    parts.append(_half_first(a["ffn_w1_2"][0], a["ffn_w2_2"][0]))
    gi = a["gm_w_in_2"][0]
    parts.append(_moving(gi[:, 2048:4096], 8))
    parts.append(_half_first(gi[:, 0:2048], a["gm_w_out_2"][0]))
    parts.append(_half_first(a["ffn_w1_2"][1], a["ffn_w2_2"][1]))
    s = np.concatenate(parts)
    assert s.shape[0] == N_UNITS, s.shape
    if N_UNITS % 2:
        s = np.concatenate([s, np.zeros((1, P, UNIT), s.dtype)])
    return np.ascontiguousarray(s.reshape(-1, 2, P, UNIT).transpose(0, 2, 1, 3)).reshape(-1, P, 2 * UNIT)


def _cols(x):
    import numpy as np
    return np.asarray(x).reshape(-1, P).T


def _ada(i):
    import numpy as np
    w, b = np.asarray(i["ada_w_2"]), np.asarray(i["ada_b_2"])
    chunks, bias = [], []
    for it in range(4):
        layer = it // 2
        todo = [(layer, (it % 2) * 6 + r) for r in range(6)] + [(0, it)]
        for l, c in todo:
            chunks.append(w[l][:, c * T:(c + 1) * T].reshape(KT, P, T).transpose(1, 0, 2).reshape(P, KT * T))
            bias.append(_cols(b[l][c * T:(c + 1) * T]))
    return np.stack(chunks), np.concatenate(bias, 1)


def _vectors(i, ada_bias):
    import numpy as np
    a = {k: np.asarray(x) for k, x in i.items()}
    twice = lambda x: np.concatenate([x, x])
    got = {
        "norm1": a["norm1_g"][0], "gate_a": a["b_gate"][0][:1024], "gate_b": a["b_gate"][0][1024:],
        "lb0": a["lb_logits"][0], "lb1": a["lb_logits"][1], "hg_norm": a["hg_norm_g"][0],
        "norm2": a["norm2_g"][0], "final": a["final_g"], "mix0": a["norm_mix_g_2"][0],
        "ffn0": a["norm_ffn_g_2"][0], "mix1": a["norm_mix_g_2"][1], "ffn1": a["norm_ffn_g_2"][1],
        "q_a_norm": a["mla_q_a_norm_2"][0], "kv_a_norm": a["mla_kv_a_norm_2"][0],
        "q_nope": a["mla_q_norm_2"][0][:128], "q_rope": twice(a["mla_q_norm_2"][0][128:]),
        "k_nope": a["mla_k_norm_2"][0][:128], "k_rope": twice(a["mla_k_norm_2"][0][128:]),
        "ln_g": a["gm_ln_g_2"][0], "ln_b": a["gm_ln_b_2"][0], "c": a["c_2"][0], "c_ctx": a["c_ctx_2"],
    }
    cols = [ada_bias if n == "ada_b" else _cols(got[n]) for n in VECS]
    return np.ascontiguousarray(np.concatenate(cols, 1))


def _constants():
    import numpy as np
    s, t = np.arange(P)[:, None], np.arange(P)[None, :]
    f = lambda x: x.astype(np.float32)
    levels = [f(s == t)]
    for m in HGRN_LEVELS:
        same = s // (2 * m) == t // (2 * m)
        levels.append(f(same & (s // m % 2 == 0) & (t // m % 2 == 1)))
    restart = np.ones((P, T), np.float32)
    restart[:, ::P] = 0
    a = np.concatenate([-f(s >= t), f(s >= t) * np.float32(-1e30), f(s < t)] + levels + [restart], 1)
    rot = np.zeros((P, P), np.float32)
    for base in (0, 64):
        for half in (0, 32):
            for j in range(16):
                o = base + half + j
                rot[o + 16, o] = -1
                rot[o, o + 16] = 1
    rows = T // 64
    row = np.repeat(np.arange(rows, dtype=np.float32), 64)
    col = np.tile(np.arange(64, dtype=np.float32), rows)
    inv = np.float32(10000.0) ** (-np.arange(0, 32, 2, dtype=np.float32) / np.float32(32))
    ar, ac = row[:, None] * inv[None, :], col[:, None] * inv[None, :]
    ang = np.concatenate([ar, ar, ac, ac], -1)
    ang = np.concatenate([ang, ang], -1).T
    half = np.stack([np.arange(P) < 64, np.arange(P) >= 64], 1)
    b = np.concatenate([rot, np.cos(ang), np.sin(ang), half], 1).astype(np.float32)
    return np.ascontiguousarray(a), np.ascontiguousarray(b), np.eye(P, dtype=np.float32)


def _arrays(inputs):
    import numpy as np
    ada, ada_bias = _ada(inputs)
    ca, cb, ident = _constants()
    fm = lambda x, n: np.ascontiguousarray(np.asarray(x)[0].T.reshape(KT, P, n).transpose(1, 0, 2)).reshape(P, KT * n)
    ws = np.asarray(inputs["gm_ws_2"])[0]
    return {
        "weights": _stream(inputs), "ada": ada, "x_t": fm(inputs["x"], T), "ctx_t": fm(inputs["ctx_2"], TC),
        "vecs_in": _vectors(inputs, ada_bias), "const_a": ca, "const_b": cb, "ident_in": ident,
        "ws_t": np.ascontiguousarray(ws.transpose(2, 0, 1)).reshape(P, KT * P),
        "bs_in": np.ascontiguousarray(np.asarray(inputs["gm_bs_2"])[0]).reshape(1, KT * P),
    }


def kernel(**inputs):
    import numpy as np
    import concourse.bacc as bacc
    from concourse.bass_utils import run_bass_kernel_spmd

    nc = bacc.Bacc("TRN2", target_bir_lowering=False, num_devices=1)
    arrays = _arrays(inputs)
    aps = {n: nc.dram_tensor(n, a.shape, mybir.dt.from_np(a.dtype), kind="ExternalInput").ap()
           for n, a in arrays.items()}
    out = nc.dram_tensor("out", (P, KT * T), F32, kind="ExternalOutput").ap()
    build_program(nc, out=out, **aps)
    r = run_bass_kernel_spmd(nc, [arrays], core_ids=[0])
    got = np.asarray(r.results[0]["out"]).reshape(P, KT, T)
    return np.ascontiguousarray(got.transpose(2, 1, 0)).reshape(1, T, D_MODEL)
```

```python
from contextlib import ExitStack

import concourse.bass as bass
from concourse import mybir

P = 128
T = 512
TC = 256
TK = T + TC
KT = 8
NC4 = T // P
SB_HEADS = 8
HG_HEADS = 4
MLA_HEADS = 8
EPS = 1e-6
D_MODEL = 1024
UNIT = 1024
W_SLOTS = 4
RAW_SLOTS = 4
CHUNK_UNITS = 2
HGRN_LEVELS = (64, 32, 16, 8, 4, 2, 1)
ADA_CHUNKS = 28
ADA_PER_IT = 7

F32 = mybir.dt.float32
F32R = mybir.dt.float32r
I32 = mybir.dt.int32
ALU = mybir.AluOpType
ACT = mybir.ActivationFunctionType

STREAM = [
    ("sb_q", 4), ("sb_k", 4), ("sb_v", 4), ("hg_f", 4), ("hg_q", 4), ("hg_i", 4), ("hg_g", 4),
    ("merge", 24), ("w_out", 8), ("ff0", 64),
    ("q_a", 3), ("kv_a", 3), ("q_b", 5), ("k_b", 2), ("v_b", 2), ("mla_o", 8), ("ff1", 64),
    ("gm_v", 16), ("gm_u", 32), ("ff2", 64),
]
N_UNITS = sum(n for _, n in STREAM)
FIRST = {}
_at = 0
for _name, _n in STREAM:
    FIRST[_name] = _at
    _at += _n

VECS = {}
_at = 0
for _name, _n in [
    ("norm1", 8), ("gate_a", 8), ("gate_b", 8), ("lb0", 4), ("lb1", 4), ("hg_norm", 4), ("norm2", 8),
    ("final", 8), ("mix0", 8), ("ffn0", 8), ("mix1", 8), ("ffn1", 8), ("q_a_norm", 3),
    ("kv_a_norm", 2), ("q_nope", 1), ("q_rope", 1), ("k_nope", 1), ("k_rope", 1), ("ln_g", 16),
    ("ln_b", 16), ("ada_b", 4 * ADA_CHUNKS), ("c", 8), ("c_ctx", 8),
]:
    VECS[_name] = (_at, _n)
    _at += _n
N_VECS = _at

CONSTS = {}
_at = 0
for _name, _n in [("neg_tri", P), ("big_neg", P), ("strict", P), ("levels", 8 * P), ("restart", T)]:
    CONSTS[_name] = (_at, _n)
    _at += _n
N_CONST_A = _at
_at = 0
for _name, _n in [("rot", P), ("cos", T), ("sin", T)]:
    CONSTS[_name] = (_at, _n)
    _at += _n
N_CONST_B = _at


def build_program(nc, weights, ada, x_t, ctx_t, vecs_in, const_a, const_b, ident_in, fold_in, ws_t, bs_in, out):
    ctx = ExitStack()
    with ctx:
        KB = 1024
        a0 = (nc.sbuf_base + 31) // 32 * 32

        def at(name, off, cols, dt=F32):
            return nc.alloc_sbuf_tensor_at(name, [P, cols], dt, offset=a0 + off)

        raw = at("raw", 0, RAW_SLOTS * 2 * UNIT)
        w_hi = at("w_hi", 32 * KB, W_SLOTS * UNIT, F32R)
        w_lo = at("w_lo", 48 * KB, W_SLOTS * UNIT, F32R)
        XH0, HH0, HL0, H0 = 64 * KB, 96 * KB, 112 * KB, 128 * KB
        M0 = 144 * KB
        x_hi = at("x_hi", XH0, KT * T, F32R)
        x_lo = at("x_lo", XH0 + 16 * KB, KT * T, F32R)
        h_hi = at("h_hi", HH0, KT * T, F32R)
        h_lo = at("h_lo", HL0, KT * T, F32R)
        hres = at("hres", H0, KT * T)
        n_sq = at("n_sq", M0 + 54 * KB, 2 * T)
        n_acc = at("n_acc", M0 + 58 * KB, T)
        l_sq = at("l_sq", HL0, 2 * TK)
        l_acc = at("l_acc", HL0 + 6 * KB, TK)
        g_sq = at("g_sq", M0 + 46 * KB, 2 * T)
        g_acc = at("g_acc", M0 + 50 * KB, T)
        g_r = at("g_r", M0 + 29 * KB, T)
        n_r = at("n_r", HL0 + 9 * KB, TK)
        n_t = at("n_t", HL0 + 12 * KB, 2 * T)
        S0 = M0 + 60 * KB
        ones = at("ones", S0, P)
        ident = at("ident", S0 + 512, P)
        neg_ones = at("neg_ones", S0 + 1024, P)
        fold = at("fold", S0 + 1024, P)
        vecs = at("vecs", S0 + 1536, N_VECS)
        mods = at("mods", S0 + 1536 + 4 * N_VECS + 12, 4 * ADA_CHUNKS)
        derived = at("derived", S0 + 1536 + 4 * N_VECS + 12 + 448, 120)

        cst_a = at("cst_a", M0, N_CONST_A)
        sb_q = at("sb_q", M0 + 8 * KB, 4 * T)
        sb_k = at("sb_k", M0 + 16 * KB, 4 * T)
        sb_v = at("sb_v", M0 + 24 * KB, 4 * T)
        sb_e = at("sb_e", M0 + 32 * KB, 1280)
        sb_l = at("sb_l", M0 + 37 * KB, 1280)
        sp_hi = at("sp_hi", M0 + 42 * KB, 2 * 1280, F32R)
        sp_lo = at("sp_lo", H0, 2 * 1280, F32R)
        sb_sp = at("sb_sp", H0 + 10 * KB, 1280)
        sb_m = at("sb_m", M0 + 57 * KB, 4 * P, F32R)
        sb_w = at("sb_w", M0 + 52 * KB, 1280)
        hg_b = at("hg_b", M0 + 8 * KB, 4 * T)
        hg_k = at("hg_k", M0 + 16 * KB, 4 * T)
        hg_q = at("hg_q", M0 + 24 * KB, 4 * T)
        hg_v = at("hg_v", M0 + 32 * KB, 4 * T)
        hg_a = at("hg_a", M0 + 40 * KB, 4 * T)
        hg_a2 = at("hg_a2", HL0 + 8 * KB, 4 * T)
        hg_raw = at("hg_raw", HH0 + 8 * KB, 4 * T)
        hf_in = at("hf_in", HL0 + 8 * KB, 4 * T)
        hg_p = at("hg_p", M0 + 48 * KB, 4 * T)
        hg_s = at("hg_s", M0 + 56 * KB, 2 * T)
        hg_off = at("hg_off", H0, 4 * 6 * P)
        hg_edge = at("hg_edge", H0 + 12 * KB, 2 * 4 * P)
        m_hi = at("m_hi", M0, KT * T, F32R)
        m_lo = at("m_lo", M0 + 16 * KB, KT * T, F32R)
        m_t = at("m_t", M0 + 32 * KB, 6 * T)
        ada_w = at("ada_w", M0, 2 * 4096)
        ada_acc = at("ada_acc", M0 + 32 * KB, 2 * T)
        ada_x = at("ada_x", M0 + 36 * KB, ADA_PER_IT * 16)
        f_r = at("f_r", M0 + 46 * KB, 2 * T)
        f_s = at("f_s", M0 + 50 * KB, 2 * T)
        cst_b = at("cst_b", M0, N_CONST_B)
        cq_hi = at("cq_hi", M0 + 5 * KB, 3 * T, F32R)
        cq_lo = at("cq_lo", M0 + 11 * KB, 3 * T, F32R)
        ck_hi = at("ck_hi", M0 + 17 * KB, 2 * TK, F32R)
        ck_lo = at("ck_lo", M0 + 23 * KB, 2 * TK, F32R)
        kpe = at("kpe", M0 + 29 * KB, TK)
        ml_v = at("ml_v", M0 + 36 * KB, 6 * 1024)
        ctxx = at("ctxx", M0 + 36 * KB, KT * TC)
        cq_raw = at("cq_raw", M0 + 44 * KB, 3 * T)
        ck_raw = at("ck_raw", M0 + 50 * KB, 2 * TK)
        kpe_raw = at("kpe_raw", M0 + 56 * KB, TK)
        kpe_sq = at("kpe_sq", M0 + 32 * KB, TK)
        q_sq = at("q_sq", M0 + 36 * KB, 6 * T)
        q_rp = at("q_rp", M0 + 48 * KB, 2 * T)
        k_sq = at("k_sq", M0 + 5 * KB, 2 * TK)
        k_r = at("k_r", M0 + 11 * KB, 2 * TK)
        q_tmp = at("q_tmp", XH0 + 30 * KB, T)
        c_hi = at("c_hi", HH0, KT * TC, F32R)
        c_lo = at("c_lo", HH0 + 8 * KB, KT * TC, F32R)
        qn = at("qn", XH0, MLA_HEADS * T)
        qr = at("qr", XH0 + 16 * KB, 4 * T)
        kr_a = at("kr_a", XH0 + 24 * KB, 2 * TK)
        kn = at("kn", HH0, MLA_HEADS * TK)
        kr_b = at("kr_b", HH0 + 24 * KB, 2 * TK)
        at_p = at("at_p", M0, 2 * TK)
        at_pt = at("at_pt", M0 + 6 * KB, 12 * T)
        o_hi = at("o_hi", XH0, KT * T, F32R)
        o_lo = at("o_lo", HH0, KT * T, F32R)
        gv = at("gv", M0, 4 * 2048)
        wst = at("wst", M0 + 32 * KB, KT * P)
        rs_b = at("rs_b", M0 + 36 * KB, KT * P)
        bs_b = at("bs_b", M0 + 40 * KB, KT * P)
        extra = at("extra", M0 + 44 * KB, 16 * P)
        g_u = at("g_u", M0 + 52 * KB, T)
        g_t = at("g_t", M0 + 54 * KB, T)
        g_s = at("g_s", M0 + 56 * KB, T)
        g_st = at("g_st", M0 + 58 * KB, 104)
        bs_row = at("bs_row", M0, KT * P)

        ps = ctx.enter_context(nc.psum_tensor("ps", [P, 8, T], F32))

        names = (
            ["raw_in%d" % i for i in range(RAW_SLOTS)] + ["x_in%d" % i for i in range(4)]
            + ["split_turn", "w_high", "w_ready", "unit_started", "a_full", "a_free", "d_full", "d_free"]
            + ["x_loaded", "vecs_loaded", "small_loaded", "ones_set", "act_order", "dve_order"]
            + ["n_squared", "n_added", "n_total", "n_log", "n_scale", "n_scaled", "n_high", "n_done"]
            + ["g_squared", "g_added", "g_scale", "final_done"]
            + ["sp_matrices", "sp_scores", "sp_log", "sp_soft", "sp_split_high", "sp_split", "sp_decay",
               "sp_weights", "sp_out", "sp_high", "sp_low"]
            + ["hp_zero", "lb_diff", "lb_ready", "silu_c", "silu_done", "hf_full", "hf_taken", "hf_sig", "hf_neg", "hf_f",
               "hf_k", "hf_qs", "hf_q", "hf_log", "hf_b"]
            + ["lv_diff0", "lv_diff1", "lv_exp0", "lv_exp1", "lv_pair0", "lv_pair1", "lv_score", "lv_kept",
               "off_diff", "off_exp", "ho_ready",
               "off_score", "off_kept", "ho_out", "ho_sq", "ho_total", "ho_log", "ho_scale", "ho_norm",
               "hg_sig", "hg_silu", "hg_gate", "ho_high", "ho_low"]
            + ["mg_sum", "mg_high", "mg_low"]
            + ["f_square", "f_high", "f_low", "ada_in0", "ada_in1", "ada_used", "ada_step", "ada_turned",
               "ada_folded", "ada_cols", "fold_loaded", "bank7_free", "mod_ready"]
            + ["ctx_loaded", "cstb_loaded", "qb_copy", "qb_sums", "qb_rot", "qb_rope", "rq_log", "rq_exp",
               "rq_ready", "kpe_scaled", "kpe_squared", "kpe_rot", "kpe_done", "kb_copy", "kb_sum", "kb_r",
               "kb_norm"]
            + ["q_joined", "k_joined", "s_full", "s_max", "s_exp", "p_norm", "t_full", "t_copied", "o_full",
               "o_high", "o_low"]
            + ["gm_loaded", "gm_rows", "gm_copy", "gm_extra", "gv_var", "gv_log", "gv_rstd", "gv_norm",
               "gu_mul", "gu_high", "gu_low", "stored"]
        )
        sem = {n: ctx.enter_context(nc.semaphore(n)) for n in names}

        def v(name, j=0, n=1):
            o = VECS[name][0] + j
            return vecs[:, o:o + n]

        def tile(t, j, w=T):
            return t[:, j * w:(j + 1) * w]

        D_C, D_CC, D_LB, D_OLB, D_GAIN, D_RQ, D_AT = 0, 8, 16, 20, 24, 64, 96

        def dcol(o, n=1):
            return derived[:, o:o + n]

        def mod_col(layer, part, j):
            fb = part * KT + j
            chunk = fb // 4
            return (layer * 2 + chunk // 6) * 4 * ADA_PER_IT + (chunk % 6) * 4 + fb % 4

        def ctx_col(part, j):
            fb = part * KT + j
            return (fb // 4) * 4 * ADA_PER_IT + 24 + fb % 4

        def mcol(c):
            return mods[:, c:c + 1]

        A_TILES = [("sb_qk", 8), ("sb_v", 4), ("hg_i", 4), ("hg_g", 4), ("merge", 16), ("ff0", 32),
                   ("q_a", 3), ("kv_a", 6), ("q_b", 12), ("kv_b", 28), ("ff1", 32),
                   ("gm_v", 16), ("gm_u", 16), ("ff2", 32)]
        D_TILES = [("merge", 16), ("w_out", 8), ("ff0", 32), ("mla_o", 8),
                   ("ff1", 32), ("gm_u", 32), ("ff2", 32)]

        def firsts(table):
            n, found = 0, {}
            for name, k in table:
                found[name] = n
                n += k
            found["end"] = n
            return found

        A = firsts(A_TILES)
        D = firsts(D_TILES)
        NORMS = [("norm1", 8), ("norm2", 8), ("final", 8), ("ctx", 8), ("cq", 3), ("ck", 2),
                 ("ffn0", 8), ("mix1", 8), ("ffn1", 8)]
        DIRECT = ("norm1", "norm2", "ffn0", "mix1", "ffn1")
        ADDED = {n: k - 2 if n in DIRECT else k - 1 for n, k in NORMS}
        NSQ = firsts([(n, ADDED[n]) for n, _ in NORMS])
        NT = firsts(NORMS)
        NI = {n: i for i, (n, _) in enumerate(NORMS)}

        V_AFTER = (2, 1, 2, 1, 2, 1, 2, 1)
        V_FIRST = [sum(V_AFTER[:h]) for h in range(MLA_HEADS)]

        def k_tile(h):
            return A["kv_b"] + 2 * h + V_FIRST[h]

        def v_tile(i):
            h = max(g for g in range(MLA_HEADS) if V_FIRST[g] <= i)
            return A["kv_b"] + 2 * (h + 1) + i

        G_AFTER = (1, 3, 5, 7)
        LEVEL_TILES = 4 * (len(HGRN_LEVELS) + 1)

        def lv_bank(n):
            return n % 6

        def lv_factor(lv):
            return hg_a if lv % 2 else hg_a2

        def level_view(t, pr, m_):
            return t[:, pr * 2 * T:(pr + 1) * 2 * T].rearrange("p (g s m) -> p g s m", s=2, m=m_)

        def second_halves(t, m_):
            return t.rearrange("p (g s m) -> p g s m", s=2, m=m_)[:, :, 1, :]

        def level_diff(eng, lv, pr):
            m_ = HGRN_LEVELS[lv]
            b = level_view(hg_b, pr, m_)
            ref = b[:, :, 0:1, m_ - 1:m_].broadcast_to([P, T // m_, 2, m_])
            if lv >= 2:
                eng.wait_ge(sem["lv_score"], 4 * (lv - 1) + 2 * pr + 2)
            eng.tensor_tensor(level_view(lv_factor(lv), pr, m_), b, ref, ALU.subtract)\
                .then_inc(sem["lv_diff%d" % pr], 1)

        def level_pair(eng, lv, pr):
            m_ = HGRN_LEVELS[lv]
            a = level_view(lv_factor(lv), pr, m_)
            eng.wait_ge(sem["lv_exp%d" % pr], lv + 1)
            eng.tensor_tensor(a[:, :, 0, :], a[:, :, 0, :], level_view(hg_k, pr, m_)[:, :, 0, :], ALU.mult)
            eng.tensor_tensor(a[:, :, 1, :], a[:, :, 1, :], level_view(hg_q, pr, m_)[:, :, 1, :], ALU.mult)\
                .then_inc(sem["lv_pair%d" % pr], 1)

        def gate_unit(j, g):
            return FIRST["merge"] + (2 * j if j < 2 else 3 * j - 1) + g

        def branch_unit(j):
            return FIRST["merge"] + min(3 * j + 4, 23)

        def squares_at(name):
            return (l_sq, l_acc) if name in ("cq", "ck") else (n_sq, n_acc)

        def wait_pos(eng, s, value):
            if not isinstance(value, int) or value > 0:
                eng.wait_ge(sem[s], value)

        block = ctx.enter_context(nc.Block())

        @block.sync
        def _(sp):
            def load_x(i):
                sp.dma_start(hres[:, 2 * i * T:2 * (i + 1) * T], x_t[:, 2 * i * T:2 * (i + 1) * T])\
                    .then_inc(sem["x_in%d" % i], 16)

            def load_chunk(c, slot):
                sp.dma_start(raw[:, slot * 2 * UNIT:(slot + 1) * 2 * UNIT], weights[c, :, :])\
                    .then_inc(sem["raw_in%d" % slot], 16)

            load_x(0)
            load_x(1)
            load_chunk(0, 0)
            load_x(2)
            load_x(3)
            sp.dma_start(vecs[:, :], vecs_in).then_inc(sem["vecs_loaded"], 16)
            for c in range(1, RAW_SLOTS):
                load_chunk(c, c)
                if c == 2:
                    sp.dma_start(ident[:, :], ident_in).then_inc(sem["small_loaded"], 16)
                    sp.dma_start(cst_a[:, :], const_a).then_inc(sem["small_loaded"], 16)
            n_chunks = (N_UNITS + 1) // CHUNK_UNITS
            rounds = n_chunks // RAW_SLOTS
            with sp.Fori(1, rounds) as r:
                for s in range(RAW_SLOTS):
                    sp.wait_ge(sem["w_ready"], r * 8 - 8 + 2 * s + 2)
                    load_chunk(r * RAW_SLOTS + s, s)
            for c in range(rounds * RAW_SLOTS, n_chunks):
                sp.wait_ge(sem["w_ready"], 2 * (c - RAW_SLOTS) + 2)
                load_chunk(c, c % RAW_SLOTS)

        @block.gpsimd
        def _(pool):
            def split_unit(u, k, first=False):
                if k % 2 == 0:
                    slot = k // 2
                    pool.wait_ge(sem["raw_in%d" % slot], (u - k) * 2 + 16)
                src = raw[:, k * UNIT:(k + 1) * UNIT]
                s = k % W_SLOTS
                if not first:
                    pool.wait_ge(sem["unit_started"], u - W_SLOTS + 2)
                pool.sem_inc(sem["split_turn"], 1)
                pool.tensor_scalar(tile(w_hi, s, UNIT), src, 1.0, 1.0, ALU.mult, ALU.mult)\
                    .then_inc(sem["w_high"], 1)
                pool.wait_ge(sem["w_high"], u + 1)
                pool.tensor_tensor(tile(w_lo, s, UNIT), src, tile(w_hi, s, UNIT).bitcast(F32), ALU.subtract)\
                    .then_inc(sem["w_ready"], 1)

            for u in range(8):
                split_unit(u, u, u < W_SLOTS)
            with pool.Fori(1, FIRST["hg_g"] // 8) as r:
                for k in range(8):
                    split_unit(r * 8 + k, k)
            for k in range(3):
                split_unit(FIRST["hg_g"] + k, k)
            pool.wait_ge(sem["hf_b"], 4)
            level_diff(pool, 0, 1)
            pool.wait_ge(sem["hf_k"], 4)
            pool.wait_ge(sem["hf_q"], 4)
            for lv in range(len(HGRN_LEVELS)):
                level_pair(pool, lv, 1)
                if lv + 1 < len(HGRN_LEVELS):
                    level_diff(pool, lv + 1, 1)
            for k in range(3, 8):
                split_unit(FIRST["hg_g"] + k, k)
            u_last = FIRST["q_a"] - 4
            with pool.Fori(FIRST["hg_g"] // 8 + 1, u_last // 8) as r:
                for k in range(8):
                    split_unit(r * 8 + k, k)
            for j in range(8):
                if j < 6:
                    split_unit(u_last + j, j)
                if j >= 1:
                    pool.wait_ge(sem["g_squared"], j + 1)
                    if j > 1:
                        pool.wait_ge(sem["g_added"], j - 1)
                    pool.tensor_tensor(g_acc[:, :], g_acc[:, :], tile(g_sq, (j - 1) % 2), ALU.add)\
                        .then_inc(sem["g_added"], 1)
            for j in (6, 7):
                split_unit(u_last + j, j)
            with pool.Fori(u_last // 8 + 1, N_UNITS // 8) as r:
                for k in range(8):
                    split_unit(r * 8 + k, k)
            for u in range(N_UNITS // 8 * 8, N_UNITS):
                split_unit(u, u % 8)

        @block.tensor
        def _(pe):
            def w(t, u, j):
                return t[:, (u % W_SLOTS) * UNIT + j * P:(u % W_SLOTS) * UNIT + (j + 1) * P]

            def start_unit(u, ready=None):
                pe.wait_ge(sem["w_ready"], (u if ready is None else ready) + 1)

            def group(dst, u, parts, first=True, last=True, new_unit=True, each=None, ready=None):
                if new_unit:
                    start_unit(u, ready)
                n = len(parts)
                for i, (j, hi, lo) in enumerate(parts):
                    if each is not None:
                        each(i)
                    m = pe.matmul(dst, w(w_hi, u, j), lo, start=first and i == 0, stop=False)
                    if new_unit and i == 0:
                        m.then_inc(sem["unit_started"], 1)
                    pe.matmul(dst, w(w_hi, u, j), hi, start=False, stop=False)
                    m = pe.matmul(dst, w(w_lo, u, j), hi, start=False, stop=last and i == n - 1)
                return m

            def side_by_side(dsts, u, parts, full, high, low, ready=None):
                n = len(parts)
                for i, (j, hi, lo) in enumerate(parts[:-1]):
                    high(i)
                    for g, dst in enumerate(dsts):
                        if i == 0:
                            start_unit(u + g, None if ready is None else ready + g)
                        m = pe.matmul(dst, w(w_hi, u + g, j), hi, start=i == 0, stop=False)
                        if g == 0 and i == 0:
                            m.then_inc(sem["unit_started"], 1)
                        pe.matmul(dst, w(w_lo, u + g, j), hi, start=False, stop=False)
                    low(i)
                    for g, dst in enumerate(dsts):
                        pe.matmul(dst, w(w_hi, u + g, j), lo, start=False, stop=False)
                j, hi, lo = parts[-1]
                high(n - 1)
                low(n - 1)
                for g, dst in enumerate(dsts):
                    m = pe.matmul(dst, w(w_hi, u + g, j), lo, start=False, stop=False)
                    if g > 0:
                        m.then_inc(sem["unit_started"], 1)
                    pe.matmul(dst, w(w_hi, u + g, j), hi, start=False, stop=False)
                    pe.matmul(dst, w(w_lo, u + g, j), hi, start=False, stop=True).then_inc(sem[full], 1)

            def a_bank(n):
                wait_pos(pe, "a_free", n - 3)
                return ps[:, n % 4, :]

            def d_bank(n):
                wait_pos(pe, "d_free", n - 1)
                return ps[:, 4 + n % 2, :]

            def x_parts(hi=x_hi, lo=x_lo, k=KT, w_=T, first_tile=0):
                return [(first_tile + j, tile(hi, j, w_), tile(lo, j, w_)) for j in range(k)]

            def stat(name, w_=T):
                i = NI[name]
                pe.wait_ge(sem["n_added"], NSQ[name] + ADDED[name])
                if name == "ctx":
                    pe.wait_ge(sem["g_scale"], 1)
                if i:
                    pe.wait_ge(sem["n_scale"], i)
                acc = squares_at(name)[1]
                direct = name in DIRECT
                m = pe.matmul(ps[:, 6, 0:min(w_, T)], ones[:, :], acc[:, 0:min(w_, T)], start=True,
                              stop=not direct)
                if direct:
                    k = dict(NORMS)[name]
                    pe.wait_ge(sem["n_squared"], NT[name] + k)
                    m = pe.matmul(ps[:, 6, :], ones[:, :], tile(n_sq, (k - 2) % 2), start=False, stop=True)
                if w_ > T:
                    m = pe.matmul(ps[:, 7, 0:w_ - T], ones[:, :], acc[:, T:w_], start=True, stop=True)
                if name == "final":
                    pe.wait_ge(sem["d_free"], D["mla_o"])
                    pe.wait_ge(sem["g_added"], KT)
                    m = pe.matmul(ps[:, 4, :], ones[:, :], g_acc[:, :], start=True, stop=True)
                m.then_inc(sem["n_total"], 1)

            def norm_waits(name):
                def each(i):
                    pe.wait_ge(sem["n_done"], NT[name] + i + 1)
                return each

            def norm_high(name):
                def high(i):
                    pe.wait_ge(sem["n_high"], NT[name] + i + 1)
                return high

            def feature_major(first_u, n, a0_, pool="a", each=None, high=None):
                first = 0
                if each is not None:
                    first = 2
                    side_by_side([a_bank(a0_), a_bank(a0_ + 1)], first_u, x_parts(), "a_full", high,
                                 each)
                for j in range(first, n):
                    dst = a_bank(a0_ + j) if pool == "a" else d_bank(a0_ + j)
                    group(dst, first_u + j, x_parts()).then_inc(sem[pool + "_full"], 1)

            def token_major(first_u, a0_, n_cols=1, each=None):
                for cb in range(n_cols):
                    for uu in range(4):
                        u = first_u + cb * 4 + uu
                        start_unit(u)
                        if each is not None and cb == 0:
                            each(2 * uu + 1)
                        s0 = (u % W_SLOTS) * UNIT
                        for c in range(NC4):
                            n = a0_ + cb * 4 + c
                            dst = a_bank(n) if uu == 0 else ps[:, n % 4, :]
                            for kk in range(2):
                                k = uu * 2 + kk
                                xh = x_hi[:, k * T + c * P:k * T + (c + 1) * P]
                                xl = x_lo[:, k * T + c * P:k * T + (c + 1) * P]
                                wh = w_hi[:, s0 + kk * T:s0 + (kk + 1) * T]
                                wl = w_lo[:, s0 + kk * T:s0 + (kk + 1) * T]
                                m = pe.matmul(dst, xl, wh, start=k == 0, stop=False)
                                if c == 0 and kk == 0:
                                    m.then_inc(sem["unit_started"], 1)
                                pe.matmul(dst, xh, wh, start=False, stop=False)
                                m = pe.matmul(dst, xh, wl, start=False, stop=k == KT - 1)
                            if uu == 3:
                                m.then_inc(sem["a_full"], 1)

            pe.wait_ge(sem["ones_set"], 2)
            stat("norm1")
            feature_major(FIRST["sb_q"], 8, A["sb_qk"], each=norm_waits("norm1"), high=norm_high("norm1"))
            token_major(FIRST["sb_v"], A["sb_v"])

            def z(h, i):
                b = (h % 2) * 3
                if i == 3:
                    return ps[:, b + 1, 0:P]
                return ps[:, b + i, i * P:T]

            def head_half(h):
                return slice(64 * (h % 2), 64 * (h % 2) + 64)

            def sb_scores(h):
                hp = head_half(h)
                if h < 2:
                    pe.wait_ge(sem["a_free"], A["hg_i"])
                else:
                    pe.wait_ge(sem["sp_weights"], 4 * (h - 1))
                for i in (0, 1, 2, 3):
                    m = pe.matmul(z(h, i), sb_k[hp, (h // 2) * T + i * P:(h // 2) * T + (i + 1) * P],
                                  sb_q[hp, (h // 2) * T + i * P:(h // 2 + 1) * T], start=i != 3, stop=True,
                                  skip_group_check=True)
                m.then_inc(sem["sp_scores"], 1)

            def sb_decay(h):
                seg = [0, 512, 896, 1152]
                tri, one, eye, neg = (tile(sb_m, k, P) for k in range(4))
                pe.wait_ge(sem["sp_split"], h + 1)

                def add(dst, matrix, i2):
                    o = (h % 2) * 1280 + seg[i2]
                    for part in (sp_hi, sp_lo):
                        m = pe.matmul(dst, matrix, part[:, o:o + T - i2 * P], start=False, stop=True,
                                      skip_group_check=True)
                    return m

                for i in range(4):
                    zi = z(h, i)
                    pe.matmul(zi[:, 0:P], eye, neg, start=False, stop=True, skip_group_check=True)
                    m = add(zi, tri, i)
                    for i2 in range(i + 1, 4):
                        m = add(zi[:, (i2 - i) * P:T - i * P], one, i2)
                m.then_inc(sem["sp_decay"], 1)

            def sb_values(h):
                seg = [0, 512, 896, 1152]
                dst = ps[head_half(h), 6, :]
                if h:
                    pe.wait_ge(sem["sp_low"], h)
                for i in range(4):
                    pe.wait_ge(sem["sp_weights"], 4 * h + i + 1)
                    m = pe.matmul(dst[:, i * P:T], sb_v[:, i * T + h * 64:i * T + (h + 1) * 64],
                                  sb_w[:, seg[i]:seg[i] + T - i * P], start=i == 0, stop=i == 3,
                                  skip_group_check=True)
                m.then_inc(sem["sp_out"], 1)

            def hg_products(n, part):
                if part == 0 and n:
                    pe.wait_ge(sem["hf_taken"], n)
                m = group(ps[:, 7, :], FIRST["hg_f"] + n, x_parts()[4 * part:4 * part + 4], first=part == 0,
                          last=part == 1, new_unit=part == 0)
                if part == 1:
                    m.then_inc(sem["hf_full"], 1)

            pe.wait_ge(sem["sp_matrices"], 4)
            sb_scores(0)
            for h in range(SB_HEADS):
                if h + 1 < SB_HEADS:
                    sb_scores(h + 1)
                hg_products(h, 0)
                sb_decay(h)
                hg_products(h, 1)
                sb_values(h)

            pe.wait_ge(sem["sp_weights"], 4 * SB_HEADS)
            token_major(FIRST["hg_i"], A["hg_i"])

            def gate_products(j):
                n = A["hg_g"] + j
                if j == 0:
                    pe.wait_ge(sem["sp_low"], SB_HEADS)
                    pe.wait_ge(sem["hf_taken"], SB_HEADS)
                if j >= 2:
                    pe.wait_ge(sem["a_free"], n - 1)
                group(ps[:, 6 + j % 2, :], FIRST["hg_g"] + j, x_parts()).then_inc(sem["a_full"], 1)

            pe.wait_ge(sem["a_free"], A["hg_g"])
            pe.wait_ge(sem["hf_k"], 4)
            pe.wait_ge(sem["hf_q"], 4)
            for lv in range(len(HGRN_LEVELS) + 1):
                for h in range(HG_HEADS):
                    n = lv * 4 + h
                    if n >= 6:
                        pe.wait_ge(sem["lv_kept"], n - 5)
                    if lv:
                        pe.wait_ge(sem["lv_pair%d" % (h // 2)], lv)
                    for c in range(NC4):
                        o = h * T + c * P
                        if lv == 0:
                            l, r, n_out = hg_k[:, o:o + P], hg_q[:, o:o + P], P
                        else:
                            l = lv_factor(lv - 1)[:, o:o + P]
                            r = second_halves(l, HGRN_LEVELS[lv - 1])
                            n_out = P // 2
                        m = pe.matmul(ps[:, lv_bank(n), c * n_out:(c + 1) * n_out], l, r, start=True, stop=True)
                    m.then_inc(sem["lv_score"], 1)
                if lv in G_AFTER:
                    gate_products(G_AFTER.index(lv))
            for h in range(HG_HEADS):
                pe.wait_ge(sem["ho_ready"], h + 1)
                n = LEVEL_TILES + 2 * h
                pe.wait_ge(sem["lv_kept"], min(n + 1 - 5, LEVEL_TILES))
                if n + 1 - 6 >= LEVEL_TILES:
                    pe.wait_ge(sem["off_kept"], (n + 1 - 6 - LEVEL_TILES) // 2 + 1)
                km = lambda c: hg_k[:, h * T + c * P:h * T + (c + 1) * P]
                qp = lambda c: hg_q[:, h * T + c * P:h * T + (c + 1) * P]
                k0 = hg_edge[:, h * P:(h + 1) * P]
                q3 = hg_edge[:, (4 + h) * P:(5 + h) * P]
                pairs = [(km(0), qp(1)), (km(2), qp(3)), (k0, qp(2)), (k0, q3), (km(1), qp(2)), (km(1), q3)]
                for i, (l, r) in enumerate(pairs):
                    o = (i % 4) * P
                    m = pe.matmul(ps[:, lv_bank(n + i // 4), o:o + P], l, r, start=True, stop=True)
                m.then_inc(sem["off_score"], 1)
            pe.wait_ge(sem["lv_kept"], LEVEL_TILES)
            OFF = {(0, 1): 0, (2, 3): 1, (0, 2): 2, (0, 3): 3, (1, 2): 4, (1, 3): 5}
            for h in range(HG_HEADS):
                pe.wait_ge(sem["off_kept"], max(h + 1, 2))
                if h == 2:
                    pe.wait_ge(sem["a_free"], A["merge"])
                for tc in range(NC4):
                    for sc in range(tc + 1):
                        if sc == tc:
                            r = hg_p[:, h * T + tc * P:h * T + (tc + 1) * P]
                        else:
                            o = (h * 6 + OFF[(sc, tc)]) * P
                            r = hg_off[:, o:o + P]
                        m = pe.matmul(ps[:, 4 + h, tc * P:(tc + 1) * P],
                                      hg_v[:, sc * T + h * P:sc * T + (h + 1) * P], r,
                                      start=sc == 0, stop=sc == tc)
                m.then_inc(sem["ho_out"], 1)

            def gate(j, g):
                group(a_bank(A["merge"] + 2 * j + g), gate_unit(j, g), x_parts()).then_inc(sem["a_full"], 1)

            gate(0, 0)
            for h in range(HG_HEADS):
                pe.wait_ge(sem["ho_sq"], h + 1)
                if h >= 2:
                    pe.wait_ge(sem["ho_log"], h - 1)
                pe.matmul(ps[:, 2 + h % 2, :], ones[:, :], tile(hg_b, h), start=True, stop=True)\
                    .then_inc(sem["ho_total"], 1)
            gate(0, 1)
            pe.wait_ge(sem["ho_log"], HG_HEADS)
            for j in range(KT):
                if j + 1 < KT:
                    gate(j + 1, 0)
                    gate(j + 1, 1)
                if j == 0:
                    pe.wait_ge(sem["sp_low"], SB_HEADS)
                    pe.wait_ge(sem["ho_low"], HG_HEADS)
                branch = lambda g: [(4 * g + k, tile(h_hi, 4 * g + k), tile(h_lo, 4 * g + k)) for k in range(4)]
                group(d_bank(D["merge"] + 2 * j), branch_unit(j), branch(0)).then_inc(sem["d_full"], 1)
                group(d_bank(D["merge"] + 2 * j + 1), branch_unit(j), branch(1), new_unit=False)\
                    .then_inc(sem["d_full"], 1)

            def merged(i):
                pe.wait_ge(sem["mg_low"], i + 1)
            side_by_side([d_bank(D["w_out"]), d_bank(D["w_out"] + 1)], FIRST["w_out"], x_parts(m_hi, m_lo),
                         "d_full", lambda i: pe.wait_ge(sem["mg_high"], i + 1), merged)
            for j in range(2, KT):
                group(d_bank(D["w_out"] + j), FIRST["w_out"] + j, x_parts(m_hi, m_lo)).then_inc(sem["d_full"], 1)

            def feed_forward(name, norm, n_ff, with_ada):
                u0, a0_, d0_ = FIRST[name], A[name], D[name]
                with pe.Fori(0, 4) as it:
                    bank = lambda j: ps[:, (a0_ + j) % 4, :]
                    pe.wait_ge(sem["a_free"], a0_ + it * 8 - 2)
                    side_by_side([bank(0), bank(1)], u0, x_parts(), "a_full", norm_high(norm), norm_waits(norm),
                                 u0 + it * 16)
                    for j in range(2, 8):
                        pe.wait_ge(sem["a_free"], a0_ + it * 8 + j - 3)
                        group(bank(j), u0 + j, x_parts(), ready=u0 + it * 16 + j).then_inc(sem["a_full"], 1)

                    def hidden(i):
                        pe.wait_ge(sem["f_low"], it * 8 + n_ff * 32 + i + 1)

                    def hidden_high(i):
                        pe.wait_ge(sem["f_high"], it * 8 + n_ff * 32 + i + 1)
                    bank = lambda j: ps[:, 4 + (d0_ + j) % 2, :]
                    pe.wait_ge(sem["d_free"], d0_ + it * 8)
                    side_by_side([bank(0), bank(1)], u0 + 8, x_parts(h_hi, h_lo), "d_full", hidden_high, hidden,
                                 u0 + it * 16 + 8)
                    for j in range(2, 8):
                        pe.wait_ge(sem["d_free"], d0_ + it * 8 + j - 1)
                        group(bank(j), u0 + 8 + j, x_parts(h_hi, h_lo), ready=u0 + it * 16 + 8 + j)\
                            .then_inc(sem["d_full"], 1)
                    if with_ada:
                        pe.wait_ge(sem["fold_loaded"], 16)
                        pe.wait_ge(sem["ada_folded"], it * ADA_PER_IT + ADA_PER_IT)
                        pe.wait_ge(sem["bank7_free"], it + 1)
                        pe.matmul(ps[:, 7, 0:16 * ADA_PER_IT], fold[:, :], ada_x[:, :], start=True, stop=True)\
                            .then_inc(sem["ada_cols"], 1)

            stat("norm2")
            feed_forward("ff0", "norm2", 0, True)
            stat("final")

            side_by_side([a_bank(A["q_a"] + j) for j in range(3)], FIRST["q_a"], x_parts(), "a_full",
                         norm_high("final"), norm_waits("final"))
            def latent(j, main):
                u = FIRST["kv_a"] + j
                if main:
                    start_unit(u)
                    x = x_parts()
                    dst = a_bank(A["kv_a"] + j)
                    group(dst, u, x[0:1], last=False, new_unit=j == 0)
                    group(dst, u, x[1:], first=False, new_unit=False).then_inc(sem["a_full"], 1)
                else:
                    group(a_bank(A["kv_a"] + 3 + j)[:, 0:TC], u, x_parts(c_hi, c_lo, w_=TC), new_unit=j > 0,
                          each=norm_waits("ctx") if j == 0 else None).then_inc(sem["a_full"], 1)

            latent(0, True)
            stat("ctx", TC)
            latent(1, True)
            latent(2, True)
            stat("cq")
            for j in range(3):
                latent(j, False)
            def query_sums(pr):
                pe.wait_ge(sem["q_joined"], pr + 1)
                sq = lambda i, o: q_sq[:, ((pr % 2) * 3 + i) * T + o:((pr % 2) * 3 + i) * T + o + P]
                for hh in range(2):
                    for c in range(NC4):
                        col = (pr * 2 + hh) * 4 + c
                        m = pe.matmul(ps[:, 6, col:col + 1], sq(hh, c * P), ones[:, 0:1], start=True, stop=True)
                m.then_inc(sem["qb_sums"], 1)
                pe.wait_ge(sem["qb_copy"], 3 * pr + 3)
                if pr >= 1:
                    pe.wait_ge(sem["qb_rope"], pr)
                pe.matmul(ps[:, 5, :], cst_b[:, 0:P], tile(q_rp, pr % 2), start=True, stop=True)\
                    .then_inc(sem["qb_rot"], 1)

            for b in range(12):
                pr = b // 3
                dst = a_bank(A["q_b"] + b)
                for k in range(3):
                    t = 3 * b + k
                    u = FIRST["q_b"] + t // 8
                    if b == 0:
                        pe.wait_ge(sem["n_done"], NT["cq"] + k + 1)
                    m = group(dst, u, [(t % 8, tile(cq_hi, k), tile(cq_lo, k))], first=k == 0, last=k == 2,
                              new_unit=t % 8 == 0)
                m.then_inc(sem["a_full"], 1)
                if b == 2:
                    stat("ck", TK)
                    pe.wait_ge(sem["kpe_scaled"], 1)
                    pe.wait_ge(sem["cstb_loaded"], 16)
                    pe.matmul(ps[:, 4, :], cst_b[:, 0:P], kpe[:, TC:TK], start=True, stop=True)\
                        .then_inc(sem["kpe_rot"], 1)
                if b % 3 == 2 and pr >= 1:
                    query_sums(pr - 1)

            def key_tiles(h):
                u = FIRST["k_b"] + h // 4
                for half, (lo_, hi_) in enumerate(((0, T), (T, TK))):
                    dst = a_bank(k_tile(h) + half)[:, 0:hi_ - lo_]
                    parts = [((2 * h + k) % 8, ck_hi[:, k * TK + lo_:k * TK + hi_],
                              ck_lo[:, k * TK + lo_:k * TK + hi_]) for k in range(2)]
                    if h == 0 and half == 0:
                        pe.wait_ge(sem["n_done"], NT["ck"] + 2)
                    group(dst, u, parts, new_unit=(h % 4 == 0 and half == 0)).then_inc(sem["a_full"], 1)

            def value_tile(i):
                u = FIRST["v_b"] + i // 6
                if i % 6 == 0:
                    start_unit(u)
                dst, c = a_bank(v_tile(i)), i % 6
                s0 = (u % W_SLOTS) * UNIT
                for k in range(2):
                    kh = ck_hi[:, k * TK + c * P:k * TK + (c + 1) * P]
                    kl = ck_lo[:, k * TK + c * P:k * TK + (c + 1) * P]
                    wh = w_hi[:, s0 + k * T:s0 + (k + 1) * T]
                    wl = w_lo[:, s0 + k * T:s0 + (k + 1) * T]
                    pe.matmul(dst, kl, wh, start=k == 0, stop=False)
                    pe.matmul(dst, kh, wh, start=False, stop=False)
                    m = pe.matmul(dst, kh, wl, start=False, stop=k == 1)
                m.then_inc(sem["a_full"], 1)
                if i == sum(V_AFTER) - 1:
                    for _ in range(2):
                        pe.wait_ge(sem["a_full"], v_tile(i) + 1)
                        pe.sem_inc(sem["unit_started"], 1)

            def key_sums(h):
                pe.wait_ge(sem["k_joined"], h + 1)
                if h >= 1:
                    pe.wait_ge(sem["kb_r"], h)
                else:
                    pe.wait_ge(sem["kpe_done"], 1)
                sq = (h % 2) * TK
                for bank, lo_, hi_ in ((4, 0, T), (7, T, TK)):
                    pe.matmul(ps[:, bank, 0:hi_ - lo_], ones[:, :], k_sq[:, sq + lo_:sq + hi_], start=True,
                              stop=True).then_inc(sem["kb_sum"], 1)

            key_tiles(0)
            query_sums(3)
            for h in range(MLA_HEADS):
                for i in range(V_FIRST[h], V_FIRST[h] + V_AFTER[h]):
                    value_tile(i)
                if h + 1 < MLA_HEADS and h != 3:
                    key_tiles(h + 1)
                key_sums(h)
                if h == 3:
                    key_tiles(4)

            def at_scores(s, half):
                h, c = divmod(s, 4)
                b = (s % 3) * 2
                if half == 0:
                    if s >= 3:
                        pe.wait_ge(sem["s_exp"], s - 2)
                    if s % 4 == 0:
                        pe.wait_ge(sem["kb_norm"], h + 1)
                    if s == 0:
                        pe.wait_ge(sem["a_free"], A["ff1"])
                        pe.wait_ge(sem["qb_rope"], 4)
                    if s == 2:
                        pe.wait_ge(sem["kb_r"], MLA_HEADS)
                hp = head_half(h)
                pair = h // 2
                krt, kro = (kr_a, pair * TK) if pair < 2 else (kr_b, (pair - 2) * TK)
                lo_, hi_ = ((0, T), (T, TK))[half]
                dst = ps[:, b + half, 0:hi_ - lo_]
                pe.matmul(dst, qn[:, h * T + c * P:h * T + (c + 1) * P],
                          kn[:, h * TK + lo_:h * TK + hi_], start=True, stop=False)
                m = pe.matmul(dst, qr[hp, pair * T + c * P:pair * T + (c + 1) * P],
                              krt[hp, kro + lo_:kro + hi_], start=False, stop=True)
                if half == 1:
                    m.then_inc(sem["s_full"], 1)

            def at_turn(s, half):
                if half == 0:
                    pe.wait_ge(sem["p_norm"], s + 1)
                if s == 0 and half == 0:
                    pe.wait_ge(sem["rq_log"], 1)
                else:
                    pe.wait_ge(sem["t_copied"], 2 * s + half)
                for k in range(3):
                    o = (s % 2) * TK + (half * 3 + k) * P
                    m = pe.transpose(ps[:, 6, k * P:(k + 1) * P], at_p[:, o:o + P], ident[:, :])
                m.then_inc(sem["t_full"], 1)

            def at_values(h):
                pe.wait_ge(sem["t_copied"], 8 * (h + 1))
                if h >= 1:
                    pe.wait_ge(sem["o_low"], h)
                for k in range(6):
                    m = pe.matmul(ps[:, 7, :], ml_v[:, k * 1024 + h * P:k * 1024 + (h + 1) * P],
                                  tile(at_pt, (h % 2) * 6 + k), start=k == 0, stop=k == 5)
                m.then_inc(sem["o_full"], 1)

            for s in range(2):
                at_scores(s, 0)
                at_scores(s, 1)
            for s in range(4 * MLA_HEADS):
                for half in range(2):
                    at_turn(s, half)
                    if s + 2 < 4 * MLA_HEADS:
                        at_scores(s + 2, half)
                if s % 4 == 0 and s > 0:
                    at_values(s // 4 - 1)
            at_values(MLA_HEADS - 1)

            def attended(i):
                pe.wait_ge(sem["o_low"], i + 1)
            pe.wait_ge(sem["t_copied"], 8 * MLA_HEADS)
            side_by_side([d_bank(D["mla_o"]), d_bank(D["mla_o"] + 1)], FIRST["mla_o"], x_parts(o_hi, o_lo),
                         "d_full", lambda i: pe.wait_ge(sem["o_high"], i + 1), attended)
            for j in range(2, KT):
                group(d_bank(D["mla_o"] + j), FIRST["mla_o"] + j, x_parts(o_hi, o_lo)).then_inc(sem["d_full"], 1)
            pe.wait_ge(sem["o_low"], MLA_HEADS)
            stat("ffn0")
            feed_forward("ff1", "ffn0", 1, False)

            stat("mix1")
            pe.wait_ge(sem["gm_loaded"], 32)
            pe.wait_ge(sem["d_free"], D["gm_u"])
            for i in range(2):
                pe.matmul(ps[:, 4 + i, :], ones[:, :], wst[:, i * T:(i + 1) * T], start=True, stop=True)\
                    .then_inc(sem["gm_rows"], 1)
            pe.wait_ge(sem["n_scale"], NI["mix1"] + 1)
            for i in range(2):
                pe.matmul(ps[:, 6 + i, :], ones[0:1, :], bs_row[0:1, i * T:(i + 1) * T], start=True, stop=True)\
                    .then_inc(sem["gm_rows"], 1)
            token_major(FIRST["gm_v"], A["gm_v"], 4, norm_waits("mix1"))

            def gate_in(f):
                u = FIRST["gm_u"] + (f // 8) * 16 + f % 8
                group(a_bank(A["gm_u"] + f), u, x_parts()).then_inc(sem["a_full"], 1)

            def mixing(f):
                dst = d_bank(D["gm_u"] + (f // 8) * 16 + f % 8)
                if f == 0:
                    pe.wait_ge(sem["gm_copy"], 4)
                    pe.wait_ge(sem["gv_norm"], 4)
                for c in range(NC4):
                    m = pe.matmul(dst[:, c * P:(c + 1) * P], gv[:, c * 2048 + f * P:c * 2048 + (f + 1) * P],
                                  wst[:, (f // 2) * P:(f // 2 + 1) * P], start=True, stop=True)
                m.then_inc(sem["d_full"], 1)

            for half in range(2):
                for f in (0, 1):
                    gate_in(half * 8 + f)
                for f in (0, 1):
                    mixing(half * 8 + f)
                for f in range(2, 8):
                    mixing(half * 8 + f)
                    gate_in(half * 8 + f)

                def mixed(i, half=half):
                    pe.wait_ge(sem["gu_low"], half * 8 + i + 1)

                def mixed_high(i, half=half):
                    pe.wait_ge(sem["gu_high"], half * 8 + i + 1)
                n, u = D["gm_u"] + half * 16 + 8, FIRST["gm_u"] + half * 16 + 8
                side_by_side([d_bank(n), d_bank(n + 1)], u, x_parts(h_hi, h_lo), "d_full", mixed_high, mixed)
                for j in range(2, 8):
                    group(d_bank(n + j), u + j, x_parts(h_hi, h_lo)).then_inc(sem["d_full"], 1)
            stat("ffn1")
            feed_forward("ff2", "ffn1", 2, False)

        NH = NT
        NK = dict(NORMS)

        def norm_spec(name):
            main = lambda j: tile(hres, j)
            xs = (lambda j: tile(x_hi, j), lambda j: tile(x_lo, j))
            gain = lambda n: (lambda j: dcol(D_GAIN + 8 * n + j))
            return {
                "norm1": (main, T, 1024, lambda j: v("norm1", j), None, xs),
                "norm2": (main, T, 1024, lambda j: v("norm2", j), None, xs),
                "final": (main, T, 1024, gain(0), lambda j: mcol(mod_col(0, 0, j)), xs),
                "ctx": (lambda j: tile(ctxx, j, TC), TC, 1024, gain(1), lambda j: mcol(ctx_col(0, j)),
                        (lambda j: tile(c_hi, j, TC), lambda j: tile(c_lo, j, TC))),
                "cq": (lambda j: tile(cq_raw, j), T, 384, lambda j: v("q_a_norm", j), None,
                       (lambda j: tile(cq_hi, j), lambda j: tile(cq_lo, j))),
                "ck": (lambda j: tile(ck_raw, j, TK), TK, 256, lambda j: v("kv_a_norm", j), None,
                       (lambda j: tile(ck_hi, j, TK), lambda j: tile(ck_lo, j, TK))),
                "ffn0": (main, T, 1024, gain(2), lambda j: mcol(mod_col(0, 3, j)), xs),
                "mix1": (main, T, 1024, gain(3), lambda j: mcol(mod_col(1, 0, j)), xs),
                "ffn1": (main, T, 1024, gain(4), lambda j: mcol(mod_col(1, 3, j)), xs),
            }[name]

        def square_of(name, j):
            squares, w_ = squares_at(name)[0], norm_spec(name)[1]
            step = TK if squares is l_sq else T
            return squares[:, ((j - 1) % 2) * step:((j - 1) % 2) * step + w_]

        def norm_t(name, j):
            return tile(l_sq, j % 2, TK) if name == "ck" else n_t[:, (j % 2) * T:(j % 2) * T + norm_spec(name)[1]]

        seg = [0, 512, 896, 1152]
        AX_X = mybir.AxisListType.X

        def ps_pair(b):
            return ps[:, b:b + 2, :].rearrange("p b t -> p (b t)")

        def zt(h, i):
            b = (h % 2) * 3
            return ps[:, b + 1, 0:P] if i == 3 else ps[:, b + i, i * P:T]

        def half_of(h):
            return slice(64 * (h % 2), 64 * (h % 2) + 64)

        @block.scalar
        def _(act):
            def ordered(s, value):
                act.wait_ge(sem[s], value)

            def copy(out_, in_):
                return act.activation(out_, in_, ACT.Copy)

            def exp_tables():
                act.preload_act_table_set("natural_log_exp_and_others")

            def load_ada(chunk, slot):
                act.dma_start(tile(ada_w, slot, 4096), ada[bass.ds(chunk, 1), :, :].rearrange("a p n -> (a p) n"))\
                    .then_inc(sem["ada_in%d" % slot], 16)

            def squares(name, ready):
                src, w_ = norm_spec(name)[0:2]
                i = NI[name]
                acc = squares_at(name)[1]
                for j in range(NK[name]):
                    ready(j)
                    if j == 0:
                        if i and name != "cq":
                            act.wait_ge(sem["n_total"], i)
                        buf = acc[:, 0:w_]
                    else:
                        if j >= 3:
                            act.wait_ge(sem["n_added"], NSQ[name] + j - 2)
                        buf = square_of(name, j)
                    act.activation(buf, src(j), ACT.Square).then_inc(sem["n_squared"], 1)
                    if name == "final":
                        if j >= 3:
                            act.wait_ge(sem["g_added"], j - 2)
                        act.activation(tile(g_sq, (j - 1) % 2) if j else g_acc[:, :], src(j), ACT.Square,
                                       scale=v("final", j)).then_inc(sem["g_squared"], 1)
                if name == "norm2":
                    for chunk in range(2):
                        load_ada(chunk, chunk)
                if name == "final":
                    act.wait_ge(sem["ada_used"], ADA_CHUNKS + 1)
                    act.dma_start(cst_b[:, :], const_b).then_inc(sem["cstb_loaded"], 16)
                    act.wait_ge(sem["ada_cols"], 4)
                    act.dma_start(ctxx[:, :], ctx_t).then_inc(sem["ctx_loaded"], 16)

            def scale_and_high(name):
                src, w_, feats, _, shift, dst = norm_spec(name)
                i, k = NI[name], NK[name]
                act.wait_ge(sem["n_total"], i + 1)
                if i:
                    act.wait_ge(sem["n_done"], NT[name])
                pieces = [(6, 0, min(w_, T))] + ([(7, T, w_)] if w_ > T else [])
                if name == "final":
                    pieces = [(4, 0, T)]
                for bank, lo_, hi_ in pieces:
                    m = act.activation(n_r[:, lo_:hi_], ps[:, bank, 0:hi_ - lo_], ACT.Ln,
                                       bias=EPS * EPS if name == "final" else EPS, scale=1.0 / feats)
                m.then_inc(sem["n_log"], 1)
                ordered("n_log", i + 1)
                act.activation(n_r[:, 0:w_], n_r[:, 0:w_], ACT.Exp, scale=-0.5).then_inc(sem["n_scale"], 1)
                for j in range(k):
                    act.wait_ge(sem["n_scaled"], NH[name] + j + 1)
                    t = norm_t(name, j)
                    if shift is None:
                        m = copy(dst[0](j), t)
                    else:
                        m = act.activation(dst[0](j), t, ACT.Identity, bias=shift(j))
                    m.then_inc(sem["n_high"], 1)
                if name == "final":
                    act.activation(g_r[:, :], ps[:, 6, :], ACT.Ln, bias=EPS, scale=1.0 / feats)\
                        .then_inc(sem["act_order"], 1)
                    ordered("act_order", 2 * SB_HEADS + 2)
                    act.activation(g_r[:, :], g_r[:, :], ACT.Exp, scale=-0.5).then_inc(sem["g_scale"], 1)

            def norm(name, ready):
                squares(name, ready)
                scale_and_high(name)

            def a_tile(n):
                act.wait_ge(sem["a_full"], n + 1)
                return ps[:, n % 4, :]

            def d_tile(n):
                act.wait_ge(sem["d_full"], n + 1)
                return ps[:, 4 + n % 2, :]

            def copy_out(n, dst, scale=None, bank=None):
                t = a_tile(n)
                if bank is not None:
                    t = ps[:, bank, :]
                if scale is None:
                    m = copy(dst, t)
                else:
                    m = act.activation(dst, t, ACT.Copy, scale=scale)
                m.then_inc(sem["a_free"], 1)

            exp_tables()
            norm("norm1", lambda j: act.wait_ge(sem["x_in%d" % (j // 2)], 16))
            for j in range(4):
                copy_out(A["sb_qk"] + j, tile(sb_q, j), scale=0.125)
            for j in range(4):
                copy_out(A["sb_qk"] + 4 + j, tile(sb_k, j))
            for c in range(NC4):
                copy_out(A["sb_v"] + c, tile(sb_v, c))

            def softplus(h):
                act.wait_ge(sem["sp_scores"], h + 1)
                if h:
                    ordered("sp_log", h)
                for i in range(4):
                    m = act.activation(sb_e[:, seg[i]:seg[i] + T - i * P], zt(h, i), ACT.Abs)
                m.then_inc(sem["act_order"], 1)
                ordered("act_order", 2 * h + 1)
                act.activation(sb_e[:, :], sb_e[:, :], ACT.Exp, scale=-1.0).then_inc(sem["act_order"], 1)
                ordered("act_order", 2 * h + 2)
                if h:
                    act.wait_ge(sem["sp_soft"], 4 * h)
                act.activation(sb_l[:, :], sb_e[:, :], ACT.Ln, bias=1.0).then_inc(sem["sp_log"], 1)

            def split_high(h):
                act.wait_ge(sem["sp_soft"], 4 * h + 4)
                if h >= 2:
                    act.wait_ge(sem["sp_decay"], h - 1)
                copy(tile(sp_hi, h % 2, 1280), sb_sp[:, :]).then_inc(sem["sp_split_high"], 1)

            def weights_of(h):
                act.wait_ge(sem["sp_decay"], h + 1)
                if h:
                    act.wait_ge(sem["sp_out"], h)
                for i in range(4):
                    act.activation(sb_w[:, seg[i]:seg[i] + T - i * P], zt(h, i), ACT.Exp)\
                        .then_inc(sem["sp_weights"], 1)

            def sb_high(h):
                act.wait_ge(sem["sp_out"], h + 1)
                copy(h_hi[half_of(h), (h // 2) * T:(h // 2 + 1) * T], ps[half_of(h), 6, :])\
                    .then_inc(sem["sp_high"], 1)

            act.wait_ge(sem["small_loaded"], 32)
            act.wait_ge(sem["ones_set"], 2)
            for k, src in enumerate((cst_a[:, 0:P], neg_ones[:, :], ident[:, :], cst_a[:, P:2 * P])):
                copy(tile(sb_m, k, P), src).then_inc(sem["sp_matrices"], 1)
            act.wait_ge(sem["sp_matrices"], 4)
            act.dma_start(fold[:, :], fold_in).then_inc(sem["fold_loaded"], 16)
            softplus(0)
            split_high(0)
            for h in range(SB_HEADS):
                if h + 1 < SB_HEADS:
                    softplus(h + 1)
                if h:
                    sb_high(h - 1)
                weights_of(h)
                if h + 1 < SB_HEADS:
                    split_high(h + 1)
            sb_high(SB_HEADS - 1)

            act.wait_ge(sem["lb_diff"], 1)
            act.activation(dcol(D_OLB, 4), dcol(D_LB, 4), ACT.Sigmoid, scale=-1.0).then_inc(sem["act_order"], 1)
            ordered("act_order", 2 * SB_HEADS + 1)
            act.activation(dcol(D_LB, 4), dcol(D_LB, 4), ACT.Sigmoid).then_inc(sem["lb_ready"], 1)
            act.activation(dcol(D_C, 16), vecs[:, VECS["c"][0]:VECS["c"][0] + 16], ACT.Sigmoid)\
                .then_inc(sem["silu_c"], 1)
            for j in range(4):
                act.wait_ge(sem["hf_taken"], j + 1)
                act.activation(tile(hg_b, j), tile(hf_in, j), ACT.Sigmoid).then_inc(sem["hf_sig"], 1)
                act.activation(tile(hg_k, j), tile(hf_in, j), ACT.Sigmoid, scale=-1.0).then_inc(sem["hf_neg"], 1)
            for j in range(4):
                act.wait_ge(sem["hf_taken"], 4 + j + 1)
                act.activation(tile(hg_q, j), tile(hg_raw, j), ACT.Sigmoid).then_inc(sem["hf_qs"], 1)
            exp_tables()
            for j in range(4):
                act.wait_ge(sem["hf_f"], j + 1)
                act.activation(tile(hg_a, j), tile(hg_b, j), ACT.Ln).then_inc(sem["hf_log"], 1)
            for c in range(NC4):
                copy_out(A["hg_i"] + c, tile(hg_v, c))
            act.wait_ge(sem["hf_q"], 4)

            def raw_gate(j):
                copy_out(A["hg_g"] + j, tile(hg_raw, j), bank=6 + j % 2)

            for lv, m_ in enumerate(HGRN_LEVELS):
                for pr in range(2):
                    act.wait_ge(sem["lv_diff%d" % pr], lv + 1)
                    vw = level_view(lv_factor(lv), pr, m_)
                    act.activation(vw[:, :, 0, :], vw[:, :, 0, :], ACT.Exp, scale=-1.0)
                    act.activation(vw[:, :, 1, :], vw[:, :, 1, :], ACT.Exp).then_inc(sem["lv_exp%d" % pr], 1)
                if lv - 1 in G_AFTER:
                    raw_gate(G_AFTER.index(lv - 1))
            for h in range(HG_HEADS):
                act.wait_ge(sem["off_diff"], h + 1)
                act.activation(tile(hg_a, h), tile(hg_a, h), ACT.Exp)
                if h >= 2:
                    act.wait_ge(sem["ho_ready"], h - 1)
                act.activation(tile(hg_s, h % 2), tile(hg_b, h), ACT.Exp).then_inc(sem["off_exp"], 1)
            raw_gate(3)
            for j in range(4):
                if j == 0:
                    act.wait_ge(sem["ho_ready"], HG_HEADS)
                if j >= 2:
                    act.wait_ge(sem["hg_silu"], j - 1)
                act.wait_ge(sem["a_free"], A["hg_g"] + j + 1)
                act.activation(tile(hg_s, j % 2), tile(hg_raw, j), ACT.Sigmoid).then_inc(sem["hg_sig"], 1)
            for h in range(HG_HEADS):
                act.wait_ge(sem["off_score"], h + 1)
                n = LEVEL_TILES + 2 * h
                copy(hg_off[:, h * 768:h * 768 + T], ps[:, lv_bank(n), :])
                copy(hg_off[:, h * 768 + T:(h + 1) * 768], ps[:, lv_bank(n + 1), 0:2 * P]).then_inc(sem["off_kept"], 1)
            exp_tables()
            for h in range(HG_HEADS):
                act.wait_ge(sem["ho_out"], h + 1)
                act.activation(tile(hg_b, h), ps[:, 4 + h, :], ACT.Square).then_inc(sem["ho_sq"], 1)
            act.dma_start(hres[:, :], x_t).then_inc(sem["x_loaded"], 16)

            def high_of(h):
                act.wait_ge(sem["hg_gate"], h + 1)
                copy(tile(h_hi, 4 + h), tile(hg_k, h)).then_inc(sem["ho_high"], 1)

            for h in range(HG_HEADS):
                act.wait_ge(sem["ho_total"], h + 1)
                act.activation(tile(hg_a, h), ps[:, 2 + h % 2, :], ACT.Ln, bias=EPS, scale=1.0 / P)\
                    .then_inc(sem["ho_log"], 1)
                ordered("ho_log", h + 1)
                act.activation(tile(hg_a, h), tile(hg_a, h), ACT.Exp, scale=-0.5).then_inc(sem["ho_scale"], 1)
                if h:
                    high_of(h - 1)
            high_of(HG_HEADS - 1)

            def gates_of(j):
                for g, name in enumerate(("gate_a", "gate_b")):
                    t = a_tile(A["merge"] + 2 * j + g)
                    if j == 0:
                        act.wait_ge(sem["ho_low"], HG_HEADS)
                    if j >= 2:
                        act.wait_ge(sem["d_free"], D["merge"] + 2 * (j - 2) + g + 1)
                    act.activation(tile(m_t, (j % 2) * 2 + g), t, ACT.Sigmoid, bias=v(name, j))\
                        .then_inc(sem["a_free"], 1)

            gates_of(0)
            gates_of(1)
            for j in range(KT):
                act.wait_ge(sem["mg_sum"], j + 1)
                copy(tile(m_hi, j), tile(m_t, 4)).then_inc(sem["mg_high"], 1)
                if j + 2 < KT:
                    gates_of(j + 2)
            exp_tables()

            def feed_forward(name, n_ff, with_ada):
                a0_, d0_ = A[name], D[name]

                def groups(it, last):
                    for j in range(8):
                        if with_ada and j in (3, 5, 7):
                            r = (j + 1) // 2
                            act.wait_ge(sem["ada_used"], it * 7 + r)
                            load_ada(it * 7 + r, r % 2)
                        n = it * 8 + j
                        act.wait_ge(sem["a_full"], n + a0_ + 1)
                        act.wait_ge(sem["f_square"], n + n_ff * 32 + 1)
                        act.activation(tile(f_r, j % 2), ps[:, (a0_ + j) % 4, :], ACT.Relu)\
                            .then_inc(sem["a_free"], 1)
                        act.wait_ge(sem["a_free"], n + a0_ + 1)
                        act.wait_ge(sem["d_full"], it * 8 + d0_)
                        act.activation(tile(h_hi, j), tile(f_r, j % 2), ACT.Square).then_inc(sem["f_high"], 1)
                    if with_ada:
                        for r in (5, 6):
                            act.wait_ge(sem["ada_used"], it * 7 + r)
                            load_ada(it * 7 + r, r % 2)
                        if not last:
                            for r in (1, 0):
                                act.wait_ge(sem["ada_used"], it * 7 + 8 - r)
                                load_ada(it * 7 + 7 + r, r)

                with act.Fori(0, 3) as it:
                    groups(it, False)
                groups(3, True)

            norm("norm2", lambda j: act.wait_ge(sem["d_free"], D["w_out"] + j + 1))
            feed_forward("ff0", 0, True)
            norm("final", lambda j: act.wait_ge(sem["d_free"], D["mla_o"] - 8 + j + 1))
            squares("ctx", lambda j: act.wait_ge(sem["ctx_loaded"], 16))
            for j in range(3):
                copy_out(A["q_a"] + j, tile(cq_raw, j))
            squares("cq", lambda j: ordered("a_free", A["q_a"] + j + 1))
            scale_and_high("ctx")

            def kv_row(j):
                return kpe_raw if j == 2 else ck_raw[:, j * TK:(j + 1) * TK]

            for j in range(3):
                copy_out(A["kv_a"] + j, kv_row(j)[:, TC:TK])
            scale_and_high("cq")
            for j in range(3):
                copy(kv_row(j)[:, 0:TC], a_tile(A["kv_a"] + 3 + j)[:, 0:TC]).then_inc(sem["a_free"], 1)
            act.wait_ge(sem["final_done"], KT)
            ordered("a_free", A["q_b"])
            act.activation(kpe[:, :], kpe_raw[:, :], ACT.Copy, scale=v("k_rope")).then_inc(sem["kpe_scaled"], 1)
            act.activation(kpe_sq[:, :], kpe_raw[:, :], ACT.Square).then_inc(sem["kpe_squared"], 1)
            norm("ck", lambda j: None)
            for b in range(12):
                pr, w_in = b // 3, b % 3
                t = a_tile(A["q_b"] + b)
                if w_in < 2:
                    dst, g = tile(qn, 2 * pr + w_in), "q_nope"
                else:
                    dst, g = tile(q_rp, pr % 2), "q_rope"
                    if pr >= 2:
                        act.wait_ge(sem["qb_rope"], pr - 1)
                act.activation(dst, t, ACT.Copy, scale=v(g)).then_inc(sem["qb_copy"], 1)
                if pr >= 2:
                    act.wait_ge(sem["qb_sums"], pr - 1)
                act.activation(tile(q_sq, (pr % 2) * 3 + w_in), t, ACT.Square).then_inc(sem["a_free"], 1)
            def key_squares(h):
                if h >= 2:
                    act.wait_ge(sem["kb_sum"], 2 * (h - 1))
                sq = (h % 2) * TK
                for half, (lo_, hi_) in enumerate(((0, T), (T, TK))):
                    t = a_tile(k_tile(h) + half)[:, 0:hi_ - lo_]
                    act.activation(kn[:, h * TK + lo_:h * TK + hi_], t, ACT.Copy, scale=v("k_nope"))\
                        .then_inc(sem["kb_copy"], 1)
                    act.activation(k_sq[:, sq + lo_:sq + hi_], t, ACT.Square).then_inc(sem["a_free"], 1)

            def key_scale(h):
                act.wait_ge(sem["kb_sum"], 2 * (h + 1))
                if h >= 2:
                    act.wait_ge(sem["kb_norm"], h - 1)
                o = (h % 2) * TK
                act.activation(k_r[:, o:o + T], ps[:, 4, :], ACT.Ln, bias=EPS, scale=1.0 / 192)
                act.activation(k_r[:, o + T:o + TK], ps[:, 7, 0:TC], ACT.Ln, bias=EPS, scale=1.0 / 192)\
                    .then_inc(sem["act_order"], 1)
                ordered("act_order", 2 * SB_HEADS + 2 + h + 1)
                act.activation(k_r[:, o:o + TK], k_r[:, o:o + TK], ACT.Exp, scale=-0.5).then_inc(sem["kb_r"], 1)

            key_squares(0)
            act.wait_ge(sem["qb_sums"], 4)
            act.activation(dcol(D_RQ, 32), ps[:, 6, 0:32], ACT.Ln, bias=EPS, scale=1.0 / 192)\
                .then_inc(sem["rq_log"], 1)
            ordered("rq_log", 1)
            act.activation(dcol(D_RQ, 32), dcol(D_RQ, 32), ACT.Exp, scale=-0.5).then_inc(sem["rq_exp"], 1)
            act.wait_ge(sem["qb_rope"], 4)
            for h in range(MLA_HEADS):
                for i in range(V_FIRST[h], V_FIRST[h] + V_AFTER[h]):
                    cb, c = divmod(i, 6)
                    copy_out(v_tile(i), ml_v[:, c * 1024 + cb * T:c * 1024 + (cb + 1) * T])
                if h + 1 < MLA_HEADS and h != 3:
                    key_squares(h + 1)
                key_scale(h)
                if h == 3:
                    key_squares(4)

            def at_exp(s):
                act.wait_ge(sem["s_max"], s + 1)
                if s >= 2:
                    act.wait_ge(sem["t_full"], 2 * (s - 1))
                elif s == 0:
                    act.wait_ge(sem["kb_norm"], MLA_HEADS)
                b = (s % 3) * 2
                act.activation(tile(at_p, s % 2, TK), ps_pair(b)[:, 0:TK], ACT.Exp,
                               bias=dcol(D_AT + 4 * (s % 2) + 1), scale=dcol(D_RQ + s),
                               accum_out=dcol(D_AT + 4 * (s % 2) + 2)).then_inc(sem["s_exp"], 1)

            def at_copy(s, half):
                h, c = divmod(s, 4)
                if s % 4 == 0 and half == 0 and h >= 2:
                    act.wait_ge(sem["o_full"], h - 1)
                act.wait_ge(sem["t_full"], 2 * s + half + 1)
                o = ((h % 2) * 6 + half * 3) * T
                dst = at_pt[:, o:o + 3 * T].rearrange("p (k t) -> p k t", k=3)
                src = ps[:, 6, 0:3 * P].rearrange("p (k t) -> p k t", k=3)
                copy(dst[:, :, c * P:(c + 1) * P], src).then_inc(sem["t_copied"], 1)

            def o_high_of(h):
                act.wait_ge(sem["o_full"], h + 1)
                copy(tile(o_hi, h), ps[:, 7, :]).then_inc(sem["o_high"], 1)

            at_exp(0)
            for s in range(4 * MLA_HEADS):
                at_copy(s, 0)
                if s + 1 < 4 * MLA_HEADS:
                    at_exp(s + 1)
                at_copy(s, 1)
                if s % 4 == 1 and s > 4:
                    o_high_of(s // 4 - 1)
            o_high_of(MLA_HEADS - 1)
            norm("ffn0", lambda j: act.wait_ge(sem["d_free"], D["mla_o"] + j + 1))
            act.dma_start(wst[:, :], ws_t).then_inc(sem["gm_loaded"], 16)
            act.dma_start(bs_row[0:1, :], bs_in).then_inc(sem["gm_loaded"], 16)
            feed_forward("ff1", 1, False)
            norm("mix1", lambda j: act.wait_ge(sem["d_free"], D["gm_u"] - 8 + j + 1))
            act.preload_act_table(ACT.Gelu)
            for cb in range(4):
                for c in range(NC4):
                    n = A["gm_v"] + cb * 4 + c
                    act.activation(gv[:, c * 2048 + cb * T:c * 2048 + (cb + 1) * T], a_tile(n), ACT.Gelu)\
                        .then_inc(sem["a_free"], 1)
            act.wait_ge(sem["gv_var"], 4)
            exp_tables()
            var = g_st[:, 96:104].rearrange("p (c s) -> p c s", s=2)[:, :, 1]
            act.activation(var, var, ACT.Ln, bias=EPS).then_inc(sem["gv_log"], 1)
            ordered("gv_log", 1)
            act.activation(var, var, ACT.Exp, scale=-0.5).then_inc(sem["gv_rstd"], 1)
            for half in range(2):
                for j in range(8):
                    f = half * 8 + j
                    t = a_tile(A["gm_u"] + f)
                    if f == 0:
                        act.wait_ge(sem["gm_extra"], 16)
                    else:
                        act.wait_ge(sem["gu_mul"], f)
                    act.activation(g_u[:, :], t, ACT.Gelu).then_inc(sem["a_free"], 1)
                    act.wait_ge(sem["gu_mul"], f + 1)
                    act.wait_ge(sem["d_full"], D["gm_u"] + half * 16)
                    copy(tile(h_hi, j), g_s[:, :]).then_inc(sem["gu_high"], 1)
            exp_tables()
            norm("ffn1", lambda j: act.wait_ge(sem["d_free"], D["ff2"] - 8 + j + 1))
            feed_forward("ff2", 2, False)
            for j in range(KT):
                act.wait_ge(sem["d_free"], D["end"] - 8 + j + 1)
                act.dma_start(out[:, j * T:(j + 1) * T], tile(hres, j)).then_inc(sem["stored"], 16)
            act.wait_ge(sem["stored"], 16 * KT)

        @block.vector
        def _(dve):
            class Order:
                n = 0

            def ordered(ins):
                Order.n += 1
                ins.then_inc(sem["dve_order"], 1)
                dve.wait_ge(sem["dve_order"], Order.n)

            def add_square(name, j):
                w_ = norm_spec(name)[1]
                acc = squares_at(name)[1][:, 0:w_]
                dve.wait_ge(sem["n_squared"], NT[name] + j + 1)
                if j > 1:
                    dve.wait_ge(sem["n_added"], NSQ[name] + j - 1)
                dve.tensor_tensor(acc, acc, square_of(name, j), ALU.add).then_inc(sem["n_added"], 1)

            def add_squares(name, added=0):
                for j in range(added + 1, ADDED[name] + 1):
                    add_square(name, j)

            def scale_and_low(name):
                src, w_, _, gain, shift, dst = norm_spec(name)
                i, k = NI[name], NK[name]
                dve.wait_ge(sem["n_scale"], i + 1)
                scale = n_r[:, 0:w_]

                def scaled(j):
                    if j >= 2:
                        dve.wait_ge(sem["n_high"], NH[name] + j - 1)
                        dve.wait_ge(sem["n_done"], NT[name] + j - 1)
                    dve.scalar_tensor_tensor(norm_t(name, j), src(j), gain(j), scale, ALU.mult, ALU.mult)\
                        .then_inc(sem["n_scaled"], 1)

                scaled(0)
                for j in range(k):
                    if j + 1 < k:
                        scaled(j + 1)
                    dve.wait_ge(sem["n_high"], NH[name] + j + 1)
                    high = dst[0](j).bitcast(F32)
                    if shift is None:
                        m = dve.tensor_tensor(dst[1](j), norm_t(name, j), high, ALU.subtract)
                    else:
                        m = dve.scalar_tensor_tensor(dst[1](j), norm_t(name, j), shift(j), high, ALU.add,
                                                     ALU.subtract)
                    m.then_inc(sem["n_done"], 1)

            def norm(name, added=0):
                add_squares(name, added)
                scale_and_low(name)

            def d_tile(n):
                dve.wait_ge(sem["d_full"], n + 1)
                return ps[:, 4 + n % 2, :]

            dve.memset(ones[:, :], 1.0).then_inc(sem["ones_set"], 1)
            dve.memset(neg_ones[:, :], -1.0).then_inc(sem["ones_set"], 1)
            dve.sem_inc(sem["f_square"], 2)
            dve.sem_inc(sem["ada_used"], 1)
            dve.sem_inc(sem["bank7_free"], 1)
            add_squares("norm1")
            dve.wait_ge(sem["vecs_loaded"], 16)
            scale_and_low("norm1")
            dve.wait_ge(sem["small_loaded"], 32)

            def soft(h):
                dve.wait_ge(sem["sp_log"], h + 1)
                if h:
                    dve.wait_ge(sem["sp_split"], h)
                for i in range(4):
                    m = dve.scalar_tensor_tensor(sb_sp[:, seg[i]:seg[i] + T - i * P], zt(h, i), 0.0,
                                                 sb_l[:, seg[i]:seg[i] + T - i * P], ALU.max, ALU.add)
                ordered(m)
                for i in range(4):
                    d = sb_sp[:, seg[i]:seg[i] + P]
                    dve.tensor_tensor(d, d, cst_a[:, CONSTS["strict"][0]:CONSTS["strict"][0] + P], ALU.mult)\
                        .then_inc(sem["sp_soft"], 1)

            def split_low(h):
                dve.wait_ge(sem["sp_split_high"], h + 1)
                dve.tensor_tensor(tile(sp_lo, h % 2, 1280), sb_sp[:, :], tile(sp_hi, h % 2, 1280).bitcast(F32),
                                  ALU.subtract).then_inc(sem["sp_split"], 1)

            def sb_low(h):
                dve.wait_ge(sem["sp_high"], h + 1)
                c0 = (h // 2) * T
                dve.tensor_tensor(h_lo[half_of(h), c0:c0 + T], ps[half_of(h), 6, :],
                                  h_hi[half_of(h), c0:c0 + T].bitcast(F32), ALU.subtract)\
                    .then_inc(sem["sp_low"], 1)

            def take_products(n):
                dve.wait_ge(sem["hf_full"], n + 1)
                dve.tensor_copy(tile(hf_in if n < 4 else hg_raw, n % 4), ps[:, 7, :]).then_inc(sem["hf_taken"], 1)

            soft(0)
            split_low(0)
            for h in range(SB_HEADS):
                if h:
                    take_products(h - 1)
                if h + 1 < SB_HEADS:
                    soft(h + 1)
                if h:
                    sb_low(h - 1)
                if h + 1 < SB_HEADS:
                    split_low(h + 1)
            take_products(SB_HEADS - 1)
            sb_low(SB_HEADS - 1)

            dve.tensor_tensor(dcol(D_LB, 4), v("lb0", 0, 4), v("lb1", 0, 4), ALU.subtract).then_inc(sem["lb_diff"], 1)
            dve.memset(hg_p[:, :], 0.0).then_inc(sem["hp_zero"], 1)
            dve.wait_ge(sem["lb_ready"], 1)
            dve.wait_ge(sem["silu_c"], 1)
            dve.tensor_tensor(dcol(D_C, 16), dcol(D_C, 16), vecs[:, VECS["c"][0]:VECS["c"][0] + 16], ALU.mult)\
                .then_inc(sem["silu_done"], 1)
            for j in range(4):
                dve.wait_ge(sem["hf_sig"], j + 1)
                dve.tensor_scalar(tile(hg_b, j), tile(hg_b, j), dcol(D_OLB + j), dcol(D_LB + j), ALU.mult,
                                  ALU.add).then_inc(sem["hf_f"], 1)
                dve.wait_ge(sem["hf_neg"], j + 1)
                dve.tensor_scalar(tile(hg_k, j), tile(hg_k, j), dcol(D_OLB + j), None, ALU.mult)\
                    .then_inc(sem["hf_k"], 1)
            restart = cst_a[:, CONSTS["restart"][0]:CONSTS["restart"][0] + T]
            for j in range(4):
                dve.wait_ge(sem["hf_log"], j + 1)
                dve.tensor_tensor_scan(tile(hg_b, j), restart, tile(hg_a, j), 0.0, ALU.mult, ALU.add)\
                    .then_inc(sem["hf_b"], 1)
            dve.wait_ge(sem["hf_b"], 4)
            level_diff(dve, 0, 0)
            for j in range(4):
                dve.wait_ge(sem["hf_qs"], j + 1)
                dve.tensor_tensor(tile(hg_q, j), tile(hg_raw, j), tile(hg_q, j), ALU.mult).then_inc(sem["hf_q"], 1)

            def keep(lv):
                o = CONSTS["levels"][0] + lv * P
                mask = cst_a[:, o:o + P].bitcast(I32)
                if lv:
                    m_ = HGRN_LEVELS[lv - 1]
                    g_ = P // 2 // m_
                    mask = second_halves(mask, m_).unsqueeze(1).broadcast_to([P, NC4, g_, m_])
                else:
                    mask = mask.unsqueeze(1).broadcast_to([P, NC4, P])
                for h in range(HG_HEADS):
                    bank = lv_bank(lv * 4 + h)
                    dve.wait_ge(sem["lv_score"], lv * 4 + h + 1)
                    if lv:
                        dve.wait_ge(sem["lv_kept"], (lv - 1) * 4 + h + 1)
                    else:
                        dve.wait_ge(sem["hp_zero"], 1)
                    if lv:
                        dst = tile(hg_p, h).rearrange("p (c g s m) -> p c g s m", c=NC4, s=2, m=m_)[:, :, :, 1, :]
                        src = ps[:, bank, 0:T // 2].rearrange("p (c g m) -> p c g m", c=NC4, m=m_)
                    else:
                        dst = tile(hg_p, h).rearrange("p (c t) -> p c t", c=NC4)
                        src = ps[:, bank, :].rearrange("p (c t) -> p c t", c=NC4)
                    dve.copy_predicated(dst, mask, src).then_inc(sem["lv_kept"], 1)

            dve.wait_ge(sem["hf_q"], 4)
            for lv in range(len(HGRN_LEVELS)):
                level_pair(dve, lv, 0)
                if lv + 1 < len(HGRN_LEVELS):
                    level_diff(dve, lv + 1, 0)
                keep(lv)
            dve.wait_ge(sem["lv_score"], 4 * 7)
            dve.wait_ge(sem["lv_pair1"], len(HGRN_LEVELS))
            for h in range(HG_HEADS):
                b = tile(hg_b, h).rearrange("p (c t) -> p c t", c=NC4)
                dve.tensor_tensor(tile(hg_a, h).rearrange("p (c t) -> p c t", c=NC4),
                                  b[:, :, P - 1:P].broadcast_to([P, NC4, P]), b, ALU.subtract)\
                    .then_inc(sem["off_diff"], 1)
            for h in range(HG_HEADS):
                dve.wait_ge(sem["off_exp"], h + 1)
                k, q, ep = tile(hg_k, h), tile(hg_q, h), tile(hg_s, h % 2)
                dve.tensor_tensor(k, k, tile(hg_a, h), ALU.mult)
                ordered(dve.tensor_tensor(q, q, ep, ALU.mult))
                dve.tensor_scalar(hg_edge[:, h * P:(h + 1) * P], k[:, 0:P], ep[:, 2 * P - 1:2 * P], None, ALU.mult)
                dve.tensor_scalar(hg_edge[:, (4 + h) * P:(5 + h) * P], q[:, 3 * P:T], ep[:, 3 * P - 1:3 * P],
                                  None, ALU.mult).then_inc(sem["ho_ready"], 1)
            keep(len(HGRN_LEVELS))
            for j in range(4):
                dve.wait_ge(sem["hg_sig"], j + 1)
                dve.tensor_tensor(tile(hg_raw, j), tile(hg_raw, j), tile(hg_s, j % 2), ALU.mult)\
                    .then_inc(sem["hg_silu"], 1)

            def low_of(h):
                dve.wait_ge(sem["ho_high"], h + 1)
                dve.tensor_tensor(tile(h_lo, 4 + h), tile(hg_k, h), tile(h_hi, 4 + h).bitcast(F32), ALU.subtract)\
                    .then_inc(sem["ho_low"], 1)

            dve.wait_ge(sem["hg_silu"], HG_HEADS)
            for h in range(HG_HEADS):
                dve.wait_ge(sem["ho_scale"], h + 1)
                dve.scalar_tensor_tensor(tile(hg_p, h), ps[:, 4 + h, :], v("hg_norm", h), tile(hg_a, h),
                                         ALU.mult, ALU.mult).then_inc(sem["ho_norm"], 1)
                dve.wait_ge(sem["ho_norm"], h + 1)
                dve.tensor_tensor(tile(hg_k, h), tile(hg_p, h), tile(hg_raw, h), ALU.mult).then_inc(sem["hg_gate"], 1)
                if h:
                    low_of(h - 1)
            low_of(HG_HEADS - 1)

            for j in range(KT):
                for g in range(2):
                    n = 2 * j + g
                    dve.wait_ge(sem["a_free"], A["merge"] + n + 1)
                    if g == 0 and j:
                        dve.wait_ge(sem["mg_high"], j)
                        dve.wait_ge(sem["mg_low"], j)
                    dve.tensor_tensor(tile(m_t, 4 + g), d_tile(D["merge"] + n), tile(m_t, (j % 2) * 2 + g), ALU.mult)\
                        .then_inc(sem["d_free"], 1)
                dve.wait_ge(sem["d_free"], D["merge"] + 2 * j + 2)
                dve.tensor_tensor(tile(m_t, 4), tile(m_t, 4), tile(m_t, 5), ALU.add).then_inc(sem["mg_sum"], 1)
                dve.wait_ge(sem["mg_high"], j + 1)
                dve.tensor_tensor(tile(m_lo, j), tile(m_t, 4), tile(m_hi, j).bitcast(F32), ALU.subtract)\
                    .then_inc(sem["mg_low"], 1)

            def add_out(n, j, gate, bank=None):
                dve.wait_ge(sem["d_full"], n + 1)
                src = ps[:, bank if bank is not None else 4 + n % 2, :]
                dve.scalar_tensor_tensor(tile(hres, j), src, gate, tile(hres, j), ALU.mult, ALU.add)\
                    .then_inc(sem["d_free"], 1)

            dve.wait_ge(sem["x_loaded"], 16)
            for j in range(KT):
                add_out(D["w_out"] + j, j, 1.0)
                if j >= 2:
                    add_square("norm2", j - 1)
            norm("norm2", KT - 2)

            def feed_forward(name, n_ff, gate, with_ada, next_norm):
                a0_, d0_ = A[name], D[name]

                def groups(it, last):
                    def ada_part(slot_no):
                        if not with_ada or not 1 <= slot_no <= 14:
                            return
                        r, part = divmod(slot_no - 1, 2)
                        cvec = D_CC if r == 6 else D_C
                        acc = tile(ada_acc, r % 2)
                        if part == 0:
                            dve.wait_ge(sem["ada_in%d" % (r % 2)], it * (64 if r % 2 == 0 else 48) + 16 * (r // 2) + 16)
                            if r >= 2:
                                dve.wait_ge(sem["ada_folded"], it * 7 + r - 1)
                        for k in range(4 * part, 4 * part + 4):
                            wk = ada_w[:, (r % 2) * 4096 + k * T:(r % 2) * 4096 + (k + 1) * T]
                            if k == 0:
                                m = dve.tensor_scalar(acc, wk, dcol(cvec + k), None, ALU.mult)
                            else:
                                dve.wait_ge(sem["ada_step"], it * 56 + r * 8 + k)
                                m = dve.scalar_tensor_tensor(acc, wk, dcol(cvec + k), acc, ALU.mult, ALU.add)
                            m.then_inc(sem["ada_step"], 1)
                        if part == 1:
                            dve.wait_ge(sem["ada_step"], it * 56 + r * 8 + 8)
                            dve.sem_inc(sem["ada_used"], 1)
                            dve.wait_ge(sem["f_low"], it * 8 + min(slot_no, 7) + 1)
                            dve.transpose(tile(f_s, 1), acc).then_inc(sem["ada_turned"], 1)
                            dve.wait_ge(sem["ada_turned"], it * 7 + r + 1)
                            dve.tensor_reduce(ada_x[:, r * 16:(r + 1) * 16],
                                              tile(f_s, 1).rearrange("p (j r) -> p j r", r=32), AX_X, ALU.add)\
                                .then_inc(sem["ada_folded"], 1)

                    for j in range(8):
                        n = it * 8 + j
                        dve.wait_ge(sem["a_free"], n + a0_ + 1)
                        if with_ada and j in (3, 5, 7):
                            dve.wait_ge(sem["ada_folded"], it * 7 + (j - 1) // 2)
                        dve.tensor_tensor(tile(f_s, j % 2), tile(f_r, j % 2), tile(f_r, j % 2), ALU.mult)\
                            .then_inc(sem["f_square"], 1)
                        dve.wait_ge(sem["f_square"], n + n_ff * 32 + 3)
                        dve.wait_ge(sem["f_high"], n + n_ff * 32 + 1)
                        dve.tensor_tensor(tile(h_lo, j), tile(f_s, j % 2), tile(h_hi, j).bitcast(F32), ALU.subtract)\
                            .then_inc(sem["f_low"], 1)
                        ada_part(j)
                    for j in range(8):
                        dve.wait_ge(sem["d_full"], it * 8 + d0_ + j + 1)
                        dve.scalar_tensor_tensor(tile(hres, j), ps[:, 4 + (d0_ + j) % 2, :], gate(j), tile(hres, j),
                                                 ALU.mult, ALU.add).then_inc(sem["d_free"], 1)
                        ada_part(8 + j)
                        if last and next_norm is not None and j >= 2:
                            add_square(next_norm, j - 1)
                    if last and next_norm == "final":
                        add_square("final", KT - 1)
                        dve.wait_ge(sem["n_added"], NSQ["final"] + KT - 1)
                        dve.wait_ge(sem["g_added"], KT - 1)
                        dve.scalar_tensor_tensor(g_acc[:, :], n_acc[:, :], EPS, g_acc[:, :], ALU.mult, ALU.add)\
                            .then_inc(sem["g_added"], 1)
                    if with_ada:
                        dve.wait_ge(sem["ada_cols"], it + 1)
                        for b in range(4):
                            own = slice(32 * b, 32 * b + 32)
                            sums = ps[own, 7, 0:16 * ADA_PER_IT].rearrange("p (c b) -> p c b", b=4)[:, :, b]
                            m = dve.tensor_copy(mods[own, bass.ds(it * 28, 28)], sums)
                        m.then_inc(sem["bank7_free"], 1)

                with dve.Fori(0, 3) as it:
                    groups(it, False)
                groups(3, True)

            dve.wait_ge(sem["silu_done"], 1)
            feed_forward("ff0", 0, lambda j: 1.0, True, "final")
            dve.wait_ge(sem["bank7_free"], 5)
            ordered(dve.tensor_tensor(mods[:, :], mods[:, :], v("ada_b", 0, 4 * ADA_CHUNKS), ALU.add))
            for n, (name, cols) in enumerate((("mix0", lambda j: mod_col(0, 1, j)), ("mix0", lambda j: ctx_col(1, j)),
                                              ("ffn0", lambda j: mod_col(0, 4, j)), ("mix1", lambda j: mod_col(1, 1, j)),
                                              ("ffn1", lambda j: mod_col(1, 4, j)))):
                for j in (0, 4):
                    m = dve.scalar_tensor_tensor(dcol(D_GAIN + 8 * n + j, 4), mods[:, cols(j):cols(j) + 4], 1.0,
                                                 v(name, j, 4), ALU.add, ALU.mult)
            ordered(m)
            dve.tensor_tensor(dcol(D_GAIN, 8), dcol(D_GAIN, 8), v("final", 0, 8), ALU.mult)\
                .then_inc(sem["mod_ready"], 1)
            dve.wait_ge(sem["mod_ready"], 1)
            scale_and_low("final")
            add_squares("ctx")
            add_squares("cq")
            scale_and_low("ctx")
            dve.wait_ge(sem["g_scale"], 1)
            for j in range(KT):
                dve.scalar_tensor_tensor(tile(hres, j), tile(hres, j), v("final", j), g_r[:, :], ALU.mult, ALU.mult)\
                    .then_inc(sem["final_done"], 1)
            scale_and_low("cq")
            norm("ck")
            cos = cst_b[:, P:P + T]
            sin = cst_b[:, P + T:P + 2 * T]
            dve.wait_ge(sem["kpe_rot"], 1)
            dve.tensor_tensor(q_tmp[:, :], ps[:, 4, :], sin, ALU.mult)
            ordered(dve.tensor_tensor(kpe[:, TC:TK], kpe[:, TC:TK], cos, ALU.mult))
            dve.tensor_tensor(kpe[:, TC:TK], kpe[:, TC:TK], q_tmp[:, :], ALU.add).then_inc(sem["kpe_done"], 1)
            def join_queries(pr):
                dve.wait_ge(sem["a_free"], A["q_b"] + 3 * pr + 3)
                at_ = lambda i: tile(q_sq, (pr % 2) * 3 + i)
                for hh in range(2):
                    hp = slice(64 * hh, 64 * hh + 64)
                    m = dve.tensor_tensor(at_(hh)[hp, :], at_(hh)[hp, :], at_(2)[hp, :], ALU.add)
                m.then_inc(sem["q_joined"], 1)

            def turn_queries(pr):
                dve.wait_ge(sem["qb_rot"], pr + 1)
                if pr:
                    dve.wait_ge(sem["qb_rope"], pr)
                else:
                    dve.wait_ge(sem["kpe_done"], 1)
                dve.tensor_tensor(q_tmp[:, :], ps[:, 5, :], sin, ALU.mult)
                ordered(dve.tensor_tensor(tile(qr, pr), tile(q_rp, pr % 2), cos, ALU.mult))
                dve.tensor_tensor(tile(qr, pr), tile(qr, pr), q_tmp[:, :], ALU.add).then_inc(sem["qb_rope"], 1)

            def join_keys(h):
                dve.wait_ge(sem["a_free"], k_tile(h) + 2)
                if h == 0:
                    dve.wait_ge(sem["kpe_squared"], 1)
                t = k_sq[0:64, (h % 2) * TK:(h % 2 + 1) * TK]
                dve.tensor_tensor(t, t, kpe_sq[0:64, :], ALU.add).then_inc(sem["k_joined"], 1)

            join_queries(0)
            for pr in range(4):
                if pr + 1 < 4:
                    join_queries(pr + 1)
                turn_queries(pr)
            join_keys(0)
            for h in range(MLA_HEADS):
                hp, pair = half_of(h), h // 2
                krt, kro = (kr_a, pair * TK) if pair < 2 else (kr_b, (pair - 2) * TK)
                if h + 1 < MLA_HEADS and h != 3:
                    join_keys(h + 1)
                dve.wait_ge(sem["kb_r"], h + 1)
                o = (h % 2) * TK
                dve.tensor_tensor(kn[:, h * TK:(h + 1) * TK], kn[:, h * TK:(h + 1) * TK], k_r[:, o:o + TK], ALU.mult)
                dve.tensor_tensor(krt[hp, kro:kro + TK], kpe[hp, :], k_r[hp, o:o + TK], ALU.mult)\
                    .then_inc(sem["kb_norm"], 1)
                if h == 3:
                    join_keys(4)
            dve.wait_ge(sem["rq_exp"], 1)
            dve.tensor_scalar(dcol(D_RQ, 32), dcol(D_RQ, 32), 192.0 ** -0.5, None, ALU.mult)\
                .then_inc(sem["rq_ready"], 1)
            dve.wait_ge(sem["rq_ready"], 1)

            def at_max(s):
                b = (s % 3) * 2
                o = D_AT + 4 * (s % 2)
                dve.wait_ge(sem["s_full"], s + 1)
                if s >= 2:
                    dve.wait_ge(sem["p_norm"], s - 1)
                ordered(dve.tensor_reduce(dcol(o), ps_pair(b)[:, 0:TK], AX_X, ALU.max))
                dve.tensor_scalar(dcol(o + 1), dcol(o), dcol(D_RQ + s), -1.0, ALU.mult, ALU.mult)\
                    .then_inc(sem["s_max"], 1)

            def at_norm(s):
                o = D_AT + 4 * (s % 2)
                dve.wait_ge(sem["s_exp"], s + 1)
                ordered(dve.reciprocal(dcol(o + 3), dcol(o + 2)))
                p = tile(at_p, s % 2, TK)
                dve.tensor_scalar(p, p, dcol(o + 3), None, ALU.mult).then_inc(sem["p_norm"], 1)

            def o_low_of(h):
                dve.wait_ge(sem["o_high"], h + 1)
                dve.tensor_tensor(tile(o_lo, h), ps[:, 7, :], tile(o_hi, h).bitcast(F32), ALU.subtract)\
                    .then_inc(sem["o_low"], 1)

            at_max(0)
            at_norm(0)
            at_max(1)
            for s in range(4 * MLA_HEADS):
                if s + 1 < 4 * MLA_HEADS:
                    at_norm(s + 1)
                if s + 2 < 4 * MLA_HEADS:
                    at_max(s + 2)
                if s % 4 == 1 and s > 4:
                    o_low_of(s // 4 - 1)
            o_low_of(MLA_HEADS - 1)
            for j in range(KT):
                add_out(D["mla_o"] + j, j, mcol(mod_col(0, 2, j)))
                if j >= 2:
                    add_square("ffn0", j - 1)
            norm("ffn0", KT - 2)
            feed_forward("ff1", 1, lambda j: mcol(mod_col(0, 5, j)), False, "mix1")

            norm("mix1", KT - 2)
            for i in range(4):
                dve.wait_ge(sem["gm_rows"], i + 1)
                dst = (rs_b if i < 2 else bs_b)[:, (i % 2) * T:(i % 2 + 1) * T]
                dve.tensor_copy(dst, ps[:, 4 + i, :]).then_inc(sem["gm_copy"], 1)
            dve.wait_ge(sem["gm_copy"], 4)
            for f in range(16):
                g = f // 2
                dve.scalar_tensor_tensor(extra[:, f * P:(f + 1) * P], rs_b[:, g * P:(g + 1) * P], v("ln_b", f),
                                         bs_b[:, g * P:(g + 1) * P], ALU.mult, ALU.add)\
                    .then_inc(sem["gm_extra"], 1)
            for q in range(4):
                for c in range(NC4):
                    dve.wait_ge(sem["a_free"], A["gm_v"] + 4 * q + c + 1)
                    m = dve.bn_stats(g_st[:, c * 24 + q * 6:c * 24 + q * 6 + 6],
                                     gv[:, c * 2048 + q * T:c * 2048 + (q + 1) * T])
            ordered(m)
            for c in range(NC4):
                dve.bn_aggr(g_st[:, 96 + 2 * c:98 + 2 * c], g_st[:, c * 24:c * 24 + 24]).then_inc(sem["gv_var"], 1)
            dve.wait_ge(sem["gv_rstd"], 1)
            for c in range(NC4):
                g = gv[:, c * 2048:(c + 1) * 2048]
                dve.tensor_scalar(g, g, g_st[:, 96 + 2 * c:97 + 2 * c], g_st[:, 97 + 2 * c:98 + 2 * c],
                                  ALU.subtract, ALU.mult).then_inc(sem["gv_norm"], 1)
            for half in range(2):
                for j in range(8):
                    f = half * 8 + j
                    n = D["gm_u"] + half * 16 + j
                    dve.wait_ge(sem["d_full"], n + 1)
                    ex = extra[:, f * P:(f + 1) * P].unsqueeze(1).broadcast_to([P, NC4, P])
                    src = ps[:, 4 + n % 2, :].rearrange("p (c t) -> p c t", c=NC4)
                    if f:
                        dve.wait_ge(sem["gu_mul"], f)
                    dve.scalar_tensor_tensor(g_t[:, :].rearrange("p (c t) -> p c t", c=NC4), src, v("ln_g", f), ex,
                                             ALU.mult, ALU.add).then_inc(sem["d_free"], 1)
                    dve.wait_ge(sem["d_free"], n + 1)
                    dve.wait_ge(sem["a_free"], A["gm_u"] + f + 1)
                    if f:
                        dve.wait_ge(sem["gu_high"], f)
                        dve.wait_ge(sem["gu_low"], f)
                    dve.tensor_tensor(g_s[:, :], g_t[:, :], g_u[:, :], ALU.mult).then_inc(sem["gu_mul"], 1)
                    dve.wait_ge(sem["gu_high"], f + 1)
                    dve.tensor_tensor(tile(h_lo, j), g_s[:, :], tile(h_hi, j).bitcast(F32), ALU.subtract)\
                        .then_inc(sem["gu_low"], 1)
                for j in range(8):
                    add_out(D["gm_u"] + half * 16 + 8 + j, j, mcol(mod_col(1, 2, j)))
                    if half and j >= 2:
                        add_square("ffn1", j - 1)
            norm("ffn1", KT - 2)
            feed_forward("ff2", 2, lambda j: mcol(mod_col(1, 5, j)), False, None)


def _units(w, k_tiles, m_tiles):
    t = w.reshape(k_tiles, P, m_tiles, P).transpose(2, 0, 1, 3).reshape(k_tiles * m_tiles, P, P)
    return _pack(t)


def _pack(tiles):
    import numpy as np
    n = tiles.shape[0]
    if n % 8:
        tiles = np.concatenate([tiles, np.zeros((8 - n % 8, P, P), tiles.dtype)])
    return tiles.reshape(-1, 8, P, P).transpose(0, 2, 1, 3).reshape(-1, P, UNIT)


def _moving(w, k_tiles):
    n = w.shape[1] // T
    return w.reshape(k_tiles // 2, 2, P, n, T).transpose(3, 0, 2, 1, 4).reshape(-1, P, UNIT)


def _half_first(w1, w2):
    import numpy as np
    parts = []
    for g in range(w2.shape[0] // (8 * P)):
        s = slice(g * 8 * P, (g + 1) * 8 * P)
        parts += [_units(w1[:, s], 8, 8), _units(w2[s, :], 8, 8)]
    return np.concatenate(parts)


def _stream(i):
    import numpy as np
    a = {k: np.asarray(x) for k, x in i.items()}
    w = a["w_in"][0]
    cut = lambda o, n: w[:, o:o + n]
    parts = [_units(cut(0, 512), 8, 4), _units(cut(512, 512), 8, 4), _moving(cut(1024, 512), 8),
             _units(cut(1536, 512), 8, 4), _units(cut(2560, 512), 8, 4), _moving(cut(2048, 512), 8),
             _units(cut(3072, 512), 8, 4)]
    ga, gb = _units(cut(3584, 1024), 8, 8), _units(cut(4608, 1024), 8, 8)
    both = np.concatenate([a["w_o_sb"][0], a["w_o_hg"][0]])
    o = _units(both, 8, 8)
    merge = [ga[0], gb[0], ga[1], gb[1], o[0]]
    for j in range(2, 8):
        merge += [ga[j], gb[j], o[j - 1]]
    parts.append(np.stack(merge + [o[7]]))
    parts.append(_units(a["w_out"][0], 8, 8))
    parts.append(_half_first(a["w_ff1"][0], a["w_ff2"][0]))
    parts.append(_units(a["mla_wq_a_2"][0], 8, 3))
    kva = a["mla_wkv_a_2"][0]
    parts.append(_units(np.concatenate([kva, kva[:, 256:320]], 1), 8, 3))
    qb = a["mla_wq_b_2"][0].reshape(384, MLA_HEADS, 192)
    blocks = []
    for pr in range(4):
        blocks += [qb[:, 2 * pr, 0:128], qb[:, 2 * pr + 1, 0:128],
                   np.concatenate([qb[:, 2 * pr, 128:192], qb[:, 2 * pr + 1, 128:192]], 1)]
    parts.append(_units(np.concatenate(blocks, 1), 3, 12))
    kvb = a["mla_wkv_b_2"][0].reshape(256, MLA_HEADS, 256)
    parts.append(_units(np.ascontiguousarray(kvb[:, :, 0:128]).reshape(256, 1024), 2, 8))
    parts.append(_moving(np.ascontiguousarray(kvb[:, :, 128:256]).reshape(256, 1024), 2))
    parts.append(_units(a["mla_wo_2"][0], 8, 8))
    parts.append(_half_first(a["ffn_w1_2"][0], a["ffn_w2_2"][0]))
    gi = a["gm_w_in_2"][0]
    parts.append(_moving(gi[:, 2048:4096], 8))
    parts.append(_half_first(gi[:, 0:2048], a["gm_w_out_2"][0]))
    parts.append(_half_first(a["ffn_w1_2"][1], a["ffn_w2_2"][1]))
    s = np.concatenate(parts)
    assert s.shape[0] == N_UNITS, s.shape
    if N_UNITS % 2:
        s = np.concatenate([s, np.zeros((1, P, UNIT), s.dtype)])
    return np.ascontiguousarray(s.reshape(-1, 2, P, UNIT).transpose(0, 2, 1, 3)).reshape(-1, P, 2 * UNIT)


def _cols(x):
    import numpy as np
    return np.asarray(x).reshape(-1, P).T


def _ada(i):
    import numpy as np
    w, b = np.asarray(i["ada_w_2"]), np.asarray(i["ada_b_2"])
    chunks, bias = [], []
    for it in range(4):
        layer = it // 2
        todo = [(layer, (it % 2) * 6 + r) for r in range(6)] + [(0, it)]
        for l, c in todo:
            chunks.append(w[l][:, c * T:(c + 1) * T].reshape(KT, P, T).transpose(1, 0, 2).reshape(P, KT * T))
            bias.append(_cols(b[l][c * T:(c + 1) * T]))
    return np.stack(chunks), np.concatenate(bias, 1)


def _vectors(i, ada_bias):
    import numpy as np
    a = {k: np.asarray(x) for k, x in i.items()}
    twice = lambda x: np.concatenate([x, x])
    got = {
        "norm1": a["norm1_g"][0], "gate_a": a["b_gate"][0][:1024], "gate_b": a["b_gate"][0][1024:],
        "lb0": a["lb_logits"][0], "lb1": a["lb_logits"][1], "hg_norm": a["hg_norm_g"][0],
        "norm2": a["norm2_g"][0], "final": a["final_g"], "mix0": a["norm_mix_g_2"][0],
        "ffn0": a["norm_ffn_g_2"][0], "mix1": a["norm_mix_g_2"][1], "ffn1": a["norm_ffn_g_2"][1],
        "q_a_norm": a["mla_q_a_norm_2"][0], "kv_a_norm": a["mla_kv_a_norm_2"][0],
        "q_nope": a["mla_q_norm_2"][0][:128], "q_rope": twice(a["mla_q_norm_2"][0][128:]),
        "k_nope": a["mla_k_norm_2"][0][:128], "k_rope": twice(a["mla_k_norm_2"][0][128:]),
        "ln_g": a["gm_ln_g_2"][0], "ln_b": a["gm_ln_b_2"][0], "c": a["c_2"][0], "c_ctx": a["c_ctx_2"],
    }
    cols = [ada_bias if n == "ada_b" else _cols(got[n]) for n in VECS]
    return np.ascontiguousarray(np.concatenate(cols, 1))


def _constants():
    import numpy as np
    s, t = np.arange(P)[:, None], np.arange(P)[None, :]
    f = lambda x: x.astype(np.float32)
    levels = [f(s == t)]
    for m in HGRN_LEVELS:
        same = s // (2 * m) == t // (2 * m)
        levels.append(f(same & (s // m % 2 == 0) & (t // m % 2 == 1)))
    restart = np.ones((P, T), np.float32)
    restart[:, ::P] = 0
    a = np.concatenate([-f(s >= t), f(s >= t) * np.float32(-1e30), f(s < t)] + levels + [restart], 1)
    rot = np.zeros((P, P), np.float32)
    for base in (0, 64):
        for half in (0, 32):
            for j in range(16):
                o = base + half + j
                rot[o + 16, o] = -1
                rot[o, o + 16] = 1
    rows = T // 64
    row = np.repeat(np.arange(rows, dtype=np.float32), 64)
    col = np.tile(np.arange(64, dtype=np.float32), rows)
    inv = np.float32(10000.0) ** (-np.arange(0, 32, 2, dtype=np.float32) / np.float32(32))
    ar, ac = row[:, None] * inv[None, :], col[:, None] * inv[None, :]
    ang = np.concatenate([ar, ar, ac, ac], -1)
    ang = np.concatenate([ang, ang], -1).T
    b = np.concatenate([rot, np.cos(ang), np.sin(ang)], 1).astype(np.float32)
    return np.ascontiguousarray(a), np.ascontiguousarray(b), np.eye(P, dtype=np.float32)


def _arrays(inputs):
    import numpy as np
    ada, ada_bias = _ada(inputs)
    ca, cb, ident = _constants()
    fm = lambda x, n: np.ascontiguousarray(np.asarray(x)[0].T.reshape(KT, P, n).transpose(1, 0, 2)).reshape(P, KT * n)
    ws = np.asarray(inputs["gm_ws_2"])[0]
    return {
        "weights": _stream(inputs), "ada": ada, "x_t": fm(inputs["x"], T), "ctx_t": fm(inputs["ctx_2"], TC),
        "vecs_in": _vectors(inputs, ada_bias), "const_a": ca, "const_b": cb, "ident_in": ident, "fold_in": np.tile(np.eye(32, dtype=np.float32), (4, 4)),
        "ws_t": np.ascontiguousarray(ws.transpose(2, 0, 1)).reshape(P, KT * P),
        "bs_in": np.ascontiguousarray(np.asarray(inputs["gm_bs_2"])[0]).reshape(1, KT * P),
    }


def kernel(**inputs):
    import numpy as np
    import concourse.bacc as bacc
    from concourse.bass_utils import run_bass_kernel_spmd

    nc = bacc.Bacc("TRN2", target_bir_lowering=False, num_devices=1)
    arrays = _arrays(inputs)
    aps = {n: nc.dram_tensor(n, a.shape, mybir.dt.from_np(a.dtype), kind="ExternalInput").ap()
           for n, a in arrays.items()}
    out = nc.dram_tensor("out", (P, KT * T), F32, kind="ExternalOutput").ap()
    build_program(nc, out=out, **aps)
    r = run_bass_kernel_spmd(nc, [arrays], core_ids=[0])
    got = np.asarray(r.results[0]["out"]).reshape(P, KT, T)
    return np.ascontiguousarray(got.transpose(2, 1, 0)).reshape(1, T, D_MODEL)
```
